# Optimizing a Trainium2 kernel written in Bass

```python
import math
import jax, jax.numpy as jnp
from jax import lax
import numpy as np

D_MODEL = 2048
BATCH = 1
SEQ = 256
DEPTH = 1

N_MEM = 256
NORM_EPS = 1e-6

SSD_WIDTH = D_MODEL // 2
SSD_HEAD_DIM = 64
SSD_HEADS = SSD_WIDTH // SSD_HEAD_DIM
SSD_GROUPS = 2
SSD_HEADS_PER_GROUP = SSD_HEADS // SSD_GROUPS
SSD_STATE = 128
SSD_CONV = 4
SSD_CHUNK = 128
SSD_CONV_DIM = SSD_WIDTH + 2 * SSD_GROUPS * SSD_STATE
SSD_IN = SSD_WIDTH + SSD_CONV_DIM + SSD_HEADS

RWKV_WIDTH = D_MODEL - SSD_WIDTH
RWKV_HEAD_DIM = 64
RWKV_HEADS = RWKV_WIDTH // RWKV_HEAD_DIM
RWKV_DECAY_RANK = 96
RWKV_AAA_RANK = 96
RWKV_GATE_RANK = 256
RWKV_IN = 3 * RWKV_WIDTH + RWKV_DECAY_RANK + RWKV_AAA_RANK + RWKV_GATE_RANK
RWKV_LN_EPS = 64e-5

MIX_WIDTH = SSD_WIDTH + RWKV_WIDTH
D_IN = SSD_IN + RWKV_IN

XATTN_HEADS = 4
XATTN_HEAD_DIM = D_MODEL // XATTN_HEADS

D_FF = 4 * D_MODEL


def rms_norm(x, g, eps=NORM_EPS):
    xf = x.astype(jnp.float32)
    y = xf * lax.rsqrt(jnp.mean(xf * xf, axis=-1, keepdims=True) + eps)
    return (y * g).astype(x.dtype)

def causal_depthwise_conv(u, w, b):
    y = lax.conv_general_dilated(
        u, w, window_strides=(1,), padding=[(w.shape[0] - 1, 0)],
        dimension_numbers=("NWC", "WIO", "NWC"), feature_group_count=u.shape[-1])
    return y + b

def ssd_mixer(u, conv_w, conv_b, dt_bias, a_log, d_skip, norm_g):
    f32 = jnp.float32
    bsz, seq, _ = u.shape
    G, E, P, N, Q = SSD_GROUPS, SSD_HEADS_PER_GROUP, SSD_HEAD_DIM, SSD_STATE, SSD_CHUNK
    nc = seq // Q
    z, xbc, dt = jnp.split(u, [SSD_WIDTH, SSD_WIDTH + SSD_CONV_DIM], axis=-1)
    xbc = jax.nn.silu(causal_depthwise_conv(xbc, conv_w, conv_b))
    xs, bm, cm = jnp.split(xbc, [SSD_WIDTH, SSD_WIDTH + G * N], axis=-1)
    xs = xs.astype(f32).reshape(bsz, nc, Q, G, E, P)
    bm = bm.astype(f32).reshape(bsz, nc, Q, G, N)
    cm = cm.astype(f32).reshape(bsz, nc, Q, G, N)
    dt = jax.nn.softplus(dt.astype(f32) + dt_bias.astype(f32))
    a = -jnp.exp(a_log.astype(f32))
    dt_c = dt.reshape(bsz, nc, Q, G, E)
    xdt = xs * dt_c[..., None]
    da = jnp.transpose(dt_c * a.reshape(G, E), (0, 1, 3, 4, 2))
    cs = jnp.cumsum(da, axis=-1)
    causal = jnp.tril(jnp.ones((Q, Q), dtype=bool))
    seg = cs[..., :, None] - cs[..., None, :]
    lmat = jnp.where(causal, jnp.exp(jnp.where(causal, seg, 0.0)), 0.0)
    cb = jnp.einsum('bclgn,bcsgn->bcgls', cm, bm)
    y_diag = jnp.einsum('bcgls,bcgels,bcsgep->bclgep', cb, lmat, xdt)
    decay_to_end = jnp.exp(cs[..., -1:] - cs)
    chunk_states = jnp.einsum('bcsgn,bcges,bcsgep->bcgepn', bm, decay_to_end, xdt)
    chunk_decay = jnp.exp(cs[..., -1])

    def carry_state(h, inp):
        st, dec = inp
        return h * dec[..., None, None] + st, h

    h0 = jnp.zeros((bsz, G, E, P, N), f32)
    _, start_states = lax.scan(carry_state, h0,
                               (jnp.moveaxis(chunk_states, 1, 0), jnp.moveaxis(chunk_decay, 1, 0)))
    start_states = jnp.moveaxis(start_states, 0, 1)
    y_off = jnp.einsum('bclgn,bcgepn,bcgel->bclgep', cm, start_states, jnp.exp(cs))
    y = y_diag + y_off + xs * d_skip.astype(f32).reshape(G, E, 1)
    y = y.reshape(bsz, seq, SSD_WIDTH) * jax.nn.silu(z.astype(f32))
    yg = y.reshape(bsz, seq, G, SSD_WIDTH // G)
    yg = yg * lax.rsqrt(jnp.mean(yg * yg, axis=-1, keepdims=True) + NORM_EPS)
    y = yg.reshape(bsz, seq, SSD_WIDTH) * norm_g
    return y.astype(u.dtype)

def rwkv7_mixer(u, mu, w0, w2, a0, a2, g2, k_k, k_a, r_k, ln_w, ln_b):
    f32 = jnp.float32
    bsz, seq, _ = u.shape
    H, N, W = RWKV_HEADS, RWKV_HEAD_DIM, RWKV_WIDTH
    uf = u.astype(f32)
    u_prev = jnp.pad(uf, ((0, 0), (1, 0), (0, 0)))[:, :-1]
    uf = uf + (u_prev - uf) * mu
    r, k, v, pw, pa, pg = jnp.split(
        uf, [W, 2 * W, 3 * W, 3 * W + RWKV_DECAY_RANK,
             3 * W + RWKV_DECAY_RANK + RWKV_AAA_RANK], axis=-1)
    w_log = -jax.nn.softplus(-(w0 + jnp.tanh(pw) @ w2)) - 0.5
    decay = jnp.exp(-jnp.exp(w_log))
    iclr = jax.nn.sigmoid(a0 + pa @ a2)
    gate = jax.nn.sigmoid(pg) @ g2
    heads = lambda t: t.reshape(bsz, seq, H, N)
    kk = heads(k * k_k)
    kk = kk / jnp.maximum(jnp.sqrt(jnp.sum(kk * kk, axis=-1, keepdims=True)), 1e-12)
    k = k * (1.0 + (iclr - 1.0) * k_a)
    r, k, v, decay, iclr = heads(r), heads(k), heads(v), heads(decay), heads(iclr)

    def step(state, inp):
        r_t, w_t, k_t, v_t, kk_t, a_t = inp
        sa = jnp.einsum('bhij,bhj->bhi', state, -kk_t)
        state = (state * w_t[:, :, None, :]
                 + sa[..., None] * (kk_t * a_t)[:, :, None, :]
                 + v_t[..., None] * k_t[:, :, None, :])
        return state, jnp.einsum('bhij,bhj->bhi', state, r_t)

    seq_first = lambda t: jnp.moveaxis(t, 1, 0)
    s0 = jnp.zeros((bsz, H, N, N), f32)
    _, y = lax.scan(step, s0, (seq_first(r), seq_first(decay), seq_first(k),
                               seq_first(v), seq_first(kk), seq_first(iclr)))
    y = jnp.moveaxis(y, 0, 1)
    mean = jnp.mean(y, axis=-1, keepdims=True)
    var = jnp.mean(jnp.square(y - mean), axis=-1, keepdims=True)
    y = ((y - mean) * lax.rsqrt(var + RWKV_LN_EPS)).reshape(bsz, seq, W) * ln_w + ln_b
    bonus = jnp.sum(r * k * r_k, axis=-1, keepdims=True) * v
    y = (y + bonus.reshape(bsz, seq, W)) * gate
    return y.astype(u.dtype)

def memory_cross_attention(h, m, wq, wk, wv, wo):
    bsz, seq, _ = h.shape
    q = (h @ wq).reshape(bsz, seq, XATTN_HEADS, XATTN_HEAD_DIM)
    k = (m @ wk).reshape(bsz, m.shape[1], XATTN_HEADS, XATTN_HEAD_DIM)
    v = (m @ wv).reshape(bsz, m.shape[1], XATTN_HEADS, XATTN_HEAD_DIM)
    scores = jnp.einsum('bshd,bmhd->bhsm', q, k).astype(jnp.float32) * (XATTN_HEAD_DIM ** -0.5)
    p = jax.nn.softmax(scores, axis=-1).astype(v.dtype)
    o = jnp.einsum('bhsm,bmhd->bshd', p, v).reshape(bsz, seq, D_MODEL)
    return o @ wo

def first_inputs(seed: int = 0) -> dict:
    key = jax.random.key(seed)
    ks = iter(jax.random.split(key, 40))
    nrm = lambda shape, scale: jax.random.normal(next(ks), shape, jnp.float32) * scale
    uni = lambda shape, lo, hi: jax.random.uniform(next(ks), shape, jnp.float32, lo, hi)
    L = DEPTH
    dt0 = jnp.exp(uni((L, SSD_HEADS), math.log(1e-3), math.log(1e-1)))
    return {
        "x": nrm((BATCH, SEQ, D_MODEL), 1.0),
        "mem": nrm((BATCH, N_MEM, D_MODEL), 1.0),
        "norm_mix_g": 1.0 + nrm((L, D_MODEL), 0.02),
        "w_in": nrm((L, D_MODEL, D_IN), D_MODEL ** -0.5),
        "ssd_conv_w": nrm((L, SSD_CONV, 1, SSD_CONV_DIM), SSD_CONV ** -0.5),
        "ssd_conv_b": nrm((L, SSD_CONV_DIM), 0.01),
        "ssd_dt_bias": dt0 + jnp.log(-jnp.expm1(-dt0)),
        "ssd_a_log": jnp.log(uni((L, SSD_HEADS), 1.0, 16.0)),
        "ssd_d": 1.0 + nrm((L, SSD_HEADS), 0.1),
        "ssd_norm_g": 1.0 + nrm((L, SSD_WIDTH), 0.02),
        "rwkv_mu": uni((L, RWKV_IN), 0.0, 1.0),
        "rwkv_w0": uni((L, RWKV_WIDTH), -6.0, -1.0),
        "rwkv_w2": nrm((L, RWKV_DECAY_RANK, RWKV_WIDTH), 0.5 * RWKV_DECAY_RANK ** -0.5),
        "rwkv_a0": nrm((L, RWKV_WIDTH), 0.1),
        "rwkv_a2": nrm((L, RWKV_AAA_RANK, RWKV_WIDTH), RWKV_AAA_RANK ** -0.5),
        "rwkv_g2": nrm((L, RWKV_GATE_RANK, RWKV_WIDTH), RWKV_GATE_RANK ** -0.5),
        "rwkv_k_k": 0.85 + nrm((L, RWKV_WIDTH), 0.05),
        "rwkv_k_a": 1.0 + nrm((L, RWKV_WIDTH), 0.05),
        "rwkv_r_k": nrm((L, RWKV_HEADS, RWKV_HEAD_DIM), 0.1),
        "rwkv_ln_w": 1.0 + nrm((L, RWKV_WIDTH), 0.02),
        "rwkv_ln_b": nrm((L, RWKV_WIDTH), 0.01),
        "w_out": nrm((L, MIX_WIDTH, D_MODEL), MIX_WIDTH ** -0.5),
        "norm_x_g": 1.0 + nrm((L, D_MODEL), 0.02),
        "norm_mem_g": 1.0 + nrm((L, D_MODEL), 0.02),
        "xattn_wq": nrm((L, D_MODEL, D_MODEL), D_MODEL ** -0.5),
        "xattn_wk": nrm((L, D_MODEL, D_MODEL), D_MODEL ** -0.5),
        "xattn_wv": nrm((L, D_MODEL, D_MODEL), D_MODEL ** -0.5),
        "xattn_wo": nrm((L, D_MODEL, D_MODEL), D_MODEL ** -0.5),
        "norm_ffn_g": 1.0 + nrm((L, D_MODEL), 0.02),
        "ffn_w1": nrm((L, D_MODEL, D_FF), D_MODEL ** -0.5),
        "ffn_w2": nrm((L, D_FF, D_MODEL), D_FF ** -0.5),
        "final_norm_g": 1.0 + nrm((D_MODEL,), 0.02),
    }

def first_block(x, mem, norm_mix_g, w_in, ssd_conv_w, ssd_conv_b, ssd_dt_bias, ssd_a_log,
              ssd_d, ssd_norm_g, rwkv_mu, rwkv_w0, rwkv_w2, rwkv_a0, rwkv_a2, rwkv_g2,
              rwkv_k_k, rwkv_k_a, rwkv_r_k, rwkv_ln_w, rwkv_ln_b, w_out, norm_x_g,
              norm_mem_g, xattn_wq, xattn_wk, xattn_wv, xattn_wo, norm_ffn_g, ffn_w1,
              ffn_w2, final_norm_g):
    for l in range(DEPTH):
        h = rms_norm(x, norm_mix_g[l])
        u = h @ w_in[l]
        y_ssd = ssd_mixer(u[..., :SSD_IN], ssd_conv_w[l], ssd_conv_b[l], ssd_dt_bias[l],
                          ssd_a_log[l], ssd_d[l], ssd_norm_g[l])
        y_rwkv = rwkv7_mixer(u[..., SSD_IN:], rwkv_mu[l], rwkv_w0[l], rwkv_w2[l], rwkv_a0[l],
                             rwkv_a2[l], rwkv_g2[l], rwkv_k_k[l], rwkv_k_a[l], rwkv_r_k[l],
                             rwkv_ln_w[l], rwkv_ln_b[l])
        x = x + jnp.concatenate([y_ssd, y_rwkv], axis=-1) @ w_out[l]
        h = rms_norm(x, norm_x_g[l])
        m = rms_norm(mem, norm_mem_g[l])
        x = x + memory_cross_attention(h, m, xattn_wq[l], xattn_wk[l], xattn_wv[l], xattn_wo[l])
        h = rms_norm(x, norm_ffn_g[l])
        x = x + jnp.square(jax.nn.relu(h @ ffn_w1[l])) @ ffn_w2[l]
    return rms_norm(x, final_norm_g)


N_Q_HEADS = 16
N_KV_HEADS = 2
HEAD_DIM = 64
Q_PER_KV = N_Q_HEADS // N_KV_HEADS
WINDOW = 128
BLOCK = 128
ATTN_WIDTH = N_Q_HEADS * HEAD_DIM
KV_WIDTH = N_KV_HEADS * HEAD_DIM
SSM_GROUP = 16
SSM_GROUPS = 32
SSM_WIDTH = SSM_GROUP * SSM_GROUPS
SSM_STATE = 64
DT_MIN = 0.001
DT_MAX = 0.1
D_FF_2 = 5632
CONV_WIDTH = 3
RMS_EPS = 1e-6
IN_COLS = ATTN_WIDTH + 2 * KV_WIDTH + SSM_WIDTH + 2 * D_MODEL
SPLIT_POINTS = (ATTN_WIDTH, ATTN_WIDTH + KV_WIDTH, ATTN_WIDTH + 2 * KV_WIDTH,
                ATTN_WIDTH + 2 * KV_WIDTH + SSM_WIDTH,
                ATTN_WIDTH + 2 * KV_WIDTH + SSM_WIDTH + D_MODEL)
NEG_BIG = -1e30


def rms_norm_2(x, g):
    xf = x.astype(jnp.float32)
    y = xf * lax.rsqrt(jnp.mean(xf * xf, axis=-1, keepdims=True) + RMS_EPS)
    return (y * g.astype(jnp.float32)).astype(x.dtype)

def sliding_window_attention(q, k, v, sinks):
    b, l = q.shape[0], q.shape[1]
    nb = l // BLOCK
    qb = q.reshape(b, nb, BLOCK, N_KV_HEADS, Q_PER_KV, HEAD_DIM)
    kb = k.reshape(b, nb, BLOCK, N_KV_HEADS, HEAD_DIM)
    vb = v.reshape(b, nb, BLOCK, N_KV_HEADS, HEAD_DIM)

    def with_prev(t):
        prev = jnp.pad(t, ((0, 0), (1, 0), (0, 0), (0, 0), (0, 0)))[:, :-1]
        return jnp.concatenate([prev, t], axis=2)

    kx = with_prev(kb)
    vx = with_prev(vb)
    scores = jnp.einsum('bnqgrd,bnsgd->bngrqs', qb, kx).astype(jnp.float32) * (HEAD_DIM ** -0.5)
    q_idx = jnp.arange(BLOCK)[:, None]
    s_idx = jnp.arange(2 * BLOCK)[None, :]
    dist = q_idx + BLOCK - s_idx
    band = (dist >= 0) & (dist < WINDOW)
    valid = band[None] & ((jnp.arange(nb)[:, None, None] > 0) | (s_idx[None] >= BLOCK))
    slopes = 2.0 ** (-8.0 * jnp.arange(1, N_Q_HEADS + 1, dtype=jnp.float32) / N_Q_HEADS)
    slopes = slopes.reshape(N_KV_HEADS, Q_PER_KV)
    alibi = -slopes[:, :, None, None] * dist.astype(jnp.float32)[None, None]
    scores = scores + alibi[None, None]
    scores = jnp.where(valid[None, :, None, None], scores, NEG_BIG)
    sink = sinks.astype(jnp.float32).reshape(N_KV_HEADS, Q_PER_KV)[None, None, :, :, None, None]
    m = jnp.maximum(jnp.max(scores, axis=-1, keepdims=True), sink)
    p = jnp.exp(scores - m)
    p = p / (jnp.sum(p, axis=-1, keepdims=True) + jnp.exp(sink - m))
    out = jnp.einsum('bngrqs,bnsgd->bnqgrd', p.astype(v.dtype), vx)
    return out.reshape(b, l, ATTN_WIDTH)

def s5_ssm(u, a_re, a_im, log_dt, b_re, b_im, c_re, c_im, d_skip):
    bsz, l = u.shape[0], u.shape[1]
    ug = u.reshape(bsz, l, SSM_GROUPS, SSM_GROUP)
    dt = jnp.exp(log_dt)[:, None]
    mag = jnp.exp(a_re * dt)
    ab_re = mag * jnp.cos(a_im * dt)
    ab_im = mag * jnp.sin(a_im * dt)
    nr = ab_re - 1.0
    ni = ab_im
    den = a_re * a_re + a_im * a_im
    z_re = (nr * a_re + ni * a_im) / den
    z_im = (ni * a_re - nr * a_im) / den
    bb_re = z_re[..., None] * b_re - z_im[..., None] * b_im
    bb_im = z_re[..., None] * b_im + z_im[..., None] * b_re
    bu_re = jnp.einsum('gph,blgh->blgp', bb_re, ug)
    bu_im = jnp.einsum('gph,blgh->blgp', bb_im, ug)
    a_re_t = jnp.broadcast_to(ab_re, bu_re.shape)
    a_im_t = jnp.broadcast_to(ab_im, bu_im.shape)

    def combine(left, right):
        a1r, a1i, b1r, b1i = left
        a2r, a2i, b2r, b2i = right
        return (a1r * a2r - a1i * a2i,
                a1r * a2i + a1i * a2r,
                a2r * b1r - a2i * b1i + b2r,
                a2r * b1i + a2i * b1r + b2i)

    _, _, xs_re, xs_im = lax.associative_scan(combine, (a_re_t, a_im_t, bu_re, bu_im), axis=1)
    y = (jnp.einsum('ghp,blgp->blgh', c_re, xs_re)
         - jnp.einsum('ghp,blgp->blgh', c_im, xs_im)
         + d_skip.reshape(SSM_GROUPS, SSM_GROUP) * ug)
    return y.reshape(bsz, l, SSM_WIDTH)

def causal_depthwise_conv_2(x, w, b):
    l = x.shape[1]
    xp = jnp.pad(x, ((0, 0), (CONV_WIDTH - 1, 0), (0, 0)))
    y = b
    for k in range(CONV_WIDTH):
        y = y + w[k] * xp[:, k:k + l]
    return y

def second_inputs(seed: int = 0) -> dict:
    key = jax.random.key(seed)
    ks = jax.random.split(key, 24)
    f32 = jnp.float32
    nrm = lambda k, shape, s: jax.random.normal(k, shape, f32) * s
    x = jax.random.normal(ks[0], (BATCH, SEQ, D_MODEL), f32)
    attn_norm_g = 1.0 + nrm(ks[1], (DEPTH, D_MODEL), 0.02)
    w_in = nrm(ks[2], (DEPTH, D_MODEL, IN_COLS), D_MODEL ** -0.5)
    b_in = nrm(ks[3], (DEPTH, IN_COLS), 0.02)
    attn_sinks = nrm(ks[4], (DEPTH, N_Q_HEADS), 0.5)
    ssm_a_re = -0.5 + nrm(ks[5], (DEPTH, SSM_GROUPS, SSM_STATE), 0.01)
    ssm_a_im = (jnp.pi * jnp.arange(SSM_STATE, dtype=f32))[None, None, :] + nrm(ks[6], (DEPTH, SSM_GROUPS, SSM_STATE), 0.01)
    ssm_log_dt = jax.random.uniform(ks[7], (DEPTH, SSM_GROUPS), f32, minval=math.log(DT_MIN), maxval=math.log(DT_MAX))
    ssm_b_re = nrm(ks[8], (DEPTH, SSM_GROUPS, SSM_STATE, SSM_GROUP), (2 * SSM_GROUP) ** -0.5)
    ssm_b_im = nrm(ks[9], (DEPTH, SSM_GROUPS, SSM_STATE, SSM_GROUP), (2 * SSM_GROUP) ** -0.5)
    ssm_c_re = nrm(ks[10], (DEPTH, SSM_GROUPS, SSM_GROUP, SSM_STATE), (2 * SSM_STATE) ** -0.5)
    ssm_c_im = nrm(ks[11], (DEPTH, SSM_GROUPS, SSM_GROUP, SSM_STATE), (2 * SSM_STATE) ** -0.5)
    ssm_d = nrm(ks[12], (DEPTH, SSM_WIDTH), 1.0)
    w_glu = nrm(ks[13], (DEPTH, SSM_WIDTH, 2 * SSM_WIDTH), SSM_WIDTH ** -0.5)
    b_glu = nrm(ks[14], (DEPTH, 2 * SSM_WIDTH), 0.02)
    w_branch_attn = nrm(ks[15], (DEPTH, ATTN_WIDTH, D_MODEL), ATTN_WIDTH ** -0.5)
    w_branch_ssm = nrm(ks[16], (DEPTH, SSM_WIDTH, D_MODEL), SSM_WIDTH ** -0.5)
    w_out = nrm(ks[17], (DEPTH, D_MODEL, D_MODEL), D_MODEL ** -0.5)
    ffn_norm_g = 1.0 + nrm(ks[18], (DEPTH, D_MODEL), 0.02)
    w_up = nrm(ks[19], (DEPTH, D_MODEL, 2 * D_FF_2), D_MODEL ** -0.5)
    conv_w = nrm(ks[20], (DEPTH, CONV_WIDTH, D_FF_2), CONV_WIDTH ** -0.5)
    conv_b = nrm(ks[21], (DEPTH, D_FF_2), 0.02)
    w_down = nrm(ks[22], (DEPTH, D_FF_2, D_MODEL), D_FF_2 ** -0.5)
    final_norm_g = 1.0 + nrm(ks[23], (D_MODEL,), 0.02)
    return {"x": x, "attn_norm_g": attn_norm_g, "w_in": w_in, "b_in": b_in, "attn_sinks": attn_sinks,
            "ssm_a_re": ssm_a_re, "ssm_a_im": ssm_a_im, "ssm_log_dt": ssm_log_dt,
            "ssm_b_re": ssm_b_re, "ssm_b_im": ssm_b_im, "ssm_c_re": ssm_c_re, "ssm_c_im": ssm_c_im,
            "ssm_d": ssm_d, "w_glu": w_glu, "b_glu": b_glu, "w_branch_attn": w_branch_attn,
            "w_branch_ssm": w_branch_ssm, "w_out": w_out, "ffn_norm_g": ffn_norm_g, "w_up": w_up,
            "conv_w": conv_w, "conv_b": conv_b, "w_down": w_down, "final_norm_g": final_norm_g}

def second_block(x, attn_norm_g, w_in, b_in, attn_sinks, ssm_a_re, ssm_a_im, ssm_log_dt, ssm_b_re, ssm_b_im,
              ssm_c_re, ssm_c_im, ssm_d, w_glu, b_glu, w_branch_attn, w_branch_ssm, w_out, ffn_norm_g,
              w_up, conv_w, conv_b, w_down, final_norm_g):
    bsz, seq = x.shape[0], x.shape[1]
    for i in range(DEPTH):
        h = rms_norm_2(x, attn_norm_g[i])
        proj = h @ w_in[i] + b_in[i]
        q, k, v, u, gate_attn, gate_ssm = jnp.split(proj, SPLIT_POINTS, axis=-1)
        q = q.reshape(bsz, seq, N_Q_HEADS, HEAD_DIM)
        k = k.reshape(bsz, seq, N_KV_HEADS, HEAD_DIM)
        v = v.reshape(bsz, seq, N_KV_HEADS, HEAD_DIM)
        attn = sliding_window_attention(q, k, v, attn_sinks[i])
        y = s5_ssm(u, ssm_a_re[i], ssm_a_im[i], ssm_log_dt[i], ssm_b_re[i], ssm_b_im[i],
                   ssm_c_re[i], ssm_c_im[i], ssm_d[i])
        y_val, y_gate = jnp.split(jax.nn.gelu(y, approximate=False) @ w_glu[i] + b_glu[i], 2, axis=-1)
        ssm = y_val * jax.nn.sigmoid(y_gate)
        merged = (jax.nn.sigmoid(gate_attn) * (attn @ w_branch_attn[i])
                  + jax.nn.sigmoid(gate_ssm) * (ssm @ w_branch_ssm[i]))
        x = x + merged @ w_out[i]
        h = rms_norm_2(x, ffn_norm_g[i])
        val, gate = jnp.split(h @ w_up[i], 2, axis=-1)
        gate = causal_depthwise_conv_2(gate, conv_w[i], conv_b[i])
        x = x + (val * jax.nn.gelu(gate, approximate=False)) @ w_down[i]
    return rms_norm_2(x, final_norm_g)


def setup_inputs(seed=0):
    out = dict(first_inputs(seed))
    for name, value in second_inputs(seed + 1).items():
        if name != "x":
            out[name + "_2"] = value
    return out


def reference(
    x, mem, norm_mix_g, w_in, ssd_conv_w, ssd_conv_b, ssd_dt_bias, ssd_a_log, ssd_d, ssd_norm_g,
    rwkv_mu, rwkv_w0, rwkv_w2, rwkv_a0, rwkv_a2, rwkv_g2, rwkv_k_k, rwkv_k_a, rwkv_r_k,
    rwkv_ln_w, rwkv_ln_b, w_out, norm_x_g, norm_mem_g, xattn_wq, xattn_wk, xattn_wv, xattn_wo,
    norm_ffn_g, ffn_w1, ffn_w2, final_norm_g, attn_norm_g_2, w_in_2, b_in_2, attn_sinks_2,
    ssm_a_re_2, ssm_a_im_2, ssm_log_dt_2, ssm_b_re_2, ssm_b_im_2, ssm_c_re_2, ssm_c_im_2,
    ssm_d_2, w_glu_2, b_glu_2, w_branch_attn_2, w_branch_ssm_2, w_out_2, ffn_norm_g_2, w_up_2,
    conv_w_2, conv_b_2, w_down_2, final_norm_g_2,
):
    x = first_block(
        x, mem, norm_mix_g, w_in, ssd_conv_w, ssd_conv_b, ssd_dt_bias, ssd_a_log, ssd_d,
        ssd_norm_g, rwkv_mu, rwkv_w0, rwkv_w2, rwkv_a0, rwkv_a2, rwkv_g2, rwkv_k_k, rwkv_k_a,
        rwkv_r_k, rwkv_ln_w, rwkv_ln_b, w_out, norm_x_g, norm_mem_g, xattn_wq, xattn_wk,
        xattn_wv, xattn_wo, norm_ffn_g, ffn_w1, ffn_w2, final_norm_g,
    )
    return second_block(
        x, attn_norm_g_2, w_in_2, b_in_2, attn_sinks_2, ssm_a_re_2, ssm_a_im_2, ssm_log_dt_2,
        ssm_b_re_2, ssm_b_im_2, ssm_c_re_2, ssm_c_im_2, ssm_d_2, w_glu_2, b_glu_2,
        w_branch_attn_2, w_branch_ssm_2, w_out_2, ffn_norm_g_2, w_up_2, conv_w_2, conv_b_2,
        w_down_2, final_norm_g_2,
    )


_drawn_inputs = setup_inputs


def setup_inputs(seed=0):
    import zlib

    import numpy as np

    out = dict(_drawn_inputs(seed))
    spreads = {}
    factors = {'ssd_conv_b': 5.883,
     'ssd_norm_g': 4.377,
     'rwkv_w2': 6.392,
     'rwkv_a0': 3.647,
     'rwkv_k_k': 4.021,
     'rwkv_k_a': 2.707,
     'rwkv_ln_w': 7.649,
     'rwkv_ln_b': 8.0,
     'norm_x_g': 8.0,
     'norm_mem_g': 8.0,
     'norm_ffn_g': 2.973,
     'attn_norm_g_2': 6.805,
     'b_in_2': 4.392,
     'attn_sinks_2': 17.051,
     'ssm_a_re_2': 64.0,
     'ssm_a_im_2': 30.192,
     'ssm_log_dt_2': 37.48,
     'ssm_b_re_2': 41.376,
     'ssm_b_im_2': 46.216,
     'ssm_c_re_2': 42.456,
     'ssm_c_im_2': 42.584,
     'b_glu_2': 8.0,
     'ffn_norm_g_2': 3.642,
     'conv_b_2': 5.382,
     'final_norm_g_2': 7.755}
    for name, (base, spread) in spreads.items():
        noise = np.random.default_rng([zlib.crc32(name.encode()), seed]).standard_normal(out[name].shape)
        drawn = base * np.exp(spread * noise) if base else spread * noise
        out[name] = __import__('jax').numpy.asarray(drawn.astype(out[name].dtype))
    for name, factor in factors.items():
        out[name] = (out[name] * factor).astype(out[name].dtype)
    return out
```

```python
from contextlib import ExitStack
from dataclasses import dataclass

import numpy as np

import concourse.bass as bass
from concourse import mybir

F32 = mybir.dt.float32
F32R = mybir.dt.float32r
I32 = mybir.dt.int32
ACT = mybir.ActivationFunctionType
ALU = mybir.AluOpType
AX = mybir.AxisListType

P = 128
T = 256
D = 2048
KT = D // P
EPS = 1e-6
UNIT = 256
CK = 4
RING = 4

RW = 1024 // P
R0, K0, V0, PG0, PW0, PA0 = 0, RW, 2 * RW, 3 * RW, 3 * RW + 2, 3 * RW + 3
RWKV_TILES = 3 * RW + 4
Z0 = RWKV_TILES
XS0 = Z0 + RW
B0 = XS0 + RW
C0 = B0 + 2
U_TILES = C0 + 2
RANK = 96
DT_ROW = RANK
NH = 16
Q = 128
NCH = T // Q
LEVELS = 7
E_HALF = float(np.exp(-0.5))
RWKV_EPS = 64e-5
XH, XD = 4, 512

Q2, K2, V2, S2, GA2, GS2 = 0, 8, 9, 10, 14, 30
U2_TILES = 46
FF2 = 5632
FT2 = FF2 // P
ST = 16
LN2 = float(np.log(2.0))

CONST_COLS = {}
for _i, _n in enumerate(["ident", "upper", "upper_in", "lower", "ones", "half_ones", "top_left"]
                        + [f"lev{k}" for k in range(LEVELS)] + ["dist", "dist_b"]):
    CONST_COLS[_n] = _i * P


def constants():
    i, j = np.arange(P)[:, None], np.arange(P)[None, :]
    lev = [((i >> (k + 1)) == (j >> (k + 1))) & (((j >> k) & 1) == 1) & (((i >> k) & 1) == 0)
           for k in range(LEVELS)]
    dist = (i + P - np.arange(2 * P)[None, :]).astype(np.float32)
    dist = np.where((dist >= 0) & (dist < P), dist, 1e32)
    parts = [i == j, i < j, i <= j, i > j, i >= 0 * j, (i // 64) == (j // 64), lev[0].T] + lev
    return np.concatenate([np.asarray(m, np.float32) * np.ones((P, P), np.float32) for m in parts]
                          + [dist.astype(np.float32)], axis=1)


class Params:

    def __init__(self):
        self.at, self.n = {}, 0

    def add(self, name, cols):
        self.at[name] = (self.n, cols)
        self.n += cols


PARAMS = Params()
for _name, _cols in [
    ("norm_mix_g", KT), ("norm_x_g", KT), ("norm_mem_g", KT), ("norm_ffn_g", KT),
    ("norm2_g", KT), ("ffn2_g", KT), ("final1_g", KT), ("final2_g", KT),
    ("mu", RWKV_TILES), ("conv", 4 * 12), ("convb", 12), ("ssd_d", RW), ("ssd_g", RW),
    ("w0", RW), ("a0", RW), ("k_k", RW), ("k_a", RW), ("r_k", RW), ("ln_w", RW), ("ln_b", RW),
    ("dt_bias", NH), ("a_log", NH), ("sinks", NH), ("slopes", NH),
    ("b_in", U2_TILES), ("b_glu", 8), ("c2", 3 * FT2), ("c2b", FT2),
    ("are", ST), ("aim", ST), ("ldt", ST), ("d2", 4),
]:
    PARAMS.add(_name, _cols)


@dataclass
class Phase:
    name: str
    w: object
    units: int
    nc: int
    body: int
    act: object
    kind: str
    out: object = None
    t0: int = 0
    src: object = None
    g: str = ""
    g0: int = 0
    p0: int = 0
    taps: int = 0
    after: object = None
    x_after: int = 0
    w0: int = 0
    sum_after: bool = False
    norm: int = 0
    base: object = None
    k: object = None


@dataclass
class Kind:
    links: int = 0
    evac: int = 0
    fin: int = 0
    pool: int = 0
    alink: int = 0

    def counts(self):
        return dict(links=self.links, evac=self.evac, fin=self.fin, pool=self.pool, alink=self.alink)


KINDS = {
    "rwkv": Kind(2, 1), "z": Kind(0, 1, 1), "conv": Kind(4, 1, 1), "acc": Kind(1),
    "resid": Kind(1, 0, 1, 1, 1), "emit": Kind(0, 0, 1, 1, 1), "sumsq": Kind(1, 0, 1, 1),
    "relu2": Kind(1, 1, 1, 1), "gate": Kind(3, 1, 1), "val": Kind(1, 1, 1, 1),
    "scaled": Kind(0, 1), "plain": Kind(), "tok": Kind(), "bias": Kind(1, 1), "sigmoid": Kind(0, 1, 1),
    "glu_gate": Kind(0, 0, 1), "glu_val": Kind(0, 1, 1, 1), "br_attn": Kind(0, 1),
    "br_ssm": Kind(1, 1, 1, 1),
}
SPLITS = ("resid", "emit", "relu2", "val", "glu_val", "br_ssm")


def at_least(eng, s, value):
    if not (isinstance(value, int) and value < 1):
        eng.wait_ge(s, value)


def pair(buf, v, t0=0):
    return buf[:, t0 + 2 * v:t0 + 2 * v + 2] if isinstance(v, int) else buf[:, bass.ds(v * 2 + t0, 2)]


def tile(buf, i):
    return buf[:, i, :] if isinstance(i, int) else buf[:, bass.ds(i, 1), :].rearrange("p a t -> p (a t)")


class Stream:

    def __init__(self, nc, stack, dram):
        self.nc, self.dram = nc, dram

        def sb(name, shape, dt=F32):
            return stack.enter_context(nc.sbuf_tensor(name, shape, dt))

        def sem(name):
            return stack.enter_context(nc.semaphore(name))

        self.x = sb("x", [P, KT, T])
        self.a0 = sb("a0", [P, KT, 2, T], F32R)
        self.consts = sb("consts", [P, dram["consts"].shape[1]])
        self.prm = sb("prm", [P, PARAMS.n])
        self.rstd = sb("rstd", [P, T])
        self.root = sb("root", [P, T])
        self.sq = sb("sq", [P, 2, T])
        self.eps = sb("eps", [P, 2])
        self.acc = stack.enter_context(nc.psum_tensor("acc", [P, 4, 512], F32))
        self.work = stack.enter_context(nc.psum_tensor("work", [P, 4, 512], F32))

        self.s_raw = [sem(f"raw_loaded{i}") for i in range(RING)]
        self.s_hi = sem("high_split")
        self.s_lo = sem("low_split")
        self.s_used = sem("chunk_multiplied")
        self.s_free = sem("banks_read")
        self.s_link = sem("vector_link")
        self.s_evac = sem("evacuated")
        self.s_alink = sem("scaled_copy")
        self.s_fin = sem("finished")
        self.s_pool = sem("low_written")
        self.s_sum = sem("squares_summed")
        self.s_root = sem("root_ready")
        self.s_rstd = sem("rstd_ready")
        self.total = dict(c=0, u=0, links=0, evac=0, fin=0, pool=0, alink=0, norm=0)

    def const(self, name, n=P):
        return self.consts[:, CONST_COLS[name]:CONST_COLS[name] + n]

    def par(self, name, i=None, n=1):
        at, cols = PARAMS.at[name]
        if i is None:
            return self.prm[:, at:at + cols]
        return self.prm[:, at + i:at + i + n] if isinstance(i, int) else self.prm[:, bass.ds(i + at, n)]

    def ring(self, stack, tag):
        nc = self.nc

        def sb(name, shape, dt=F32):
            return stack.enter_context(nc.sbuf_tensor(name + tag, shape, dt))
        self.raw = sb("raw", [P, RING, CK * UNIT])
        self.hi = sb("hi", [P, RING, CK * UNIT], F32R)
        self.lo = sb("lo", [P, RING, CK * UNIT], F32R)
        self.ta = sb("ta", [P, 2, T])
        self.tb = sb("tb", [P, 2, 2, T + 4])
        self.th = sb("th", [P, 2, 2, T])
        self.tq = sb("tq", [P, 2, T])

    def phase(self, name, w, units, nc_, body, act, kind, **kw):
        ph = Phase(name, self.dram.get(w), units, nc_, body, act, kind, **kw)
        k = KINDS[kind]
        t = self.total
        ph.base = dict(t)
        ph.k = k
        if kind != "emit":
            t["c"] += units * nc_
            t["u"] += units
        for f, a_unit in k.counts().items():
            t[f] += units * a_unit
        if ph.sum_after:
            t["norm"] += 1
            ph.norm = t["norm"]
        return ph

    def loop(self, eng, ph, step):
        bodies = ph.units // ph.body
        if bodies:
            for j in range(ph.body):
                step(j, j)
        if bodies > 1:
            with eng.Fori(1, bodies) as i:
                for j in range(ph.body):
                    step(i * ph.body + j, j)
        for j in range(ph.units - bodies * ph.body):
            step(bodies * ph.body + j, j)

    def sp(self, eng, ph, skip=0):
        def step(v, j):
            for k in range(ph.nc):
                c = (v - j) * ph.nc + (j * ph.nc + k)
                if not (isinstance(c, int) and c < skip):
                    self.load(eng, ph, c, j * ph.nc + k)
        self.loop(eng, ph, step)

    def load(self, eng, ph, c, n):
        slot = (ph.base["c"] + n) % RING
        at_least(eng, self.s_lo, c + (ph.base["c"] - RING + 1))
        eng.dma_start(self.raw[:, slot, :], ph.w[c + ph.w0]).then_inc(self.s_raw[slot], 16)

    def prefetch(self, eng, ph):
        for c in range(RING):
            self.load(eng, ph, c, c)

    def act(self, eng, phs, before=None):
        last = None
        for ph in phs:
            def step(v, j, ph=ph, last=last):
                self.act_split(eng, ph, v, j)
                if isinstance(v, int) and v == 1 and ph.sum_after:
                    eng.wait_ge(self.s_sum, ph.norm)
                    eng.activation(self.root[:], self.work[:, 3, 0:T], ACT.Sqrt, scale=1.0 / D,
                                   bias=self.eps[:, 0:1]).then_inc(self.s_root, 1)
                if not (isinstance(v, int) and v == 0):
                    self.act_finish(eng, ph, v - 1, (ph.base["u"] + j - 1) % 2)
                elif last:
                    self.act_finish(eng, last, last.units - 1, (last.base["u"] + last.units - 1) % 2)
            self.loop(eng, ph, step)
            last = ph
        self.act_finish(eng, last, last.units - 1, (last.base["u"] + last.units - 1) % 2)

    def act_split(self, eng, ph, v, j):
        c0 = ph.base["c"]
        for k in range(ph.nc):
            n = j * ph.nc + k
            slot = (c0 + n) % RING
            eng.wait_ge(self.s_raw[slot], (v - j) * ph.nc * (16 // RING) + 16 * ((c0 + n) // RING + 1))
            at_least(eng, self.s_used, (v - j) * ph.nc + (c0 + n - RING + 1))
            eng.activation(self.hi[:, slot, :], self.raw[:, slot, :], ACT.Copy).then_inc(self.s_hi, 1)

    def act_finish(self, eng, ph, v, s):
        k, b, kind = ph.k, ph.base, ph.kind
        if not k.fin:
            return
        if k.evac:
            eng.wait_ge(self.s_evac, v + (b["evac"] + 1))
        elif kind != "emit":
            eng.wait_ge(self.s_free, v + (b["u"] + 1))
        done = self.s_fin
        if kind in ("resid", "emit", "sumsq"):
            at_least(eng, self.s_pool, v + b["pool"])
            if kind == "sumsq":
                eng.activation(self.tq[:], pair(self.x, v), ACT.Square).then_inc(done, 1)
                return
            for t in range(2):
                ins = eng.activation(self.th[:, s, t, :], tile(self.x, v * 2 + t), ACT.Copy,
                                     scale=self.par(ph.g, v * 2 + t))
            ins.then_inc(self.s_alink, 1)
            eng.activation(self.tq[:], pair(self.x, v), ACT.Square)
            eng.wait_ge(self.s_alink, v + (b["alink"] + 1))
        if kind in SPLITS:
            eng.activation(pair(ph.out, v, ph.t0)[:, :, 0, :], self.th[:, s], ACT.Copy).then_inc(done, 1)
        elif kind == "z":
            eng.activation(pair(ph.out, v, ph.t0), self.tb[:, s, :, 3:3 + T], ACT.Silu).then_inc(done, 1)
        elif kind == "conv":
            eng.activation(pair(ph.out, v, ph.t0), self.th[:, s], ACT.Silu).then_inc(done, 1)
        elif kind == "gate":
            eng.activation(pair(ph.out, v, ph.t0), self.th[:, s], ACT.Gelu).then_inc(done, 1)
        elif kind in ("sigmoid", "glu_gate"):
            for t in range(2):
                ins = eng.activation(tile(ph.out, v * 2 + (ph.t0 + t)), self.tb[:, s, t, 3:3 + T],
                                     ACT.Sigmoid, bias=self.par(ph.g, v * 2 + (ph.g0 + t)))
            ins.then_inc(done, 1)

    def dve(self, eng, phs):
        last = None
        for ph in phs:
            def step(v, j, ph=ph, last=last):
                for k in range(ph.nc):
                    n = j * ph.nc + k
                    slot = (ph.base["c"] + n) % RING
                    eng.wait_ge(self.s_hi, (v - j) * ph.nc + (ph.base["c"] + n + 1))
                    eng.tensor_tensor(self.lo[:, slot, :], self.raw[:, slot, :],
                                      self.hi[:, slot, :].bitcast(F32), ALU.subtract).then_inc(self.s_lo, 1)
                if isinstance(v, int) and v == 1 and ph.sum_after:
                    eng.wait_ge(self.s_root, ph.norm)
                    eng.reciprocal(self.rstd[:], self.root[:]).then_inc(self.s_rstd, 1)
                    eng.wait_ge(self.s_rstd, ph.norm)
                if not (isinstance(v, int) and v == 0):
                    self.evacuate(eng, ph, v - 1, (ph.base["u"] + j - 1) % 2)
                elif last:
                    self.evacuate(eng, last, last.units - 1, (last.base["u"] + last.units - 1) % 2)
            self.loop(eng, ph, step)
            last = ph
        self.evacuate(eng, last, last.units - 1, (last.base["u"] + last.units - 1) % 2)

    def evacuate(self, eng, ph, v, s):
        k, b, kind = ph.k, ph.base, ph.kind
        banks = self.acc[:, 2 * s:2 * s + 2, :]
        halves = banks.rearrange("p t (h n) -> p t n h", h=2)
        eng.wait_ge(self.s_used, v * ph.nc + (b["c"] + ph.nc))
        at_least(eng, self.s_evac, v * k.evac + b["evac"])
        at_least(eng, self.s_free, v + b["u"])
        free = v + (b["u"] + 1)
        steps = [0]

        def link(ins):
            steps[0] += 1
            ins.then_inc(self.s_link, 1)
            eng.wait_ge(self.s_link, v * k.links + (b["links"] + steps[0]))

        if kind in ("resid", "acc", "sumsq"):
            xp = pair(self.x, v)
            if isinstance(v, int) and v < 2 and ph.x_after:
                eng.wait_ge(self.s_fin, ph.x_after)
            link(eng.tensor_tensor(xp, banks[:, :, 0:T], xp, ALU.add))
            eng.tensor_tensor(xp, banks[:, :, T:2 * T], xp, ALU.add).then_inc(self.s_free, 1)
            return
        if kind == "plain":
            eng.tensor_reduce(pair(ph.out, v, ph.t0), halves, AX.X, ALU.add).then_inc(self.s_free, 1)
            return
        if kind == "tok":
            at = bass.ds(v * UNIT, UNIT) if not isinstance(v, int) else slice(v * UNIT, (v + 1) * UNIT)
            eng.tensor_copy(ph.out[:, :, at], banks[:, :, 0:T]).then_inc(self.s_free, 1)
            return
        if k.fin:
            at_least(eng, self.s_fin, v + (b["fin"] - 1))
        elif isinstance(v, int) and v < 2:
            at_least(eng, self.s_fin, v + (b["fin"] - 1))
        if k.pool:
            at_least(eng, self.s_pool, v + (b["pool"] - 1))
        elif isinstance(v, int) and v < 2:
            at_least(eng, self.s_pool, v + (b["pool"] - 1))
        cur = self.tb[:, s, :, 3:3 + T]
        if kind == "glu_gate":
            eng.tensor_reduce(cur, halves, AX.X, ALU.add).then_inc(self.s_free, 1)
            return
        eng.tensor_reduce(self.ta[:], halves, AX.X, ALU.add).then_inc(self.s_free, 1)
        eng.wait_ge(self.s_free, free)
        th = self.th[:, s]
        if kind == "br_attn":
            eng.tensor_tensor(pair(ph.out, v, ph.t0), self.ta[:], pair(ph.out, v, ph.t0),
                              ALU.mult).then_inc(self.s_evac, 1)
            return
        if kind == "br_ssm":
            link(eng.tensor_tensor(cur, self.ta[:], pair(ph.src, v, ph.g0), ALU.mult))
            eng.tensor_tensor(th, cur, pair(ph.src, v), ALU.add).then_inc(self.s_evac, 1)
            return
        if kind == "glu_val":
            for t in range(2):
                ins = eng.scalar_tensor_tensor(out=self.th[:, s, t, :], in0=self.ta[:, t, :],
                                               scalar=self.par("b_glu", v * 2 + t),
                                               in1=tile(ph.src, v * 2 + t), op0=ALU.add, op1=ALU.mult)
            ins.then_inc(self.s_evac, 1)
            return
        rs = self.rstd[:].unsqueeze(1).to_broadcast([P, 2, T])
        if kind == "scaled":
            eng.tensor_tensor(pair(ph.out, v, ph.t0), self.ta[:], rs, ALU.mult).then_inc(self.s_evac, 1)
            return
        scale = eng.tensor_tensor(cur, self.ta[:], rs, ALU.mult)
        if kind in ("z", "sigmoid"):
            scale.then_inc(self.s_evac, 1)
            return
        link(scale)
        if kind == "rwkv":
            link(eng.tensor_tensor(self.ta[:], self.tb[:, s, :, 2:2 + T], cur, ALU.subtract))
            for t in range(2):
                ins = eng.scalar_tensor_tensor(out=tile(ph.out, v * 2 + (ph.t0 + t)), in0=self.ta[:, t, :],
                                               scalar=self.par("mu", v * 2 + t), in1=cur[:, t, :],
                                               op0=ALU.mult, op1=ALU.add)
            ins.then_inc(self.s_evac, 1)
        elif kind in ("conv", "gate"):
            taps = ph.taps
            for t in range(2):
                ins = eng.tensor_scalar(self.th[:, s, t, :], cur[:, t, :],
                                        self.par(ph.g, v * (2 * taps) + (ph.g0 + t * taps + taps - 1)),
                                        self.par(ph.g + "b", v * 2 + (ph.p0 + t)), ALU.mult, ALU.add)
            link(ins)
            for q in range(taps - 1):
                for t in range(2):
                    ins = eng.scalar_tensor_tensor(
                        out=self.th[:, s, t, :], in0=self.tb[:, s, t, 4 - taps + q:4 - taps + q + T],
                        scalar=self.par(ph.g, v * (2 * taps) + (ph.g0 + t * taps + q)),
                        in1=self.th[:, s, t, :], op0=ALU.mult, op1=ALU.add)
                if q < taps - 2:
                    link(ins)
            ins.then_inc(self.s_evac, 1)
        elif kind == "relu2":
            eng.scalar_tensor_tensor(out=th, in0=cur, scalar=0.0, in1=cur, op0=ALU.max,
                                     op1=ALU.mult).then_inc(self.s_evac, 1)
        elif kind == "val":
            eng.tensor_tensor(th, cur, pair(ph.src, v), ALU.mult).then_inc(self.s_evac, 1)
        elif kind == "bias":
            for t in range(2):
                ins = eng.tensor_scalar(tile(ph.out, v * 2 + (ph.t0 + t)), cur[:, t, :],
                                        self.par(ph.g, v * 2 + (ph.g0 + t)), None, ALU.add)
            ins.then_inc(self.s_evac, 1)

    def pool(self, eng, phs):
        for ph in phs:
            if ph.k.pool:
                def step(v, j, ph=ph):
                    self.pool_finish(eng, ph, v, (ph.base["u"] + j) % 2)
                self.loop(eng, ph, step)

    def pool_finish(self, eng, ph, v, s):
        b = ph.base
        eng.wait_ge(self.s_fin, v + (b["fin"] + 1))
        if ph.kind in ("resid", "emit", "sumsq"):
            if isinstance(v, int) and v == 0:
                at_least(eng, self.s_sum, b["norm"])
                ins = eng.tensor_copy(self.sq[:], self.tq[:])
            else:
                at_least(eng, self.s_pool, v + b["pool"])
                ins = eng.tensor_tensor(self.sq[:], self.sq[:], self.tq[:], ALU.add)
            if ph.kind == "sumsq":
                ins.then_inc(self.s_pool, 1)
                return
        out = pair(ph.out, v, ph.t0)
        eng.tensor_tensor(out[:, :, 1, :], self.th[:, s], out[:, :, 0, :].bitcast(F32),
                          ALU.subtract).then_inc(self.s_pool, 1)

    def pe(self, eng, phs):
        for ph in phs:
            def step(v, j, ph=ph):
                self.unit(eng, ph, v, j)
                if isinstance(v, int) and v == 0 and ph.sum_after:
                    self.sum_squares(eng, ph)
            self.loop(eng, ph, step)

    def unit(self, eng, ph, v, j):
        b = ph.base
        s = (b["u"] + j) % 2
        at_least(eng, self.s_free, v + (b["u"] - 1))
        for k in range(ph.nc):
            n = j * ph.nc + k
            slot = (b["c"] + n) % RING
            eng.wait_ge(self.s_lo, (v - j) * ph.nc + (b["c"] + n + 1))
            if isinstance(v, int) and v == 0 and ph.after:
                eng.wait_ge(self.s_pool, ph.after.base["pool"] + 2 * (k + 1))
            for t in range(2):
                bank = self.acc[:, 2 * s + t, :]
                for q in range(CK):
                    kt = CK * k + q
                    first, final = kt == 0, kt == CK * ph.nc - 1
                    a = ph.act[:, kt]
                    if ph.kind == "tok":
                        cols = slice(q * UNIT, (q + 1) * UNIT)
                        toks = slice(t * P, (t + 1) * P)
                        eng.matmul(bank[:, 0:UNIT], a[:, 0, toks], self.hi[:, slot, cols], start=first, stop=False)
                        eng.matmul(bank[:, 0:UNIT], a[:, 1, toks], self.hi[:, slot, cols], start=False, stop=False)
                        ins = eng.matmul(bank[:, 0:UNIT], a[:, 0, toks], self.lo[:, slot, cols],
                                         start=False, stop=final)
                    else:
                        cols = slice(q * UNIT + t * P, q * UNIT + (t + 1) * P)
                        eng.matmul(bank, self.hi[:, slot, cols], a.rearrange("p h n -> p (h n)"),
                                   start=first, stop=False)
                        ins = eng.matmul(bank[:, 0:T], self.lo[:, slot, cols], a[:, 0, :],
                                         start=False, stop=final)
            ins.then_inc(self.s_used, 1)

    def sum_squares(self, eng, ph):
        eng.wait_ge(self.s_pool, ph.base["pool"])
        at_least(eng, self.s_root, ph.norm - 1)
        for t in range(2):
            ins = eng.matmul(self.work[:, 3, 0:T], self.const("ones"), self.sq[:, t, :],
                             start=t == 0, stop=t == 1)
        ins.then_inc(self.s_sum, 1)


def semaphores(nc, stack):
    taken = []

    def release():
        nc.clear_and_free_semaphores(taken)
        nc.all_engine_barrier()
    stack.callback(release)

    def sem(name):
        taken.append(nc.alloc_semaphore(name=name))
        return taken[-1]
    return sem


class Link:

    def __init__(self, eng, s):
        self.eng, self.s, self.n = eng, s, 0

    def __call__(self, ins):
        self.n += 1
        ins.then_inc(self.s, 1)
        self.eng.wait_ge(self.s, self.n)


def over(ap, n):
    return ap.unsqueeze(1).to_broadcast([ap.shape[0], n, ap.shape[1]])


def spread(ap, n):
    return ap.unsqueeze(2).to_broadcast([ap.shape[0], ap.shape[1], n])


def rwkv_prepare(nc, dram, s, u, b):
    with ExitStack() as st:
        sem = semaphores(nc, st)
        w2 = alloc(nc, st, "w2", [P, 1024])
        a2 = alloc(nc, st, "a2", [P, 1024])
        f2 = alloc(nc, st, "f2", [P, 2 * RW, Q + 1])
        mid = alloc(nc, st, "mid", [P, 2 * RW])
        karg = alloc(nc, st, "karg", [P, RW])
        f1, kk, bb, kr, vt, bt, kt, sfac = (b[n] for n in ("f1", "kk", "bb", "kr", "vt", "bt", "kt", "sfac"))
        scr = kr[:].rearrange("p a b c q -> p (a b c q)")
        sa, sn = scr[:, 0:2048], scr[:, 2048:4096]
        r, k, v = (u[:, t:t + RW, :].rearrange("p a t -> p (a t)") for t in (R0, K0, V0))
        kkf, bbf = (t[:].rearrange("p a t -> p (a t)") for t in (kk, bb))
        chunks = lambda t: t.rearrange("p (a q) -> p a q", q=Q)
        bones = s.const("half_ones")
        lw, ls = sem("low_rank_loaded"), sem("vector_link_p")
        tw, dec, icl = sem("tanh_ready"), sem("decay_product"), sem("iclr_product")
        sg, ig = sem("decays_ready"), sem("iclr_ready")
        cs, ex, kraw, ksq = sem("sums_ready"), sem("exps_ready"), sem("kk_raw"), sem("kk_squared")
        nsum, nroot, nuse = sem("norm_sum"), sem("norm_root"), sem("kprime_inputs")
        bon, bsum, vtr, vcp, bvr = (sem(n) for n in ("bonus_terms", "bonus_sum", "v_turned",
                                                     "v_copied", "bonus_ready"))
        hat, tts, ttc, tmp = sem("hats_ready"), sem("hats_turned"), sem("hats_copied"), sem("scalar_link_p")
        slot = lambda psum, i: psum[:, i // 2, (i % 2) * T:(i % 2 + 1) * T]
        with nc.Block() as block:
            @block.sync
            def _(eng):
                eng.dma_start(w2[:], dram["w2"]).then_inc(lw, 16)
                eng.dma_start(a2[:], dram["a2"]).then_inc(lw, 16)

            @block.tensor
            def _(eng):
                eng.wait_ge(lw, 32)
                for j in range(RW):
                    ins = eng.matmul(slot(s.acc, j), a2[:, j * P:(j + 1) * P], u[:, PA0, :], start=True, stop=True)
                    ins.then_inc(icl, 1)
                eng.wait_ge(tw, 1)
                for j in range(RW):
                    ins = eng.matmul(slot(s.work, j), w2[:, j * P:(j + 1) * P], sn[:, 0:T], start=True, stop=True)
                    ins.then_inc(dec, 1)
                eng.wait_ge(ksq, 1)
                eng.wait_ge(sg, 1)
                for q in range(4):
                    ins = eng.matmul(s.work[:, q, :], bones, sa[:, 512 * q:512 * q + 512], start=True, stop=True)
                ins.then_inc(nsum, 1)
                eng.wait_ge(bon, 1)
                eng.wait_ge(ig, 1)
                for q in range(4):
                    ins = eng.matmul(s.acc[:, q, :], bones, sa[:, 512 * q:512 * q + 512], start=True, stop=True)
                ins.then_inc(bsum, 1)
                eng.wait_ge(nroot, 1)
                for c in range(NCH):
                    for j in range(RW):
                        ins = eng.transpose(s.work[:, 2 * c + j // 4, (j % 4) * P:(j % 4 + 1) * P],
                                            u[:, V0 + j, c * Q:(c + 1) * Q], s.const("ident"))
                ins.then_inc(vtr, 1)
                eng.wait_ge(hat, 1)
                eng.wait_ge(bvr, 1)
                for i, src in enumerate((bb, u[:, K0:K0 + RW, :])):
                    for j in range(RW):
                        ins = eng.transpose(s.acc[:, 2 * i + j // 4, (j % 4) * P:(j % 4 + 1) * P],
                                            src[:, j, 0:Q], s.const("ident"))
                ins.then_inc(tts, 1)

            @block.scalar
            def _(eng):
                eng.activation(sn[:, 0:T], u[:, PW0, :], ACT.Tanh).then_inc(tw, 1)
                for j in range(RW):
                    eng.wait_ge(icl, 2 * (j // 2) + 2)
                    ins = eng.activation(bb[:, j, :], slot(s.acc, j), ACT.Sigmoid, bias=s.par("a0", j))
                ins.then_inc(ig, 1)
                for j in range(RW):
                    eng.wait_ge(dec, 2 * (j // 2) + 2)
                    ins = eng.activation(kk[:, j, :], slot(s.work, j), ACT.Sigmoid, bias=s.par("w0", j))
                ins.then_inc(sg, 1)
                eng.activation(u[:, PG0:PG0 + 2, :], u[:, PG0:PG0 + 2, :], ACT.Sigmoid)
                eng.wait_ge(cs, 1)
                eng.activation(f2[:], f1[:], ACT.Exp, scale=E_HALF).then_inc(tmp, 1)
                eng.wait_ge(tmp, 1)
                eng.activation(f1[:], f1[:], ACT.Exp, scale=-E_HALF)
                eng.activation(sfac[:], karg[:], ACT.Exp, scale=-E_HALF).then_inc(ex, 1)
                eng.wait_ge(kraw, 1)
                eng.activation(sa, kkf, ACT.Square).then_inc(ksq, 1)
                eng.wait_ge(nsum, 1)
                eng.activation(sn, s.work[:].rearrange("p a b -> p (a b)"), ACT.Sqrt).then_inc(nroot, 1)
                eng.wait_ge(vtr, 1)
                eng.activation(vt[:].rearrange("p c a -> p (c a)"), s.work[:].rearrange("p a b -> p (a b)"),
                               ACT.Copy).then_inc(vcp, 1)
                eng.wait_ge(tts, 1)
                eng.activation(bt[:], s.acc[:, 0:2, :].rearrange("p a b -> p (a b)"), ACT.Copy)
                eng.activation(kt[:], s.acc[:, 2:4, :].rearrange("p a b -> p (a b)"), ACT.Copy)

            @block.vector
            def _(eng):
                link = Link(eng, ls)
                eng.memset(f1[:, :, 0:1], 0.0)
                eng.wait_ge(sg, 1)
                for i in range(2 * RW):
                    ins = eng.tensor_tensor_scan(f1[:, i, 1:Q + 1], s.const("ones"), kk[:, i // 2, (i % 2) * Q:(i % 2 + 1) * Q],
                                                 0.0, ALU.mult, ALU.add)
                link(ins)
                f4 = f1[:].rearrange("p (j c) q -> p j c q", c=2)
                eng.tensor_tensor(karg[:], f4[:, :, 0, Q], f4[:, :, 0, Q // 2], ALU.subtract)
                link(eng.tensor_copy(mid[:], f1[:, :, Q // 2]))
                eng.tensor_tensor(f1[:], f1[:], spread(mid[:], Q + 1), ALU.subtract)
                eng.tensor_tensor(karg[:], karg[:], mid[:].rearrange("p (j c) -> p j c", c=2)[:, :, 1],
                                  ALU.add).then_inc(cs, 1)
                for j in range(RW):
                    ins = eng.tensor_scalar(kk[:, j, :], u[:, K0 + j, :], s.par("k_k", j), None, ALU.mult)
                ins.then_inc(kraw, 1)
                eng.wait_ge(nroot, 1)
                link(eng.tensor_scalar(sn, sn, 1e-12, None, ALU.max))
                link(eng.reciprocal(sn, sn))
                link(eng.tensor_tensor(kkf, kkf, sn, ALU.mult))
                eng.wait_ge(ig, 1)
                for j in range(RW):
                    ins = eng.tensor_scalar(scr[:, j * T:(j + 1) * T], bb[:, j, :], -1.0, s.par("k_a", j),
                                            ALU.add, ALU.mult)
                link(ins)
                link(eng.scalar_tensor_tensor(out=k, in0=sa, scalar=1.0, in1=k, op0=ALU.add, op1=ALU.mult))
                eng.tensor_tensor(bbf, kkf, bbf, ALU.mult)
                for j in range(RW):
                    ins = eng.scalar_tensor_tensor(out=scr[:, j * T:(j + 1) * T], in0=u[:, R0 + j, :],
                                                   scalar=s.par("r_k", j), in1=u[:, K0 + j, :],
                                                   op0=ALU.mult, op1=ALU.mult)
                ins.then_inc(bon, 1)
                eng.wait_ge(bon, 1)
                eng.wait_ge(ex, 1)
                eng.tensor_tensor(chunks(bbf), chunks(bbf), f2[:, :, 1:Q + 1], ALU.mult)
                eng.tensor_tensor(chunks(k), chunks(k), f2[:, :, 1:Q + 1], ALU.mult).then_inc(hat, 1)
                eng.wait_ge(bsum, 1)
                eng.wait_ge(vtr, 1)
                eng.tensor_tensor(v, v, s.acc[:].rearrange("p a b -> p (a b)"), ALU.mult).then_inc(bvr, 1)


def rwkv_chunks(nc, s, u, b):
    with ExitStack() as st:
        sem = semaphores(nc, st)
        ab = alloc(nc, st, "ab", [P, 2, 4, 2, Q])
        cr = alloc(nc, st, "cr", [P, 2, 4, 2, Q])
        xm, zm, pm, lt = (alloc(nc, st, n, [P, 2, 4, Q]) for n in ("xm", "zm", "pm", "lt"))
        rh, us = (alloc(nc, st, n, [P, 2, 256]) for n in ("rh", "us"))
        sp = alloc(nc, st, "sp", [P, RW, 64])
        f1, kk, bb, kr, vt, bt, kt, sfac = (b[n] for n in ("f1", "kk", "bb", "kr", "vt", "bt", "kt", "sfac"))
        banks = (s.work, s.acc)
        (zr, krb, sc, mk, tr, xz, zz, ltr, pr, pc, qr, rr, rc, ur, uc, yr, yc, sr, sw, lk, plk) = (sem(n) for n in (
            "kr_zeroed", "kr_built", "scored", "masked", "a_turned", "x_ready", "z_started", "l_ready",
            "lx_ready", "lx_copied", "xlx_ready", "rhs_ready", "rhs_copied", "u_ready", "u_copied", "y_ready",
            "y_copied", "state_sum", "state_ready", "vector_link_c", "pool_link_c"))
        pairs = [(m, gi) for m in range(4) for gi in range(2)]
        tops = lambda name: over(s.const(name), 4)
        with nc.Block() as block:
            @block.gpsimd
            def _(eng):
                link = Link(eng, plk)
                eng.memset(kr[:], 0.0).then_inc(zr, 1)
                for m in range(4):
                    for gi in range(2):
                        it = 2 * m + gi
                        eng.wait_ge(mk, 2 * it + 1)
                        at_least(eng, ur, it - 1)
                        link(eng.tensor_tensor(zm[:, gi], ab[:, gi, :, 0, :], tops("lev0"), ALU.mult))
                        eng.tensor_tensor(zm[:, gi], tops("ident"), zm[:, gi], ALU.subtract).then_inc(zz, 1)
                    for q in range(1, LEVELS):
                        for gi in range(2):
                            at_least(eng, pr, (LEVELS - 1) * 2 * m + 2 * (q - 2) + gi + 1 if q > 1 else
                                     (LEVELS - 1) * 2 * (m - 1) + 2 * (LEVELS - 2) + gi + 1)
                            eng.tensor_tensor(lt[:, gi], ab[:, gi, :, 0, :], tops(f"lev{q}"),
                                              ALU.mult).then_inc(ltr, 1)

            @block.vector
            def _(eng):
                link = Link(eng, lk)
                f4 = f1[:].rearrange("p (j c) q -> p j c q", c=2)

                def build(c):
                    if c == 0:
                        eng.wait_ge(zr, 1)
                    else:
                        eng.wait_ge(sc, 4)
                    toks = slice(c * Q, (c + 1) * Q)
                    for h in range(2):
                        p = slice(64 * h, 64 * h + 64)
                        eng.tensor_tensor(kr[p, :, h, 0, :], kk[p, :, toks], f4[p, :, c, 0:Q], ALU.mult)
                        ins = eng.tensor_tensor(kr[p, :, h, 1, :], u[p, R0:R0 + RW, toks], f4[p, :, c, 1:Q + 1],
                                                ALU.mult)
                    ins.then_inc(krb, 1)

                for m in range(4):
                    if m % 2 == 0:
                        build(m // 2)
                    for gi in range(2):
                        it = 2 * m + gi
                        bk = banks[gi]
                        eng.wait_ge(sc, it + 1)
                        at_least(eng, yr, it - 1)
                        mask = over(s.consts[:, CONST_COLS["upper"]:CONST_COLS["upper"] + 2 * Q], 4)
                        for n, dst in ((0, ab), (2, cr)):
                            eng.tensor_tensor(dst[:, gi].rearrange("p h a q -> p h (a q)"),
                                              bk[:, n:n + 2, :].rearrange("p a (h q) -> p (a h) q", h=2),
                                              mask, ALU.mult).then_inc(mk, 1)
                        eng.wait_ge(tr, it + 1)
                        at_least(eng, qr, (LEVELS - 1) * 2 * m)
                        link(eng.scalar_tensor_tensor(out=xm[:, gi], in0=bk[:, 0, :].rearrange("p (h q) -> p h q", h=4),
                                                      scalar=-1.0, in1=tops("top_left"),
                                                      op0=ALU.mult, op1=ALU.mult))
                        eng.tensor_tensor(xm[:, gi], xm[:, gi], tops("ident"), ALU.add).then_inc(xz, 1)
                    for q in range(1, LEVELS):
                        for gi in range(2):
                            bk = banks[gi]
                            eng.wait_ge(qr, (LEVELS - 1) * 2 * m + 2 * (q - 1) + gi + 1)
                            eng.wait_ge(xz, LEVELS * 2 * m + 2 * (q - 1) + gi + 1)
                            if q == 1:
                                eng.wait_ge(zz, 2 * m + gi + 1)
                            if q < LEVELS - 1:
                                eng.tensor_tensor(xm[:, gi], xm[:, gi], bk[:, 2, :].rearrange("p (h q) -> p h q", h=4),
                                                  ALU.subtract)
                            eng.tensor_tensor(zm[:, gi], zm[:, gi], bk[:, 3, :].rearrange("p (h q) -> p h q", h=4),
                                              ALU.subtract).then_inc(xz, 1)
                    if m < 2:
                        for gi in range(2):
                            it = 2 * m + gi
                            eng.wait_ge(sr, it + 1)
                            for t in range(2):
                                j = 2 * (it % 4) + t
                                ins = eng.tensor_scalar(sp[:, j, :], banks[gi][:, 2, 64 * t:64 * t + 64],
                                                        sfac[:, j:j + 1], None, ALU.mult)
                            ins.then_inc(sw, 1)

            @block.scalar
            def _(eng):
                for m in range(4):
                    for q in range(1, LEVELS):
                        for gi in range(2):
                            n = (LEVELS - 1) * 2 * m + 2 * (q - 1) + gi
                            eng.wait_ge(pr, n + 1)
                            at_least(eng, qr, n - 1)
                            eng.activation(pm[:, gi], banks[gi][:, 1, :].rearrange("p (h q) -> p h q", h=4),
                                           ACT.Copy).then_inc(pc, 1)
                        if q == 1:
                            for gi in range(2):
                                it = 2 * m + gi
                                eng.wait_ge(rr, it + 1)
                                at_least(eng, ur, it - 1)
                                eng.activation(rh[:, gi], banks[gi][:, 0, 0:256], ACT.Copy,
                                               scale=-1.0).then_inc(rc, 1)
                    for gi in range(2):
                        it = 2 * m + gi
                        eng.wait_ge(ur, it + 1)
                        at_least(eng, yr, it - 1)
                        eng.activation(us[:, gi], banks[gi][:, 0, 256:512], ACT.Copy).then_inc(uc, 1)
                    for gi in range(2):
                        it = 2 * m + gi
                        c, g = it // 4, it % 4
                        eng.wait_ge(yr, it + 1)
                        if c == 0:
                            eng.wait_ge(krb, 1)
                        else:
                            eng.wait_ge(krb, 2)
                        eng.activation(u[:, R0 + 2 * g:R0 + 2 * g + 2, c * Q:(c + 1) * Q],
                                       banks[gi][:, 1, 0:256].rearrange("p (a q) -> p a q", a=2),
                                       ACT.Copy).then_inc(yc, 1)

            @block.tensor
            def _(eng):
                for m in range(4):
                    c = m // 2
                    eng.wait_ge(krb, c + 1)
                    heads = lambda gi: [(2 * (2 * m % 4 + gi) + h // 2, h % 2, h) for h in range(4)]
                    for gi in range(2):
                        it = 2 * m + gi
                        bk = banks[gi]
                        at_least(eng, yc, it - 1)
                        at_least(eng, sw, min(it - 1, 4))
                        for t in range(2):
                            j = 2 * (it % 4) + t
                            rhs = kr[:, j].rearrange("p h a q -> p (h a q)")
                            toks = slice(c * Q, (c + 1) * Q)
                            eng.matmul(bk[:, t, :], bb[:, j, toks], rhs, start=True, stop=True)
                            ins = eng.matmul(bk[:, 2 + t, :], u[:, K0 + j, toks], rhs, start=True, stop=True)
                        ins.then_inc(sc, 1)
                    for gi in range(2):
                        it = 2 * m + gi
                        eng.wait_ge(mk, 2 * it + 1)
                        for h in range(4):
                            ins = eng.transpose(banks[gi][:, 0, h * Q:(h + 1) * Q], ab[:, gi, h, 0, :], s.const("ident"))
                        ins.then_inc(tr, 1)
                    for q in range(1, LEVELS):
                        for gi in range(2):
                            it, n = 2 * m + gi, (LEVELS - 1) * 2 * m + 2 * (q - 1) + gi
                            bk = banks[gi]
                            eng.wait_ge(ltr, n + 1)
                            eng.wait_ge(xz, LEVELS * 2 * m + 2 * (q - 1) + gi + 1)
                            if q == 1:
                                eng.wait_ge(mk, 2 * it + 2)
                            for h in range(4):
                                ins = eng.matmul(bk[:, 1, h * Q:(h + 1) * Q], lt[:, gi, h, :], xm[:, gi, h, :],
                                                 start=True, stop=True)
                            ins.then_inc(pr, 1)
                        if q == 1:
                            for gi in range(2):
                                it = 2 * m + gi
                                for j, hh, h in heads(gi):
                                    out = banks[gi][:, 0, 64 * h:64 * h + 64]
                                    if c == 1:
                                        if h == 0:
                                            eng.wait_ge(sw, it - 3)
                                        eng.matmul(out, kr[:, j, hh, 0, :], sp[:, j, :], start=True, stop=False)
                                    hd = 2 * j + hh
                                    ins = eng.matmul(out, cr[:, gi, h, 0, :], vt[:, c, 64 * hd:64 * hd + 64],
                                                     start=c == 0, stop=True)
                                ins.then_inc(rr, 1)
                        for gi in range(2):
                            n = (LEVELS - 1) * 2 * m + 2 * (q - 1) + gi
                            bk = banks[gi]
                            eng.wait_ge(pc, n + 1)
                            if q == 1:
                                eng.wait_ge(zz, 2 * m + gi + 1)
                            for h in range(4):
                                if q < LEVELS - 1:
                                    eng.matmul(bk[:, 2, h * Q:(h + 1) * Q], zm[:, gi, h, :], pm[:, gi, h, :],
                                               start=True, stop=True)
                                ins = eng.matmul(bk[:, 3, h * Q:(h + 1) * Q], pm[:, gi, h, :], zm[:, gi, h, :],
                                                 start=True, stop=True)
                            ins.then_inc(qr, 1)
                    for gi in range(2):
                        it = 2 * m + gi
                        eng.wait_ge(rc, it + 1)
                        eng.wait_ge(xz, LEVELS * 2 * m + 2 * (LEVELS - 1) + gi + 1)
                        for h in range(4):
                            ins = eng.matmul(banks[gi][:, 0, 256 + 64 * h:320 + 64 * h], zm[:, gi, h, :],
                                             rh[:, gi, 64 * h:64 * h + 64], start=True, stop=True)
                        ins.then_inc(ur, 1)
                    for gi in range(2):
                        it = 2 * m + gi
                        eng.wait_ge(uc, it + 1)
                        for j, hh, h in heads(gi):
                            hd = 2 * j + hh
                            out = banks[gi][64 * hh:64 * hh + 64, 1, (h // 2) * Q:(h // 2 + 1) * Q]
                            if c == 1:
                                eng.matmul(out, sp[:, j, :], kr[:, j, hh, 1, :], start=True, stop=False)
                            eng.matmul(out, us[:, gi, 64 * h:64 * h + 64], ab[:, gi, h, 1, :], start=c == 0, stop=False)
                            ins = eng.matmul(out, vt[:, c, 64 * hd:64 * hd + 64], cr[:, gi, h, 1, :],
                                             start=False, stop=True)
                        ins.then_inc(yr, 1)
                        if c == 0:
                            for j, hh, h in heads(gi):
                                hd = 2 * j + hh
                                out = banks[gi][64 * hh:64 * hh + 64, 2, 64 * (h // 2):64 * (h // 2) + 64]
                                cols = slice(64 * hd, 64 * hd + 64)
                                eng.matmul(out, bt[:, cols], us[:, gi, 64 * h:64 * h + 64], start=True, stop=False)
                                ins = eng.matmul(out, kt[:, cols], vt[:, 0, cols], start=False, stop=True)
                            ins.then_inc(sr, 1)


def rwkv_output(nc, dram, s, u, b):
    with ExitStack() as st:
        sem = semaphores(nc, st)
        g2 = alloc(nc, st, "g2", [P, 2, 1024])
        yv = alloc(nc, st, "yv", [P, RW, T])
        kk, bb = b["kk"], b["bb"]
        flat = lambda t: t.rearrange("p a t -> p (a t)")
        y, bonus = u[:, R0:R0 + RW, :], u[:, V0:V0 + RW, :]
        bones = s.const("half_ones")
        ld, ms, md, sq, vs, ro, gs, fin, hi, lk = (sem(n) for n in (
            "gate_weight_loaded", "mean_sums", "centred", "centred_squared", "variance_sums",
            "deviation_ready", "gate_product", "mixed", "mixed_high", "vector_link_o"))
        slot = lambda i: s.work[:, i // 2, (i % 2) * T:(i % 2 + 1) * T]
        with nc.Block() as block:
            @block.sync
            def _(eng):
                eng.dma_start(g2[:], dram["g2"]).then_inc(ld, 16)

            @block.tensor
            def _(eng):
                for q in range(4):
                    eng.matmul(s.work[:, q, :], bones, flat(y)[:, 512 * q:512 * q + 512],
                               start=True, stop=True).then_inc(ms, 1)
                for q in range(4):
                    eng.wait_ge(sq, q + 1)
                    eng.matmul(s.acc[:, q, :], bones, flat(kk[:])[:, 512 * q:512 * q + 512],
                               start=True, stop=True).then_inc(vs, 1)
                eng.wait_ge(ld, 16)
                for j in range(RW):
                    for q in range(2):
                        ins = eng.matmul(slot(j), g2[:, q, j * P:(j + 1) * P], u[:, PG0 + q, :],
                                         start=q == 0, stop=q == 1)
                ins.then_inc(gs, 1)

            @block.scalar
            def _(eng):
                for q in range(4):
                    cols = slice(512 * q, 512 * q + 512)
                    eng.wait_ge(md, q + 1)
                    eng.activation(flat(kk[:])[:, cols], flat(yv[:])[:, cols], ACT.Square).then_inc(sq, 1)
                for q in range(4):
                    cols = slice(512 * q, 512 * q + 512)
                    eng.wait_ge(vs, q + 1)
                    eng.activation(flat(bb[:])[:, cols], s.acc[:, q, :], ACT.Sqrt, scale=1.0 / 64,
                                   bias=s.eps[:, 1:2]).then_inc(ro, 1)
                for h in range(2):
                    eng.wait_ge(fin, h + 1)
                    eng.activation(s.a0[:, RW + 4 * h:RW + 4 * h + 4, 0, :], yv[:, 4 * h:4 * h + 4, :],
                                   ACT.Copy).then_inc(hi, 1)

            @block.vector
            def _(eng):
                link = Link(eng, lk)
                for q in range(4):
                    cols = slice(512 * q, 512 * q + 512)
                    eng.wait_ge(ms, q + 1)
                    eng.scalar_tensor_tensor(out=flat(yv[:])[:, cols], in0=s.work[:, q, :], scalar=-1.0 / 64,
                                             in1=flat(y)[:, cols], op0=ALU.mult, op1=ALU.add).then_inc(md, 1)
                for h in range(2):
                    cols = slice(1024 * h, 1024 * h + 1024)
                    eng.wait_ge(ro, 2 * h + 2)
                    link(eng.reciprocal(flat(bb[:])[:, cols], flat(bb[:])[:, cols]))
                    link(eng.tensor_tensor(flat(yv[:])[:, cols], flat(yv[:])[:, cols], flat(bb[:])[:, cols], ALU.mult))
                    for j in range(4 * h, 4 * h + 4):
                        ins = eng.tensor_scalar(yv[:, j, :], yv[:, j, :], s.par("ln_w", j), s.par("ln_b", j),
                                                ALU.mult, ALU.add)
                    link(ins)
                    link(eng.tensor_tensor(flat(yv[:])[:, cols], flat(yv[:])[:, cols], flat(bonus)[:, cols], ALU.add))
                    eng.wait_ge(gs, 1)
                    eng.tensor_tensor(flat(yv[:])[:, cols], flat(yv[:])[:, cols],
                                      s.work[:, 2 * h:2 * h + 2, :].rearrange("p a b -> p (a b)"),
                                      ALU.mult).then_inc(fin, 1)
                for h in range(2):
                    eng.wait_ge(hi, h + 1)
                    eng.tensor_tensor(s.a0[:, RW + 4 * h:RW + 4 * h + 4, 1, :], yv[:, 4 * h:4 * h + 4, :],
                                      s.a0[:, RW + 4 * h:RW + 4 * h + 4, 0, :].bitcast(F32), ALU.subtract)


def rwkv(nc, dram, s, u):
    with ExitStack() as st:
        b = {n: alloc(nc, st, n, shape) for n, shape in (
            ("f1", [P, 2 * RW, Q + 1]), ("kk", [P, RW, T]), ("bb", [P, RW, T]),
            ("kr", [P, RW, 2, 2, Q]), ("vt", [P, NCH, 1024]), ("bt", [P, 1024]), ("kt", [P, 1024]),
            ("sfac", [P, RW]))}
        rwkv_prepare(nc, dram, s, u, b)
        rwkv_chunks(nc, s, u, b)
        rwkv_output(nc, dram, s, u, b)


def ssd(nc, s, u):
    with ExitStack() as st:
        sem = semaphores(nc, st)
        dtt, da, ax, ex, rz, z2, pl = (alloc(nc, st, n, [P, NCH, NH]) for n in (
            "dtt", "da", "ax", "ex", "rz", "z2", "pl"))
        ea = alloc(nc, st, "ea", [P, NH])
        dec = alloc(nc, st, "dec", [P, NH])
        xdt = alloc(nc, st, "xdt", [P, NCH, 1024])
        xdd = alloc(nc, st, "xdd", [P, 1024])
        btok = alloc(nc, st, "btok", [P, 2, P])
        stt = alloc(nc, st, "stt", [P, 1024])
        cbm = alloc(nc, st, "cbm", [P, 2, NCH, P])
        dm, el, ec, mm, cx = (alloc(nc, st, n, [P, 2, 4, P]) for n in ("dm", "el", "ec", "mm", "cx"))
        ys = alloc(nc, st, "ys", [P, RW, T])
        sqy = alloc(nc, st, "sqy", [P, RW, T])
        inv = alloc(nc, st, "inv", [P, 2, T])
        banks = (s.work, s.acc)
        (dtr, lk, axr, exr, ear, dar, decs, decr, xtr, xdr, bcr, bck, str_, stc, dmr, sgr, ecr, elr, mmr, cxr,
         yr, yd, sqr, smr, inr, outr, hir, pk) = (sem(n) for n in (
            "dt_turned", "vector_link_s", "dt_abs", "dt_exp", "a_exp", "da_ready", "end_sums", "end_decays",
            "x_turned", "xdt_ready", "bc_products", "b_copied", "states_summed", "states_copied",
            "da_masked", "segments_ready", "starts_exp", "segments_exp", "m_ready", "c_scaled",
            "y_summed", "y_read", "y_squared", "y_norm_sums", "y_norm_root", "ssd_mixed", "ssd_high",
            "pool_link_s"))
        flat = lambda t: t.rearrange("p a t -> p (a t)")
        def ssd_y(eng, it):
            c, q, gi = it // 4, it % 4, it % 2
            bk = banks[gi]
            eng.wait_ge(mmr, it + 1)
            at_least(eng, yd, it - 1)
            if c == 1:
                eng.wait_ge(cxr, it - 3)
            for h in range(4):
                hd = 4 * q + h
                out = bk[64 * (h % 2):64 * (h % 2) + 64, 2, (h // 2) * P:(h // 2 + 1) * P]
                ins = eng.matmul(out, xdt[:, c, 64 * hd:64 * hd + 64], mm[:, gi, h, :], start=True, stop=c == 0)
                if c == 1:
                    ins = eng.matmul(out, stt[:, 64 * hd:64 * hd + 64], cx[:, gi, h, :], start=False, stop=True)
            ins.then_inc(yr, 1)

        def ssd_y_last(eng):
            ssd_y(eng, 7)
            for g in range(2):
                eng.wait_ge(sqr, g + 1)
                if g == 0:
                    eng.wait_ge(yd, 8)
                for j in range(4):
                    ins = eng.matmul(s.work[:, 3 * g, 0:T], s.const("ones"), sqy[:, 4 * g + j, :],
                                     start=j == 0, stop=j == 3)
                ins.then_inc(smr, 1)

        with nc.Block() as block:
            @block.tensor
            def _(eng):
                ident = s.const("ident")
                for c in range(NCH):
                    ins = eng.transpose(s.work[:, 0, c * P:(c + 1) * P], u[:, PW0, c * Q:(c + 1) * Q], ident)
                ins.then_inc(dtr, 1)
                for g in range(2):
                    for c in range(NCH):
                        toks = slice(c * Q, (c + 1) * Q)
                        eng.matmul(s.work[:, 1, (2 * g + c) * P:(2 * g + c + 1) * P], u[:, B0 + g, toks],
                                   u[:, C0 + g, toks], start=True, stop=True)
                for g in range(2):
                    ins = eng.transpose(s.work[:, 2, g * P:(g + 1) * P], u[:, B0 + g, 0:Q], ident)
                ins.then_inc(bcr, 1)
                for c in range(NCH):
                    for j in range(RW):
                        ins = eng.transpose(s.acc[:, 2 * c + j // 4, (j % 4) * P:(j % 4 + 1) * P],
                                            u[:, XS0 + j, c * Q:(c + 1) * Q], ident)
                ins.then_inc(xtr, 1)
                eng.wait_ge(dar, 1)
                eng.matmul(s.work[:, 3, 0:NH], s.const("lower"), da[:, 0, :], start=True, stop=True).then_inc(decs, 1)
                eng.wait_ge(xdr, 2)
                eng.wait_ge(bck, 1)
                for g in range(2):
                    ins = eng.matmul(s.acc[:, g, :], btok[:, g, :], xdd[:, 512 * g:512 * g + 512], start=True, stop=True)
                ins.then_inc(str_, 1)
                for it in range(8):
                    c, q, gi = it // 4, it % 4, it % 2
                    bk = banks[gi]
                    if it == 0:
                        eng.wait_ge(bck, 2)
                        eng.wait_ge(decr, 1)
                    if it == 1:
                        eng.wait_ge(stc, 1)
                    eng.wait_ge(dmr, it + 1)
                    at_least(eng, elr, it - 1)
                    rhs = dm[:, gi].rearrange("p h q -> p (h q)")
                    if c == 1:
                        at_least(eng, ecr, it - 5)
                        eng.matmul(bk[:, 1, :], s.const("ones"), rhs, start=True, stop=True)
                    eng.matmul(bk[:, 0, :], s.const("lower"), rhs, start=True, stop=True).then_inc(sgr, 1)
                    if it >= 1:
                        ssd_y(eng, it - 1)
                ssd_y_last(eng)

            @block.scalar
            def _(eng):
                eng.activation(ea[:], s.par("a_log"), ACT.Exp).then_inc(ear, 1)
                eng.wait_ge(axr, 1)
                eng.activation(ex[:], ax[:], ACT.Exp, scale=-1.0).then_inc(exr, 1)
                eng.wait_ge(bcr, 1)
                eng.activation(flat(btok[:]), s.work[:, 2, 0:2 * P], ACT.Copy).then_inc(bck, 1)
                eng.wait_ge(decs, 1)
                eng.activation(dec[:], s.work[:, 3, 0:NH], ACT.Exp).then_inc(decr, 1)
                eng.wait_ge(str_, 1)
                eng.activation(stt[:], s.acc[:, 0:2, :].rearrange("p a b -> p (a b)"), ACT.Copy).then_inc(stc, 1)
                for it in range(8):
                    gi = it % 2
                    bk = banks[gi]
                    eng.wait_ge(sgr, it + 1)
                    at_least(eng, mmr, it - 1)
                    if it >= 4:
                        at_least(eng, cxr, it - 5)
                        eng.activation(ec[:, gi].rearrange("p h q -> p (h q)"), bk[:, 1, :], ACT.Exp).then_inc(ecr, 1)
                    eng.activation(el[:, gi].rearrange("p h q -> p (h q)"), bk[:, 0, :], ACT.Exp).then_inc(elr, 1)
                for g in range(2):
                    eng.wait_ge(outr, g + 1)
                    eng.activation(sqy[:, 4 * g:4 * g + 4, :], ys[:, 4 * g:4 * g + 4, :], ACT.Square).then_inc(sqr, 1)
                for g in range(2):
                    eng.wait_ge(smr, g + 1)
                    eng.activation(inv[:, g, :], s.work[:, 3 * g, 0:T], ACT.Sqrt, scale=1.0 / 512,
                                   bias=s.eps[:, 0:1]).then_inc(inr, 1)
                for g in range(2):
                    eng.wait_ge(outr, 3 + g)
                    eng.activation(s.a0[:, 4 * g:4 * g + 4, 0, :], ys[:, 4 * g:4 * g + 4, :], ACT.Copy).then_inc(hir, 1)

            @block.gpsimd
            def _(eng):
                for it in range(4, 8):
                    q, gi = it % 4, it % 2
                    eng.wait_ge(ecr, it - 3)
                    at_least(eng, yr, it - 1)
                    eng.tensor_tensor(cx[:, gi], ec[:, gi], over(u[:, C0 + q // 2, Q:2 * Q], 4),
                                      ALU.mult).then_inc(cxr, 1)

            @block.vector
            def _(eng):
                link = Link(eng, lk)
                eng.wait_ge(dtr, 1)
                raw = s.work[:, 0, 0:2 * P].rearrange("p (c n) -> p c n", c=NCH)[:, :, DT_ROW:DT_ROW + NH]
                link(eng.tensor_tensor(dtt[:], raw, over(s.par("dt_bias"), NCH), ALU.add))
                link(eng.scalar_tensor_tensor(out=ax[:], in0=dtt[:], scalar=-1.0, in1=dtt[:], op0=ALU.mult, op1=ALU.max))
                eng.tensor_scalar(dtt[:], dtt[:], 0.0, None, ALU.max).then_inc(axr, 1)
                eng.wait_ge(exr, 1)
                link(eng.tensor_scalar(rz[:], ex[:], 2.0, None, ALU.add))
                link(eng.reciprocal(rz[:], rz[:]))
                link(eng.tensor_tensor(rz[:], rz[:], ex[:], ALU.mult))
                link(eng.tensor_tensor(z2[:], rz[:], rz[:], ALU.mult))
                link(eng.tensor_scalar(pl[:], z2[:], 1.0 / 17, None, ALU.mult))
                for q in range(7, 0, -1):
                    link(eng.scalar_tensor_tensor(out=pl[:], in0=pl[:], scalar=1.0 / (2 * q + 1), in1=z2[:],
                                                  op0=ALU.add, op1=ALU.mult))
                link(eng.scalar_tensor_tensor(out=pl[:], in0=pl[:], scalar=1.0, in1=rz[:], op0=ALU.add, op1=ALU.mult))
                link(eng.scalar_tensor_tensor(out=dtt[:], in0=pl[:], scalar=2.0, in1=dtt[:], op0=ALU.mult, op1=ALU.add))
                eng.wait_ge(ear, 1)
                eng.scalar_tensor_tensor(out=da[:], in0=dtt[:], scalar=-1.0, in1=over(ea[:], NCH),
                                         op0=ALU.mult, op1=ALU.mult).then_inc(dar, 1)
                eng.wait_ge(xtr, 1)
                for c in range(NCH):
                    ins = eng.tensor_tensor(xdt[:, c, :].rearrange("p (h n) -> p h n", n=64),
                                            s.acc[:, 2 * c:2 * c + 2, :].rearrange("p a (h n) -> p (a h) n", n=64),
                                            spread(dtt[:, c, :], 64), ALU.mult)
                ins.then_inc(xdr, 1)
                eng.wait_ge(xdr, 1)
                eng.wait_ge(decr, 1)
                eng.tensor_tensor(xdd[:].rearrange("p (h n) -> p h n", n=64),
                                  xdt[:, 0, :].rearrange("p (h n) -> p h n", n=64), spread(dec[:], 64),
                                  ALU.mult).then_inc(xdr, 1)
                eng.wait_ge(bck, 1)
                eng.tensor_tensor(cbm[:].rearrange("p g c q -> p (g c) q"),
                                  s.work[:, 1, :].rearrange("p (g q) -> p g q", q=P), over(s.const("upper_in"), 4),
                                  ALU.mult).then_inc(bck, 1)

                def mask(it):
                    c, q, gi = it // 4, it % 4, it % 2
                    at_least(eng, sgr, it - 1)
                    eng.tensor_tensor(dm[:, gi], over(s.const("upper_in"), 4), spread(da[:, c, 4 * q:4 * q + 4], P),
                                      ALU.mult).then_inc(dmr, 1)

                eng.wait_ge(dar, 1)
                eng.wait_ge(bck, 2)
                mask(0)
                mask(1)
                for it in range(8):
                    c, q, gi = it // 4, it % 4, it % 2
                    eng.wait_ge(elr, it + 1)
                    at_least(eng, yr, it - 1)
                    eng.tensor_tensor(mm[:, gi], el[:, gi], over(cbm[:, q // 2, c, :], 4), ALU.mult).then_inc(mmr, 1)
                    if it + 2 < 8:
                        mask(it + 2)
                    eng.wait_ge(yr, it + 1)
                    for t in range(2):
                        j, toks = 2 * q + t, slice(c * Q, (c + 1) * Q)
                        ins = eng.scalar_tensor_tensor(out=ys[:, j, toks], in0=u[:, XS0 + j, toks],
                                                       scalar=s.par("ssd_d", j), in1=banks[gi][:, 2, t * P:(t + 1) * P],
                                                       op0=ALU.mult, op1=ALU.add)
                    ins.then_inc(yd, 1)
                eng.wait_ge(yd, 8)
                for g in range(2):
                    h = slice(4 * g, 4 * g + 4)
                    eng.tensor_tensor(ys[:, h, :], ys[:, h, :], u[:, Z0 + 4 * g:Z0 + 4 * g + 4, :],
                                      ALU.mult).then_inc(outr, 1)
                for g in range(2):
                    h = slice(4 * g, 4 * g + 4)
                    eng.wait_ge(inr, g + 1)
                    eng.wait_ge(sqr, g + 1)
                    link(eng.reciprocal(inv[:, g, :], inv[:, g, :]))
                    for j in range(4 * g, 4 * g + 4):
                        ins = eng.scalar_tensor_tensor(out=ys[:, j, :], in0=ys[:, j, :], scalar=s.par("ssd_g", j),
                                                       in1=inv[:, g, :], op0=ALU.mult, op1=ALU.mult)
                    ins.then_inc(outr, 1)
                for g in range(2):
                    h = slice(4 * g, 4 * g + 4)
                    eng.wait_ge(hir, g + 1)
                    eng.wait_ge(outr, 3 + g)
                    eng.tensor_tensor(s.a0[:, h, 1, :], ys[:, h, :], s.a0[:, h, 0, :].bitcast(F32), ALU.subtract)


def memory_parts(nc, dram, s, vx, kx, sem):
    mem = vx[:].rearrange("p a n -> p (a n)")
    sqs = kx[:].rearrange("p a t -> p (a t)")
    ld, sqd, sm, rt, rs, nm, hi = (sem(n) for n in (
        "memory_loaded", "memory_squared", "memory_sum", "memory_root", "memory_rstd", "memory_normed",
        "memory_high"))
    with nc.Block() as block:
        @block.sync
        def _(eng):
            eng.dma_start(mem, dram["mem"]).then_inc(ld, 16)

        @block.scalar
        def _(eng):
            eng.wait_ge(ld, 16)
            for q in range(4):
                eng.activation(sqs[:, 1024 * q:1024 * q + 1024], mem[:, 1024 * q:1024 * q + 1024],
                               ACT.Square).then_inc(sqd, 1)
            eng.wait_ge(sm, 1)
            eng.activation(s.root[:], s.work[:, 0, 0:T], ACT.Sqrt, scale=1.0 / D, bias=s.eps[:, 0:1]).then_inc(rt, 1)
            for q in range(4):
                eng.wait_ge(nm, q + 1)
                eng.activation(s.a0[:, 4 * q:4 * q + 4, 0, :], mem[:, 1024 * q:1024 * q + 1024].rearrange(
                    "p (a t) -> p a t", t=T), ACT.Copy).then_inc(hi, 1)

        @block.tensor
        def _(eng):
            for kt in range(KT):
                if kt % 4 == 0:
                    eng.wait_ge(sqd, kt // 4 + 1)
                ins = eng.matmul(s.work[:, 0, 0:T], s.const("ones"), sqs[:, kt * T:(kt + 1) * T],
                                 start=kt == 0, stop=kt == KT - 1)
            ins.then_inc(sm, 1)

        @block.vector
        def _(eng):
            eng.wait_ge(rt, 1)
            eng.reciprocal(s.rstd[:], s.root[:]).then_inc(rs, 1)
            eng.wait_ge(rs, 1)
            for q in range(4):
                for kt in range(4 * q, 4 * q + 4):
                    cols = slice(kt * T, (kt + 1) * T)
                    ins = eng.scalar_tensor_tensor(out=mem[:, cols], in0=mem[:, cols], scalar=s.par("norm_mem_g", kt),
                                                   in1=s.rstd[:], op0=ALU.mult, op1=ALU.mult)
                ins.then_inc(nm, 1)
            for q in range(4):
                eng.wait_ge(hi, q + 1)
                eng.tensor_tensor(s.a0[:, 4 * q:4 * q + 4, 1, :], mem[:, 1024 * q:1024 * q + 1024].rearrange(
                    "p (a t) -> p a t", t=T), s.a0[:, 4 * q:4 * q + 4, 0, :].bitcast(F32), ALU.subtract)


def cross_attention(nc, s, qx, kx, vx, pe_, pt, stats, a1, sem):
    scale = XD ** -0.5
    mx, sm = stats[:, 0:8], stats[:, 8:16]
    (scd, mxd, exd, nrd, trd, cpd, pvd, hid, lod, lk) = (sem(n) for n in (
        "scores", "maxima", "exps", "probs_normed", "probs_turned", "probs_copied", "outputs",
        "outputs_high", "outputs_low", "vector_link_x"))
    bank = lambda i: (s.work if i < 4 else s.acc)[:, i % 4, :]
    with nc.Block() as block:
        @block.tensor
        def _(eng):
            for i in range(8):
                h, t = i // 2, i % 2
                for d in range(4):
                    ins = eng.matmul(bank(i)[:, 0:T], qx[:, 4 * h + d, t * P:(t + 1) * P], kx[:, 4 * h + d, :],
                                     start=d == 0, stop=d == 3)
                ins.then_inc(scd, 1)
            for h in range(XH):
                eng.wait_ge(nrd, 2 * h + 2)
                for t in range(2):
                    for m in range(2):
                        ins = eng.transpose(bank(h)[:, (2 * m + t) * P:(2 * m + t + 1) * P],
                                            pe_[:, 2 * h + t, m * P:(m + 1) * P], s.const("ident"))
                ins.then_inc(trd, 1)
            for h in range(XH):
                eng.wait_ge(cpd, h + 1)
                for d in range(4):
                    b = bank(4 + (2 * h + d // 2) % 4)
                    if d % 2 == 0:
                        eng.wait_ge(exd, 8)
                        at_least(eng, lod, 2 * h + d // 2 - 3)
                    for m in range(2):
                        ins = eng.matmul(b[:, (d % 2) * T:(d % 2 + 1) * T],
                                         vx[:, m, XD * h + d * P:XD * h + (d + 1) * P], pt[:, h, m, :],
                                         start=m == 0, stop=m == 1)
                    if d % 2 == 1:
                        ins.then_inc(pvd, 1)

        @block.scalar
        def _(eng):
            for i in range(8):
                eng.wait_ge(mxd, i + 1)
                eng.activation(pe_[:, i, :], bank(i)[:, 0:T], ACT.Exp, bias=mx[:, i:i + 1], scale=scale,
                               accum_out=sm[:, i:i + 1]).then_inc(exd, 1)
            for h in range(XH):
                eng.wait_ge(trd, h + 1)
                eng.activation(pt[:, h].rearrange("p m q -> p (m q)"), bank(h), ACT.Copy).then_inc(cpd, 1)
            for n in range(8):
                eng.wait_ge(pvd, n + 1)
                eng.activation(a1[:, 2 * n:2 * n + 2, 0, :], bank(4 + n % 4).rearrange("p (a t) -> p a t", a=2),
                               ACT.Copy).then_inc(hid, 1)

        @block.vector
        def _(eng):
            link = Link(eng, lk)
            for i in range(8):
                eng.wait_ge(scd, i + 1)
                link(eng.tensor_reduce(mx[:, i:i + 1], bank(i)[:, 0:T], AX.X, ALU.max))
                eng.tensor_scalar(mx[:, i:i + 1], mx[:, i:i + 1], -scale, None, ALU.mult).then_inc(mxd, 1)
            for i in range(8):
                eng.wait_ge(exd, i + 1)
                link(eng.reciprocal(sm[:, i:i + 1], sm[:, i:i + 1]))
                eng.tensor_scalar(pe_[:, i, :], pe_[:, i, :], sm[:, i:i + 1], None, ALU.mult).then_inc(nrd, 1)
            for n in range(8):
                eng.wait_ge(hid, n + 1)
                eng.tensor_tensor(a1[:, 2 * n:2 * n + 2, 1, :], bank(4 + n % 4).rearrange("p (a t) -> p a t", a=2),
                                  a1[:, 2 * n:2 * n + 2, 0, :].bitcast(F32), ALU.subtract).then_inc(lod, 1)


def stream_block(nc, s, phs, first=None, skip=0):
    with nc.Block() as block:
        @block.sync
        def _(eng):
            for ph in phs:
                s.sp(eng, ph)

        @block.scalar
        def _(eng):
            s.act(eng, phs)

        @block.vector
        def _(eng):
            s.dve(eng, phs)

        @block.gpsimd
        def _(eng):
            s.pool(eng, phs)

        @block.tensor
        def _(eng):
            s.pe(eng, phs)


def attention_and_mlp(nc, dram, s):
    with ExitStack() as st:
        a1 = alloc(nc, st, "a1", [P, KT, 2, T], F32R)
        with ExitStack() as qkv:
            qx, kx = (alloc(nc, qkv, n, [P, KT, T]) for n in ("qx", "kx"))
            vx = alloc(nc, qkv, "vx", [P, 2, D])
            with ExitStack() as rg:
                s.ring(rg, "_x")
                with nc.Block() as block:
                    @block.vector
                    def _(eng):
                        eng.memset(s.tb[:], 0.0)
                w_out = s.phase("w_out", "w_out", 8, 4, 2, s.a0, "resid", out=a1, g="norm_x_g")
                q = s.phase("wq", "wq", 8, 4, 2, a1, "scaled", out=qx, after=w_out, sum_after=True)
                stream_block(nc, s, [w_out, q])
                memory_parts(nc, dram, s, vx, kx, semaphores(nc, rg))
                k = s.phase("wk", "wk", 8, 4, 2, s.a0, "plain", out=kx)
                v = s.phase("wv", "wv", 8, 4, 2, s.a0, "tok", out=vx)
                stream_block(nc, s, [k, v])
            with ExitStack() as xs:
                pe_ = alloc(nc, xs, "probs", [P, 8, T])
                pt = alloc(nc, xs, "probs_t", [P, XH, 2, T])
                stats = alloc(nc, xs, "stats", [P, 16])
                cross_attention(nc, s, qx, kx, vx, pe_, pt, stats, a1, semaphores(nc, xs))
        with ExitStack() as rg:
            s.ring(rg, "_f")
            with nc.Block() as block:
                @block.vector
                def _(eng):
                    eng.memset(s.tb[:], 0.0)
            wo = s.phase("wo", "wo", 8, 4, 2, a1, "resid", out=s.a0, g="norm_ffn_g")
            phs = [wo]
            for q in range(4):
                up = s.phase("ffn1", "ffn1", 8, 4, 2, s.a0, "relu2", out=a1, w0=32 * q,
                             after=wo if q == 0 else None, sum_after=q == 0)
                down = s.phase("ffn2", "ffn2", 8, 4, 2, a1, "sumsq" if q == 3 else "acc", w0=32 * q, after=up)
                phs += [up, down]
            stream_block(nc, s, phs)


def final_norm(nc, s, g, out_dram=None):
    with ExitStack() as st, nc.Block() as block:
        sem = semaphores(nc, st)
        sm, rt, rs, nm = (sem(g + n) for n in ("_sum", "_root", "_rstd", "_normed"))

        @block.tensor
        def _(eng):
            for t in range(2):
                ins = eng.matmul(s.work[:, 3, 0:T], s.const("ones"), s.sq[:, t, :], start=t == 0, stop=t == 1)
            ins.then_inc(sm, 1)

        @block.scalar
        def _(eng):
            eng.wait_ge(sm, 1)
            eng.activation(s.root[:], s.work[:, 3, 0:T], ACT.Sqrt, scale=1.0 / D, bias=s.eps[:, 0:1]).then_inc(rt, 1)

        @block.vector
        def _(eng):
            eng.wait_ge(rt, 1)
            eng.reciprocal(s.rstd[:], s.root[:]).then_inc(rs, 1)
            eng.wait_ge(rs, 1)
            for kt in range(KT):
                eng.scalar_tensor_tensor(out=s.x[:, kt, :], in0=s.x[:, kt, :], scalar=s.par(g, kt), in1=s.rstd[:],
                                         op0=ALU.mult, op1=ALU.mult).then_inc(nm, 1)

        if out_dram is not None:
            @block.sync
            def _(eng):
                for q in range(4):
                    eng.wait_ge(nm, 4 * q + 4)
                    eng.dma_start(out_dram[:, 1024 * q:1024 * q + 1024],
                                  s.x[:, 4 * q:4 * q + 4, :].rearrange("p a t -> p (a t)")).then_inc(rs, 16)
                eng.wait_ge(rs, 65)


def window_attention(nc, s, ua):
    with ExitStack() as st:
        sem = semaphores(nc, st)
        kz = alloc(nc, st, "kz", [P, 2, 2, T])
        vtk = alloc(nc, st, "vtk", [P, 2, P])
        bias = alloc(nc, st, "alibi", [P, NH, T])
        sc = alloc(nc, st, "sc", [P, NH, T])
        pt = alloc(nc, st, "ptw", [P, NH, 2, P])
        mxs, nmx, sm, sk = (alloc(nc, st, n, [P, 2, NH]) for n in ("mxs", "nmx", "smw", "skw"))
        slp = alloc(nc, st, "slp", [P, NH])
        (kzr, vtr, vtc, alr, scr, scs, mxr, exr, skr, nrm, trr, ptr, pvr, hir, lor, lk, pk) = (sem(n) for n in (
            "keys_placed", "v2_turned", "v2_copied", "alibi_ready", "scores2", "scores2_biased", "maxima2",
            "exps2", "sink_exps", "probs2_normed", "probs2_turned", "probs2_copied", "outputs2",
            "outputs2_high", "outputs2_low", "vector_link_w", "pool_link_w"))
        banks = lambda i: (s.work if i < 4 else s.acc)[:, i % 4, :]
        nk = (P, 2 * P)
        with nc.Block() as block:
            @block.gpsimd
            def _(eng):
                eng.memset(kz[:], 0.0).then_inc(kzr, 1)
                eng.tensor_scalar(slp[:], s.par("slopes"), -1.0, None, ALU.mult).then_inc(pk, 1)
                eng.wait_ge(pk, 1)
                for h in range(NH):
                    ins = eng.tensor_scalar(bias[:, h, :], s.const("dist", 2 * P), slp[:, h:h + 1], None, ALU.mult)
                ins.then_inc(alr, 1)

            @block.tensor
            def _(eng):
                for m in range(2):
                    ins = eng.transpose(s.acc[:, 3, m * P:(m + 1) * P], ua[:, V2, m * P:(m + 1) * P], s.const("ident"))
                ins.then_inc(vtr, 1)
                eng.wait_ge(kzr, 2)
                eng.wait_ge(vtc, 1)
                for n in range(2):
                    for j in range(8):
                        i = 8 * n + j
                        at_least(eng, scs, i - 7)
                        if n == 1 and j == 0:
                            eng.wait_ge(lor, 2)
                        ins = eng.matmul(banks(j)[:, 0:2 * nk[n]], ua[:, Q2 + j, n * P:(n + 1) * P],
                                         kz[:, j // 4, :, 0:nk[n]], start=True, stop=True)
                        ins.then_inc(scr, 1)
                    turns = NH // 4 * (n + 1)
                    for b in range(turns):
                        if n == 0:
                            eng.wait_ge(nrm, 4 * b + 4)
                            four = [(4 * b + q, 0) for q in range(4)]
                        else:
                            eng.wait_ge(nrm, NH + 2 * b + 2)
                            four = [(2 * b + q // 2, q % 2) for q in range(4)]
                        eng.wait_ge(scs, 8 * n + 8)
                        for q, (h, m) in enumerate(four):
                            ins = eng.transpose(banks(b)[:, q * P:(q + 1) * P], sc[:, h, m * P:(m + 1) * P],
                                                s.const("ident"))
                        ins.then_inc(trr, 1)
                    for b in range(2):
                        eng.wait_ge(ptr, (4 if n == 0 else 12))
                        for j in range(4 * b, 4 * b + 4):
                            for hh in range(2):
                                h = 2 * j + hh
                                g = h // 8
                                out = banks(2 * n + b)[64 * hh:64 * hh + 64, (j % 4) * P:(j % 4 + 1) * P]
                                for m in range(n + 1):
                                    ins = eng.matmul(out, vtk[:, m, 64 * g:64 * g + 64], pt[:, h, m, :],
                                                     start=m == 0, stop=m == n)
                        ins.then_inc(pvr, 1)

            @block.scalar
            def _(eng):
                eng.wait_ge(vtr, 1)
                eng.activation(vtk[:].rearrange("p m d -> p (m d)"), s.acc[:, 3, 0:2 * P], ACT.Copy).then_inc(vtc, 1)
                for n in range(2):
                    eng.wait_ge(mxr, n + 1)
                    eng.activation(sk[:, n, :], sk[:, n, :], ACT.Exp).then_inc(skr, 1)
                    for h in range(NH):
                        eng.activation(sc[:, h, 0:nk[n]], sc[:, h, 0:nk[n]], ACT.Exp, bias=nmx[:, n, h:h + 1],
                                       accum_out=sm[:, n, h:h + 1]).then_inc(exr, 1)
                    for b in range(4 * (n + 1)):
                        eng.wait_ge(trr, 4 * n + b + 1)
                        src = banks(b)
                        if n == 0:
                            dst = pt[:, 4 * b:4 * b + 4, 0, :]
                            eng.activation(dst, src.rearrange("p (h q) -> p h q", h=4), ACT.Copy).then_inc(ptr, 1)
                        else:
                            if b == 0:
                                eng.wait_ge(pvr, 2)
                            eng.activation(pt[:, 2 * b:2 * b + 2].rearrange("p h m q -> p (h m q)"), src,
                                           ACT.Copy).then_inc(ptr, 1)
                    for b in range(2):
                        eng.wait_ge(pvr, 2 * n + b + 1)
                        eng.activation(s.a0[:, 4 + 4 * b:8 + 4 * b, 0, n * P:(n + 1) * P],
                                       banks(2 * n + b).rearrange("p (a q) -> p a q", a=4), ACT.Copy).then_inc(hir, 1)

            @block.vector
            def _(eng):
                link = Link(eng, lk)
                eng.wait_ge(kzr, 1)
                for g in range(2):
                    for hh in range(2):
                        ins = eng.tensor_copy(kz[64 * hh:64 * hh + 64, g, hh, :], ua[64 * g:64 * g + 64, K2, :])
                ins.then_inc(kzr, 1)
                eng.wait_ge(alr, 1)
                for n in range(2):
                    w = nk[n]
                    if n == 1:
                        eng.wait_ge(trr, 4)
                    for j in range(8):
                        eng.wait_ge(scr, 8 * n + j + 1)
                        eng.scalar_tensor_tensor(out=sc[:, 2 * j:2 * j + 2, 0:w],
                                                 in0=banks(j)[:, 0:2 * w].rearrange("p (h q) -> p h q", h=2),
                                                 scalar=64 ** -0.5, in1=bias[:, 2 * j:2 * j + 2, 2 * P - w:2 * P],
                                                 op0=ALU.mult, op1=ALU.add).then_inc(scs, 1)
                    eng.wait_ge(scs, 8 * n + 8)
                    link(eng.tensor_reduce(mxs[:, n, :], sc[:, :, 0:w], AX.X, ALU.max))
                    link(eng.tensor_tensor(mxs[:, n, :], mxs[:, n, :], s.par("sinks"), ALU.max))
                    eng.tensor_scalar(nmx[:, n, :], mxs[:, n, :], -1.0, None, ALU.mult)
                    eng.tensor_tensor(sk[:, n, :], s.par("sinks"), mxs[:, n, :], ALU.subtract).then_inc(mxr, 1)
                    eng.wait_ge(skr, n + 1)
                    eng.wait_ge(exr, NH * (n + 1))
                    link(eng.tensor_tensor(sm[:, n, :], sm[:, n, :], sk[:, n, :], ALU.add))
                    link(eng.reciprocal(sm[:, n, :], sm[:, n, :]))
                    for h in range(NH):
                        eng.tensor_scalar(sc[:, h, 0:w], sc[:, h, 0:w], sm[:, n, h:h + 1], None,
                                          ALU.mult).then_inc(nrm, 1)
                    for b in range(2):
                        eng.wait_ge(hir, 2 * n + b + 1)
                        out = s.a0[:, 4 + 4 * b:8 + 4 * b, :, n * P:(n + 1) * P]
                        eng.tensor_tensor(out[:, :, 1, :], banks(2 * n + b).rearrange("p (a q) -> p a q", a=4),
                                          out[:, :, 0, :].bitcast(F32), ALU.subtract).then_inc(lor, 1)


def s5(nc, dram, s, ua):
    HT = ST // 2
    c1, c2 = 6.28125, 0.0019340515136718750
    c3 = 2 * np.pi - c1 - c2
    magic = 1.5 * 2.0 ** 23
    with ExitStack() as st:
        sem = semaphores(nc, st)
        br, bi, cr, ci, bbr, bbi, tb2 = (alloc(nc, st, "s_" + n, [P, ST, 16]) for n in (
            "br", "bi", "cr", "ci", "bbr", "bbi", "tmp"))
        dt, ar, th, mag, kq, rr, co, si, abr, abi, den, zr, zi, t1 = (alloc(nc, st, "s_" + n, [P, ST]) for n in (
            "dt", "ar", "th", "mag", "kq", "rr", "cos", "sin", "abr", "abi", "den", "zr", "zi", "t1"))
        em = alloc(nc, st, "s_em", [P, 2, 2, HT])
        sqs = alloc(nc, st, "s_sqs", [P, 2, HT])
        bd, cd = (alloc(nc, st, n, [P, 2, ST, P]) for n in ("s_bd", "s_cd"))
        btn = alloc(nc, st, "s_bt", [P, 2, HT, P])
        er, ei, xr, xi = (alloc(nc, st, n, [P, HT, T]) for n in ("s_er", "s_ei", "s_xr", "s_xi"))
        q1, q2 = (alloc(nc, st, n, [P, 2, T]) for n in ("s_q1", "s_q2"))
        w1, w2 = (alloc(nc, st, n, [P, HT, T // 2]) for n in ("s_w1", "s_w2"))
        yo = alloc(nc, st, "s_yo", [P, 4, T])
        (ld, dtd, thd, magd, rrd, sid, rcd, cod, lk, bdz, bbd, bdr, btr, btc, bur, bud, xrd, cdr, yr, ysd, gld,
         hid) = (sem(n) for n in (
             "states_loaded", "steps_exp", "angles_ready", "decays_exp", "angle_reduced", "sines_ready",
             "angle2_reduced", "cosines_ready", "vector_link_5", "bc_zeroed", "b_scaled", "b_placed", "b_turned",
             "b_copied5", "bu_ready", "bu_read", "states_ready5", "c_placed", "y_summed5", "y_ready5",
             "gelu_ready", "gelu_high"))
        bank = lambda i: (s.work if i < 4 else s.acc)[:, i % 4, :]
        with nc.Block() as block:
            @block.sync
            def _(eng):
                for n, d in (("b_re", br), ("b_im", bi), ("c_re", cr), ("c_im", ci)):
                    eng.dma_start(d[:], dram[n]).then_inc(ld, 16)

            @block.gpsimd
            def _(eng):
                def place(dst, src, sign):
                    dv = dst.rearrange("p (a b) c -> p a b c", b=4)
                    sv = src[:].rearrange("p (a b) h -> p a b h", b=4)
                    for b in range(4):
                        for g in range(2):
                            rows, at = slice(64 * g, 64 * g + 64), 32 * b + 16 * g
                            ins = eng.tensor_scalar(dv[rows, :, b, at:at + 16], sv[rows, :, b, :], sign, None, ALU.mult)
                    return ins
                eng.memset(bd[:], 0.0)
                eng.memset(cd[:], 0.0).then_inc(bdz, 1)
                eng.wait_ge(bdz, 1)
                eng.wait_ge(bbd, 1)
                place(bd[:, 0], bbr, 1.0)
                place(bd[:, 1], bbi, 1.0).then_inc(bdr, 1)
                eng.wait_ge(ld, 64)
                place(cd[:, 0], cr, 1.0)
                place(cd[:, 1], ci, -1.0).then_inc(cdr, 1)

            @block.scalar
            def _(eng):
                eng.activation(dt[:], s.par("ldt"), ACT.Exp).then_inc(dtd, 1)
                eng.wait_ge(thd, 1)
                eng.activation(mag[:], ar[:], ACT.Exp).then_inc(magd, 1)
                eng.wait_ge(rrd, 1)
                eng.activation(si[:], rr[:], ACT.Sin).then_inc(sid, 1)
                eng.wait_ge(rcd, 1)
                eng.activation(co[:], kq[:], ACT.Sin).then_inc(cod, 1)
                for half in range(2):
                    for b in range(4):
                        eng.wait_ge(btr, 4 * half + b + 1)
                        at_least(eng, bur, 4 * half)
                        eng.activation(btn[:, b // 2, 4 * (b % 2):4 * (b % 2) + 4, :].rearrange("p a c -> p (a c)"),
                                       bank(b), ACT.Copy).then_inc(btc, 1)
                for a in range(4):
                    eng.wait_ge(ysd, a + 1)
                    eng.activation(yo[:, a, :], yo[:, a, :], ACT.Gelu).then_inc(gld, 1)
                eng.wait_ge(gld, 4)
                eng.activation(s.a0[:, 0:4, 0, :], yo[:], ACT.Copy).then_inc(hid, 1)

            @block.tensor
            def _(eng):
                def outputs(half):
                    eng.wait_ge(cdr, 1)
                    eng.wait_ge(xrd, half + 1)
                    for a in range(2):
                        for b in range(4):
                            for im, xs in ((0, xr), (1, xi)):
                                ins = eng.matmul(bank(4 + a)[:, 0:T], cd[:, im, HT * half + 4 * a + b, :],
                                                 xs[:, 4 * a + b, :], start=b + im == 0, stop=b == 3 and im == 1)
                        ins.then_inc(yr, 1)

                eng.wait_ge(bdr, 1)
                for half in range(2):
                    at_least(eng, bud, 4 * half)
                    for b in range(4):
                        for q in range(4):
                            ins = eng.transpose(bank(b)[:, q * P:(q + 1) * P],
                                                bd[:, b // 2, HT * half + 4 * (b % 2) + q, :], s.const("ident"))
                        ins.then_inc(btr, 1)
                    if half == 1:
                        outputs(0)
                    eng.wait_ge(btc, 4 * half + 4)
                    at_least(eng, ysd, 2 * half)
                    for q in range(4):
                        for im in range(2):
                            for t in range(2):
                                ins = eng.matmul(bank(2 * q + im)[:, t * T:(t + 1) * T], btn[:, im, 2 * q + t, :],
                                                 ua[:, S2 + (HT * half + 2 * q + t) // 4, :], start=True, stop=True)
                        ins.then_inc(bur, 1)
                eng.wait_ge(bud, 8)
                outputs(1)

            @block.vector
            def _(eng):
                link = Link(eng, lk)
                tt, ts, stt = eng.tensor_tensor, eng.tensor_scalar, eng.scalar_tensor_tensor
                are, aim = s.par("are"), s.par("aim")

                def reduce(out, turns, offset):
                    link(ts(kq[:], turns[:], magic, None, ALU.add))
                    link(ts(kq[:], kq[:], magic, None, ALU.subtract))
                    link(stt(out=out, in0=kq[:], scalar=-c1, in1=th[:], op0=ALU.mult, op1=ALU.add))
                    link(stt(out=out, in0=kq[:], scalar=-c2, in1=out, op0=ALU.mult, op1=ALU.add))
                    link(stt(out=out, in0=kq[:], scalar=-c3, in1=out, op0=ALU.mult, op1=ALU.add))
                    link(ts(out, out, offset, None, ALU.add))
                    return ts(out, out, 3.1415925, -3.1415925, ALU.min, ALU.max)

                eng.wait_ge(dtd, 1)
                tt(ar[:], are, dt[:], ALU.mult)
                tt(th[:], aim, dt[:], ALU.mult).then_inc(thd, 1)
                eng.wait_ge(thd, 1)
                link(ts(t1[:], th[:], 1 / (2 * np.pi), None, ALU.mult))
                reduce(rr[:], t1, 0.0).then_inc(rrd, 1)
                eng.wait_ge(rrd, 1)
                link(ts(t1[:], t1[:], 0.25, None, ALU.add))
                link(reduce(t1[:], t1, np.pi / 2))
                ts(kq[:], t1[:], 1.0, None, ALU.mult).then_inc(rcd, 1)
                eng.wait_ge(rcd, 1)
                tt(den[:], are, are, ALU.mult)
                link(tt(t1[:], aim, aim, ALU.mult))
                link(tt(den[:], den[:], t1[:], ALU.add))
                link(eng.reciprocal(den[:], den[:]))
                eng.wait_ge(magd, 1)
                eng.wait_ge(sid, 1)
                eng.wait_ge(cod, 1)
                tt(abr[:], mag[:], co[:], ALU.mult)
                link(tt(abi[:], mag[:], si[:], ALU.mult))
                link(ts(abr[:], abr[:], -1.0, None, ALU.add))
                tt(zr[:], abr[:], are, ALU.mult)
                link(tt(t1[:], abi[:], aim, ALU.mult))
                link(tt(zr[:], zr[:], t1[:], ALU.add))
                link(tt(zr[:], zr[:], den[:], ALU.mult))
                tt(zi[:], abi[:], are, ALU.mult)
                link(tt(t1[:], abr[:], aim, ALU.mult))
                link(tt(zi[:], zi[:], t1[:], ALU.subtract))
                link(tt(zi[:], zi[:], den[:], ALU.mult))
                eng.wait_ge(ld, 64)
                zrw, ziw = spread(zr[:], 16), spread(zi[:], 16)
                tt(bbr[:], br[:], zrw, ALU.mult)
                link(tt(tb2[:], bi[:], ziw, ALU.mult))
                link(tt(bbr[:], bbr[:], tb2[:], ALU.subtract))
                tt(bbi[:], bi[:], zrw, ALU.mult)
                link(tt(tb2[:], br[:], ziw, ALU.mult))
                tt(bbi[:], bbi[:], tb2[:], ALU.add).then_inc(bbd, 1)
                eng.wait_ge(bbd, 1)
                for half in range(2):
                    tiles_ = slice(HT * half, HT * half + HT)
                    eng.memset(er[:, :, 0:1], 1.0)
                    eng.memset(ei[:, :, 0:1], 0.0)
                    eng.tensor_copy(em[:, 0, 0, :], co[:, tiles_])
                    link(eng.tensor_copy(em[:, 0, 1, :], si[:, tiles_]))
                    m, now = 1, 0
                    while m < T:
                        c, sn = (spread(em[:, now, i, :], m) for i in range(2))
                        e0r, e0i, v1, v2 = er[:, :, 0:m], ei[:, :, 0:m], w1[:, :, 0:m], w2[:, :, 0:m]
                        tt(v1, e0r, c, ALU.mult)
                        link(tt(v2, e0i, sn, ALU.mult))
                        link(tt(er[:, :, m:2 * m], v1, v2, ALU.subtract))
                        tt(v1, e0r, sn, ALU.mult)
                        link(tt(v2, e0i, c, ALU.mult))
                        link(tt(ei[:, :, m:2 * m], v1, v2, ALU.add))
                        if 2 * m < T:
                            tt(sqs[:, 0, :], em[:, now, 0, :], em[:, now, 0, :], ALU.mult)
                            tt(sqs[:, 1, :], em[:, now, 1, :], em[:, now, 1, :], ALU.mult)
                            link(stt(out=em[:, 1 - now, 1, :], in0=em[:, now, 0, :], scalar=2.0,
                                     in1=em[:, now, 1, :], op0=ALU.mult, op1=ALU.mult))
                            link(tt(em[:, 1 - now, 0, :], sqs[:, 0, :], sqs[:, 1, :], ALU.subtract))
                            now = 1 - now
                        m *= 2
                    for q in range(4):
                        eng.wait_ge(bur, 4 * half + q + 1)
                        if half == 1:
                            eng.wait_ge(yr, 2)
                        pr = slice(2 * q, 2 * q + 2)
                        re, im = (bank(2 * q + i).rearrange("p (a t) -> p a t", a=2) for i in range(2))
                        tt(q1[:], er[:, pr], re, ALU.mult)
                        link(tt(q2[:], ei[:, pr], im, ALU.mult))
                        link(tt(xr[:, pr], q1[:], q2[:], ALU.add))
                        tt(q1[:], er[:, pr], im, ALU.mult)
                        tt(q2[:], ei[:, pr], re, ALU.mult).then_inc(bud, 1)
                        eng.wait_ge(bud, 4 * half + q + 1)
                        link(tt(xi[:, pr], q1[:], q2[:], ALU.subtract))
                        for jl in range(2 * q, 2 * q + 2):
                            j = HT * half + jl
                            for xs in (xr, xi):
                                ins = eng.tensor_tensor_scan(xs[:, jl, :], mag[:, j:j + 1].to_broadcast([P, T]),
                                                             xs[:, jl, :], 0.0, ALU.mult, ALU.add)
                        link(ins)
                        v1, v2 = (w[:, 0:4, :].rearrange("p a t -> p (a t)").rearrange("p (a t) -> p a t", a=2)
                                  for w in (w1, w2))
                        tt(q1[:], er[:, pr], xr[:, pr], ALU.mult)
                        tt(q2[:], ei[:, pr], xi[:, pr], ALU.mult)
                        tt(v1, ei[:, pr], xr[:, pr], ALU.mult)
                        link(tt(v2, er[:, pr], xi[:, pr], ALU.mult))
                        tt(xr[:, pr], q1[:], q2[:], ALU.subtract)
                        ins = tt(xi[:, pr], v1, v2, ALU.add)
                        if q < 3:
                            link(ins)
                        else:
                            ins.then_inc(xrd, 1)
                            eng.wait_ge(xrd, half + 1)
                    for a in range(2):
                        eng.wait_ge(yr, 2 * half + a + 1)
                        at = 2 * half + a
                        stt(out=yo[:, at, :], in0=ua[:, S2 + at, :], scalar=s.par("d2", at), in1=bank(4 + a)[:, 0:T],
                            op0=ALU.mult, op1=ALU.add).then_inc(ysd, 1)
                eng.wait_ge(hid, 1)
                link(tt(s.a0[:, 0:4, 1, :], yo[:], s.a0[:, 0:4, 0, :].bitcast(F32), ALU.subtract))


def clear_pads(nc, s):
    with nc.Block() as block:
        @block.vector
        def _(eng):
            eng.memset(s.tb[:], 0.0)


def second_block(nc, dram, s, out_dram):
    final_norm(nc, s, "final1_g")
    with ExitStack() as st:
        ub = alloc(nc, st, "ub", [P, 2 * KT, T])
        with ExitStack() as uas:
            ua = alloc(nc, uas, "ua", [P, GA2, T])
            with ExitStack() as rg:
                s.ring(rg, "_2")
                clear_pads(nc, s)
                emit = s.phase("emit", "", KT // 2, 0, 2, None, "emit", out=s.a0, g="norm2_g")
                pa = s.phase("in_a", "w_in_2", GA2 // 2, 4, 2, s.a0, "bias", out=ua, g="b_in", after=emit,
                             sum_after=True)
                pb = s.phase("in_b", "w_in_2", KT, 4, 2, s.a0, "sigmoid", out=ub, g="b_in", g0=GA2,
                             w0=4 * GA2 // 2)
                phs = [pa, pb]
                with nc.Block() as block:
                    @block.sync
                    def _(eng):
                        for ph in phs:
                            s.sp(eng, ph)

                    @block.scalar
                    def _(eng):
                        for v in range(KT // 2):
                            s.act_finish(eng, emit, v, v % 2)
                        s.act(eng, phs)

                    @block.vector
                    def _(eng):
                        s.dve(eng, phs)

                    @block.gpsimd
                    def _(eng):
                        for v in range(KT // 2):
                            s.pool_finish(eng, emit, v, v % 2)

                    @block.tensor
                    def _(eng):
                        s.pe(eng, phs)
            window_attention(nc, s, ua)
            s5(nc, dram, s, ua)
        with ExitStack() as ms:
            a1 = alloc(nc, ms, "a1_2", [P, KT, 2, T], F32R)
            gl = alloc(nc, ms, "gl", [P, 4, T])
            with ExitStack() as rg:
                s.ring(rg, "_m")
                clear_pads(nc, s)
                g1 = s.phase("glu_g", "glu", 2, 1, 4, s.a0, "glu_gate", out=gl, g="b_glu", g0=4)
                g2 = s.phase("glu_v", "glu", 2, 1, 4, s.a0, "glu_val", out=s.a0, t0=12, src=gl, w0=2)
                ba = s.phase("br_attn", "br_attn", 8, 2, 2, s.a0[:, 4:12], "br_attn", out=ub)
                bs = s.phase("br_ssm", "br_ssm", 8, 1, 4, s.a0[:, 12:16], "br_ssm", out=a1, src=ub, g0=KT, after=g2)
                wo = s.phase("w_out_2", "w_out_2", 8, 4, 2, a1, "resid", out=s.a0, g="ffn2_g", after=bs)
                stream_block(nc, s, [g1, g2, ba, bs, wo])
    with ExitStack() as st:
        a1 = alloc(nc, st, "a1_3", [P, KT, 2, T], F32R)
        gb = alloc(nc, st, "gb", [P, KT, T])
        with ExitStack() as rg:
            s.ring(rg, "_3")
            clear_pads(nc, s)
            phs = []
            for q, t0 in enumerate((0, KT, 2 * KT)):
                n = min(KT, FT2 - t0)
                gate = s.phase("gate", "up_gate", n // 2, 4, 2, s.a0, "gate", out=gb, g="c2", g0=3 * t0, p0=t0,
                               taps=3, w0=2 * t0, sum_after=q == 0)
                val = s.phase("val", "up_val", n // 2, 4, 2, s.a0, "val", out=a1, src=gb, w0=2 * t0)
                down = s.phase("down", "down", 8, n // 4, 4 if n % 16 else 2, a1, "sumsq" if q == 2 else "acc",
                               w0=32 * q, after=val)
                phs += [gate, val, down]
            stream_block(nc, s, phs)
    final_norm(nc, s, "final2_g", out_dram)


def build(nc, dram, out_dram):
    with ExitStack() as whole:
        s = Stream(nc, whole, dram)
        s_load = whole.enter_context(nc.semaphore("inputs_loaded"))
        s_prm = whole.enter_context(nc.semaphore("parameters_loaded"))
        s_zero = whole.enter_context(nc.semaphore("pads_zeroed"))
        mixers(nc, dram, s, s_load, s_prm, s_zero)
        attention_and_mlp(nc, dram, s)
        second_block(nc, dram, s, out_dram)


def alloc(nc, stack, name, shape, dt=F32):
    return stack.enter_context(nc.sbuf_tensor(name, shape, dt))


def zero_pads(eng, s, s_zero):
    eng.memset(s.eps[:, 0:1], EPS)
    eng.memset(s.eps[:, 1:2], RWKV_EPS)
    eng.memset(s.tb[:], 0.0).then_inc(s_zero, 1)


def mixers(nc, dram, s, s_load, s_prm, s_zero):
    with ExitStack() as st:
        u = alloc(nc, st, "u", [P, U_TILES, T])
        with ExitStack() as rg:
            s.ring(rg, "_in")
            emit = s.phase("emit", "", KT // 2, 0, 2, None, "emit", out=s.a0, g="norm_mix_g")
            rw = s.phase("rwkv_in", "w_in", RWKV_TILES // 2, 4, 2, s.a0, "rwkv", out=u, after=emit,
                           sum_after=True)
            z = s.phase("z_in", "w_in", RW // 2, 4, 2, s.a0, "z", out=u, t0=Z0, w0=4 * Z0 // 2)
            conv = s.phase("xbc_in", "w_in", 6, 4, 2, s.a0, "conv", out=u, t0=XS0, w0=4 * XS0 // 2,
                           g="conv", taps=4)
            phs = [rw, z, conv]
            with nc.Block() as block:
                @block.sync
                def _(eng):
                    eng.dma_start(s.prm[:], dram["prm"]).then_inc(s_prm, 16)
                    eng.dma_start(s.x[:].rearrange("p a b -> p (a b)"), dram["x"]).then_inc(s_load, 16)
                    s.prefetch(eng, rw)
                    eng.dma_start(s.consts[:], dram["consts"]).then_inc(s_prm, 16)
                    s.sp(eng, rw, skip=RING)
                    s.sp(eng, z)
                    s.sp(eng, conv)

                @block.scalar
                def _(eng):
                    eng.wait_ge(s_prm, 16)
                    eng.wait_ge(s_load, 16)
                    for v in range(KT // 2):
                        s.act_finish(eng, emit, v, v % 2)
                    s.act(eng, phs)

                @block.vector
                def _(eng):
                    zero_pads(eng, s, s_zero)
                    eng.wait_ge(s_zero, 1)
                    eng.wait_ge(s_prm, 32)
                    s.dve(eng, phs)

                @block.gpsimd
                def _(eng):
                    for v in range(KT // 2):
                        s.pool_finish(eng, emit, v, v % 2)

                @block.tensor
                def _(eng):
                    eng.wait_ge(s_prm, 32)
                    s.pe(eng, phs)
        rwkv(nc, dram, s, u)
        ssd(nc, s, u)


def tiled(a):
    rows, cols = a.shape
    return np.ascontiguousarray(
        a.reshape(rows // (CK * P), CK, P, cols // UNIT, UNIT).transpose(3, 0, 2, 1, 4)
        .reshape(-1, P, CK * UNIT))


def columns(v):
    return np.ascontiguousarray(np.asarray(v).reshape(-1, P).T)


def channel_major(a):
    n = a.shape[1] // P
    return np.ascontiguousarray(a.T.reshape(n, P, -1).transpose(1, 0, 2).reshape(P, -1))


def lay_out(i):
    f = {k: np.asarray(v) for k, v in i.items()}
    w = f["w_in"][0]
    ssd, rk = 2576, 3072
    zeros = np.zeros((D, 1), np.float32)

    def cols(a, b):
        return w[:, a:b]
    tile_pw = [cols(ssd + rk, ssd + rk + RANK), cols(2560, 2576), zeros.repeat(16, 1)]
    tile_pa = [cols(ssd + rk + RANK, ssd + rk + 2 * RANK), zeros.repeat(32, 1)]
    w_in = np.concatenate([cols(ssd, ssd + rk), cols(ssd + rk + 2 * RANK, 6096)] + tile_pw + tile_pa
                          + [cols(0, 1024), cols(1024, 2560)], axis=1)
    mu = f["rwkv_mu"][0]
    z16 = np.zeros(32, np.float32)
    mu = np.concatenate([mu[0:rk], mu[rk + 2 * RANK:], mu[rk:rk + RANK], z16, mu[rk + RANK:rk + 2 * RANK], z16])

    def taps(a):
        k, c = a.shape
        return a.reshape(k, c // P, P).transpose(2, 1, 0).reshape(P, -1)

    def rows(v):
        return np.broadcast_to(v[None, :], (P, v.shape[0]))

    def states(a):
        return a.reshape(ST, P).T
    slopes = (2.0 ** (-8.0 * np.arange(1, NH + 1) / NH)).astype(np.float32)
    prm = {
        "norm_mix_g": columns(f["norm_mix_g"]), "norm_x_g": columns(f["norm_x_g"]),
        "norm_mem_g": columns(f["norm_mem_g"]), "norm_ffn_g": columns(f["norm_ffn_g"]),
        "norm2_g": columns(f["attn_norm_g_2"]), "ffn2_g": columns(f["ffn_norm_g_2"]),
        "final1_g": columns(f["final_norm_g"]), "final2_g": columns(f["final_norm_g_2"]),
        "mu": columns(mu), "conv": taps(f["ssd_conv_w"][0, :, 0]), "convb": columns(f["ssd_conv_b"]),
        "ssd_d": columns(np.repeat(f["ssd_d"][0], 64)), "ssd_g": columns(f["ssd_norm_g"]),
        "w0": columns(f["rwkv_w0"]), "a0": columns(f["rwkv_a0"]), "k_k": columns(f["rwkv_k_k"]),
        "k_a": columns(f["rwkv_k_a"]), "r_k": columns(f["rwkv_r_k"].reshape(-1)),
        "ln_w": columns(f["rwkv_ln_w"]), "ln_b": columns(f["rwkv_ln_b"]),
        "dt_bias": rows(f["ssd_dt_bias"][0]), "a_log": rows(f["ssd_a_log"][0]),
        "sinks": rows(f["attn_sinks_2"][0]), "slopes": rows(slopes),
        "b_in": columns(f["b_in_2"]), "b_glu": columns(f["b_glu_2"]),
        "c2": taps(f["conv_w_2"][0]), "c2b": columns(f["conv_b_2"]),
        "are": states(f["ssm_a_re_2"][0]), "aim": states(f["ssm_a_im_2"][0]),
        "ldt": states(np.repeat(f["ssm_log_dt_2"][0], 64)), "d2": columns(f["ssm_d_2"]),
    }
    packed = np.concatenate([prm[n] for n in PARAMS.at], axis=1)
    assert packed.shape == (P, PARAMS.n)

    def pad_rows(a, n=P):
        return np.concatenate([a, np.zeros((n - a.shape[0], a.shape[1]), np.float32)])
    w1, w2 = f["ffn_w1"][0], f["ffn_w2"][0]
    up, down = f["w_up_2"][0], f["w_down_2"][0]
    return {
        "consts": constants(), "prm": packed,
        "x": channel_major(f["x"][0]), "mem": channel_major(f["mem"][0]),
        "w_in": tiled(w_in), "w_out": tiled(f["w_out"][0]),
        "w2": pad_rows(f["rwkv_w2"][0]), "a2": pad_rows(f["rwkv_a2"][0]),
        "g2": np.ascontiguousarray(f["rwkv_g2"][0].reshape(2, P, 1024).transpose(1, 0, 2)),
        "wq": tiled(f["xattn_wq"][0]), "wk": tiled(f["xattn_wk"][0]),
        "wv": tiled(f["xattn_wv"][0]), "wo": tiled(f["xattn_wo"][0]),
        "ffn1": tiled(w1), "ffn2": np.concatenate([tiled(w2[D * q:D * (q + 1)]) for q in range(4)]),
        "w_in_2": tiled(f["w_in_2"][0]), "w_out_2": tiled(f["w_out_2"][0]),
        "glu": tiled(np.concatenate([f["w_glu_2"][0][:, 512:], f["w_glu_2"][0][:, :512]], axis=1)),
        "br_attn": tiled(f["w_branch_attn_2"][0]), "br_ssm": tiled(f["w_branch_ssm_2"][0]),
        "up_val": tiled(up[:, :FF2]), "up_gate": tiled(up[:, FF2:]),
        "down": np.concatenate([tiled(down[a:b]) for a, b in ((0, D), (D, 2 * D), (2 * D, FF2))]),
        "b_re": state_rows(f["ssm_b_re_2"][0]), "b_im": state_rows(f["ssm_b_im_2"][0]),
        "c_re": state_rows(f["ssm_c_re_2"][0].transpose(0, 2, 1)),
        "c_im": state_rows(f["ssm_c_im_2"][0].transpose(0, 2, 1)),
    }


def state_rows(a):
    return np.ascontiguousarray(a.reshape(ST, P, 16).transpose(1, 0, 2))


def kernel(**inputs):
    import concourse.bacc as bacc
    from concourse.bass_utils import run_bass_kernel_spmd

    nc = bacc.Bacc("TRN2", target_bir_lowering=False, num_devices=1)
    arrays = lay_out(inputs)
    dram = {n: nc.dram_tensor("in_" + n, a.shape, F32, kind="ExternalInput").ap() for n, a in arrays.items()}
    out = nc.dram_tensor("out_dram", (P, KT * T), F32, kind="ExternalOutput").ap()
    build(nc, dram, out)
    r = run_bass_kernel_spmd(nc, [{"in_" + n: a for n, a in arrays.items()}], core_ids=[0])
    got = r.results[0]["out_dram"]
    return got.reshape(P, KT, T).transpose(2, 1, 0).reshape(1, T, D)
```

```python
from contextlib import ExitStack
from dataclasses import dataclass

import numpy as np

import concourse.bass as bass
from concourse import mybir

F32 = mybir.dt.float32
F32R = mybir.dt.float32r
I32 = mybir.dt.int32
ACT = mybir.ActivationFunctionType
ALU = mybir.AluOpType
AX = mybir.AxisListType

P = 128
T = 256
D = 2048
KT = D // P
EPS = 1e-6
UNIT = 256
CK = 4
RING = 4

RW = 1024 // P
R0, K0, V0, PG0, PW0, PA0 = 0, RW, 2 * RW, 3 * RW, 3 * RW + 2, 3 * RW + 3
RWKV_TILES = 3 * RW + 4
Z0 = RWKV_TILES
XS0 = Z0 + RW
B0 = XS0 + RW
C0 = B0 + 2
U_TILES = C0 + 2
RANK = 96
DT_ROW = RANK
NH = 16
Q = 128
NCH = T // Q
LEVELS = 7
E_HALF = float(np.exp(-0.5))
RWKV_EPS = 64e-5
XH, XD = 4, 512

Q2, K2, V2, S2, GA2, GS2 = 0, 8, 9, 10, 14, 30
U2_TILES = 46
FF2 = 5632
FT2 = FF2 // P
ST = 16
LN2 = float(np.log(2.0))

CONST_COLS = {}
for _i, _n in enumerate(["ident", "upper", "upper_in", "lower", "ones", "half_ones", "top_left"]
                        + [f"lev{k}" for k in range(LEVELS)] + ["dist", "dist_b"]):
    CONST_COLS[_n] = _i * P


def constants():
    i, j = np.arange(P)[:, None], np.arange(P)[None, :]
    lev = [((i >> (k + 1)) == (j >> (k + 1))) & (((j >> k) & 1) == 1) & (((i >> k) & 1) == 0)
           for k in range(LEVELS)]
    dist = (i + P - np.arange(2 * P)[None, :]).astype(np.float32)
    dist = np.where((dist >= 0) & (dist < P), dist, 1e32)
    parts = [i == j, i < j, i <= j, i > j, i >= 0 * j, (i // 64) == (j // 64), lev[0].T] + lev
    return np.concatenate([np.asarray(m, np.float32) * np.ones((P, P), np.float32) for m in parts]
                          + [dist.astype(np.float32)], axis=1)


class Params:

    def __init__(self):
        self.at, self.n = {}, 0

    def add(self, name, cols):
        self.at[name] = (self.n, cols)
        self.n += cols


PARAMS = Params()
for _name, _cols in [
    ("norm_mix_g", KT), ("norm_x_g", KT), ("norm_mem_g", KT), ("norm_ffn_g", KT),
    ("norm2_g", KT), ("ffn2_g", KT), ("final1_g", KT), ("final2_g", KT),
    ("mu", RWKV_TILES), ("conv", 4 * 12), ("convb", 12), ("ssd_d", RW), ("ssd_g", RW),
    ("w0", RW), ("a0", RW), ("k_k", RW), ("k_a", RW), ("r_k", RW), ("ln_w", RW), ("ln_b", RW),
    ("dt_bias", NH), ("a_log", NH), ("sinks", NH), ("slopes", NH),
    ("b_in", U2_TILES), ("b_glu", 8), ("c2", 3 * FT2), ("c2b", FT2),
    ("are", ST), ("aim", ST), ("ldt", ST), ("d2", 4),
]:
    PARAMS.add(_name, _cols)


@dataclass
class Phase:
    name: str
    w: object
    units: int
    nc: int
    body: int
    act: object
    kind: str
    out: object = None
    t0: int = 0
    src: object = None
    g: str = ""
    g0: int = 0
    p0: int = 0
    taps: int = 0
    after: object = None
    x_after: int = 0
    w0: int = 0
    sum_after: bool = False
    norm: int = 0
    base: object = None
    k: object = None


@dataclass
class Kind:
    links: int = 0
    evac: int = 0
    fin: int = 0
    pool: int = 0
    alink: int = 0

    def counts(self):
        return dict(links=self.links, evac=self.evac, fin=self.fin, pool=self.pool, alink=self.alink)


KINDS = {
    "rwkv": Kind(2, 1), "z": Kind(0, 1, 1), "conv": Kind(4, 1, 1), "acc": Kind(1),
    "resid": Kind(1, 0, 1, 1, 1), "emit": Kind(0, 0, 1, 1, 1), "sumsq": Kind(1, 0, 1, 1),
    "relu2": Kind(1, 1, 1, 1), "gate": Kind(3, 1, 1), "val": Kind(1, 1, 1, 1),
    "scaled": Kind(0, 1), "plain": Kind(), "tok": Kind(), "bias": Kind(1, 1), "sigmoid": Kind(0, 1, 1),
    "glu_gate": Kind(0, 0, 1), "glu_val": Kind(0, 1, 1, 1), "br_attn": Kind(0, 1),
    "br_ssm": Kind(1, 1, 1, 1),
}
SPLITS = ("resid", "emit", "relu2", "val", "glu_val", "br_ssm")


def at_least(eng, s, value):
    if not (isinstance(value, int) and value < 1):
        eng.wait_ge(s, value)


def pair(buf, v, t0=0):
    return buf[:, t0 + 2 * v:t0 + 2 * v + 2] if isinstance(v, int) else buf[:, bass.ds(v * 2 + t0, 2)]


def tile(buf, i):
    return buf[:, i, :] if isinstance(i, int) else buf[:, bass.ds(i, 1), :].rearrange("p a t -> p (a t)")


class Stream:

    def __init__(self, nc, stack, dram):
        self.nc, self.dram = nc, dram

        def sb(name, shape, dt=F32):
            return stack.enter_context(nc.sbuf_tensor(name, shape, dt))

        def sem(name):
            return stack.enter_context(nc.semaphore(name))

        self.x = sb("x", [P, KT, T])
        self.a0 = sb("a0", [P, KT, 2, T], F32R)
        self.consts = sb("consts", [P, dram["consts"].shape[1]])
        self.prm = sb("prm", [P, PARAMS.n])
        self.rstd = sb("rstd", [P, T])
        self.root = sb("root", [P, T])
        self.sq = sb("sq", [P, 2, T])
        self.eps = sb("eps", [P, 2])
        self.acc = stack.enter_context(nc.psum_tensor("acc", [P, 4, 512], F32))
        self.work = stack.enter_context(nc.psum_tensor("work", [P, 4, 512], F32))

        self.s_raw = [sem(f"raw_loaded{i}") for i in range(RING)]
        self.s_hi = sem("high_split")
        self.s_lo = sem("low_split")
        self.s_used = sem("chunk_multiplied")
        self.s_free = sem("banks_read")
        self.s_link = sem("vector_link")
        self.s_evac = sem("evacuated")
        self.s_alink = sem("scaled_copy")
        self.s_fin = sem("finished")
        self.s_pool = sem("low_written")
        self.s_sum = sem("squares_summed")
        self.s_root = sem("root_ready")
        self.s_rstd = sem("rstd_ready")
        self.total = dict(c=0, u=0, links=0, evac=0, fin=0, pool=0, alink=0, norm=0)

    def const(self, name, n=P):
        return self.consts[:, CONST_COLS[name]:CONST_COLS[name] + n]

    def par(self, name, i=None, n=1):
        at, cols = PARAMS.at[name]
        if i is None:
            return self.prm[:, at:at + cols]
        return self.prm[:, at + i:at + i + n] if isinstance(i, int) else self.prm[:, bass.ds(i + at, n)]

    def ring(self, stack, tag, parts=True):
        nc = self.nc

        def sb(name, shape, dt=F32):
            return stack.enter_context(nc.sbuf_tensor(name + tag, shape, dt))
        self.raw = sb("raw", [P, RING, CK * UNIT])
        self.hi = sb("hi", [P, RING, CK * UNIT], F32R)
        self.lo = sb("lo", [P, RING, CK * UNIT], F32R)
        self.ta = sb("ta", [P, 2, T])
        self.tb = sb("tb", [P, 2, 2, T + 4])
        if not parts:
            return
        self.th = sb("th", [P, 2, 2, T])
        self.tq = sb("tq", [P, 2, T])

    def phase(self, name, w, units, nc_, body, act, kind, **kw):
        ph = Phase(name, self.dram.get(w), units, nc_, body, act, kind, **kw)
        k = KINDS[kind]
        t = self.total
        ph.base = dict(t)
        ph.k = k
        if kind != "emit":
            t["c"] += units * nc_
            t["u"] += units
        for f, a_unit in k.counts().items():
            t[f] += units * a_unit
        if ph.sum_after:
            t["norm"] += 1
            ph.norm = t["norm"]
        return ph

    def loop(self, eng, ph, step):
        bodies = ph.units // ph.body
        if bodies:
            for j in range(ph.body):
                step(j, j)
        if bodies > 1:
            with eng.Fori(1, bodies) as i:
                for j in range(ph.body):
                    step(i * ph.body + j, j)
        for j in range(ph.units - bodies * ph.body):
            step(bodies * ph.body + j, j)

    def sp(self, eng, ph, skip=0):
        def step(v, j):
            for k in range(ph.nc):
                c = (v - j) * ph.nc + (j * ph.nc + k)
                if not (isinstance(c, int) and c < skip):
                    self.load(eng, ph, c, j * ph.nc + k)
        self.loop(eng, ph, step)

    def load(self, eng, ph, c, n):
        slot = (ph.base["c"] + n) % RING
        at_least(eng, self.s_lo, c + (ph.base["c"] - RING + 1))
        eng.dma_start(self.raw[:, slot, :], ph.w[c + ph.w0]).then_inc(self.s_raw[slot], 16)

    def prefetch(self, eng, ph):
        for c in range(RING):
            self.load(eng, ph, c, c)

    def act(self, eng, phs, aside=None, emit=None):
        last = None
        for ph in phs:
            def step(v, j, ph=ph, last=last):
                self.act_split(eng, ph, v, j, emit if ph is phs[0] and isinstance(v, int) and v == 0 else None)
                if isinstance(v, int) and v == 1 and ph.sum_after:
                    eng.wait_ge(self.s_sum, ph.norm)
                    eng.activation(self.root[:], self.work[:, 3, 0:T], ACT.Sqrt, scale=1.0 / D,
                                   bias=self.eps[:, 0:1]).then_inc(self.s_root, 1)
                if isinstance(v, int) and v == 1 and aside and ph is phs[-1]:
                    aside(eng)
                if not (isinstance(v, int) and v == 0):
                    self.act_finish(eng, ph, v - 1, (ph.base["u"] + j - 1) % 2)
                elif last:
                    self.act_finish(eng, last, last.units - 1, (last.base["u"] + last.units - 1) % 2)
            self.loop(eng, ph, step)
            last = ph
        self.act_finish(eng, last, last.units - 1, (last.base["u"] + last.units - 1) % 2)

    def act_split(self, eng, ph, v, j, emit=None):
        c0 = ph.base["c"]
        for k in range(ph.nc):
            if emit:
                for pv in (2 * k, 2 * k + 1):
                    self.act_finish(eng, emit, pv, pv % 2)
            n = j * ph.nc + k
            slot = (c0 + n) % RING
            eng.wait_ge(self.s_raw[slot], (v - j) * ph.nc * (16 // RING) + 16 * ((c0 + n) // RING + 1))
            at_least(eng, self.s_used, (v - j) * ph.nc + (c0 + n - RING + 1))
            eng.activation(self.hi[:, slot, :], self.raw[:, slot, :], ACT.Copy).then_inc(self.s_hi, 1)

    def act_finish(self, eng, ph, v, s):
        k, b, kind = ph.k, ph.base, ph.kind
        if not k.fin:
            return
        if k.evac:
            eng.wait_ge(self.s_evac, v + (b["evac"] + 1))
        elif kind != "emit":
            eng.wait_ge(self.s_free, v + (b["u"] + 1))
        done = self.s_fin
        if kind in ("resid", "emit", "sumsq"):
            at_least(eng, self.s_pool, v + b["pool"])
            if kind == "sumsq":
                eng.activation(self.tq[:], pair(self.x, v), ACT.Square).then_inc(done, 1)
                return
            for t in range(2):
                ins = eng.activation(self.th[:, s, t, :], tile(self.x, v * 2 + t), ACT.Copy,
                                     scale=self.par(ph.g, v * 2 + t))
            ins.then_inc(self.s_alink, 1)
            eng.activation(self.tq[:], pair(self.x, v), ACT.Square)
            eng.wait_ge(self.s_alink, v + (b["alink"] + 1))
        if kind in SPLITS:
            eng.activation(pair(ph.out, v, ph.t0)[:, :, 0, :], self.th[:, s], ACT.Copy).then_inc(done, 1)
        elif kind == "z":
            eng.activation(pair(ph.out, v, ph.t0), self.tb[:, s, :, 3:3 + T], ACT.Silu).then_inc(done, 1)
        elif kind == "conv":
            eng.activation(pair(ph.out, v, ph.t0), self.th[:, s], ACT.Silu).then_inc(done, 1)
        elif kind == "gate":
            eng.activation(pair(ph.out, v, ph.t0), self.th[:, s], ACT.Gelu).then_inc(done, 1)
        elif kind in ("sigmoid", "glu_gate"):
            for t in range(2):
                ins = eng.activation(tile(ph.out, v * 2 + (ph.t0 + t)), self.tb[:, s, t, 3:3 + T],
                                     ACT.Sigmoid, bias=self.par(ph.g, v * 2 + (ph.g0 + t)))
            ins.then_inc(done, 1)

    def dve(self, eng, phs, aside=None):
        last = None
        for ph in phs:
            def step(v, j, ph=ph, last=last):
                for k in range(ph.nc):
                    self.split_low(eng, ph, v, j, k)
                if isinstance(v, int) and v == 1 and ph.sum_after:
                    eng.wait_ge(self.s_root, ph.norm)
                    eng.reciprocal(self.rstd[:], self.root[:]).then_inc(self.s_rstd, 1)
                    eng.wait_ge(self.s_rstd, ph.norm)
                if isinstance(v, int) and v == 1 and aside and ph is phs[-1]:
                    aside(eng)
                if not (isinstance(v, int) and v == 0):
                    self.evacuate(eng, ph, v - 1, (ph.base["u"] + j - 1) % 2)
                elif last:
                    self.evacuate(eng, last, last.units - 1, (last.base["u"] + last.units - 1) % 2)
            self.loop(eng, ph, step)
            last = ph
        self.evacuate(eng, last, last.units - 1, (last.base["u"] + last.units - 1) % 2)

    def split_low(self, eng, ph, v, j, k):
        n = j * ph.nc + k
        slot = (ph.base["c"] + n) % RING
        eng.wait_ge(self.s_hi, (v - j) * ph.nc + (ph.base["c"] + n + 1))
        eng.tensor_tensor(self.lo[:, slot, :], self.raw[:, slot, :],
                          self.hi[:, slot, :].bitcast(F32), ALU.subtract).then_inc(self.s_lo, 1)

    def evacuate(self, eng, ph, v, s):
        k, b, kind = ph.k, ph.base, ph.kind
        banks = self.acc[:, 2 * s:2 * s + 2, :]
        halves = banks.rearrange("p t (h n) -> p t n h", h=2)
        eng.wait_ge(self.s_used, v * ph.nc + (b["c"] + ph.nc))
        at_least(eng, self.s_evac, v * k.evac + b["evac"])
        at_least(eng, self.s_free, v + b["u"])
        free = v + (b["u"] + 1)
        steps = [0]

        def link(ins):
            steps[0] += 1
            ins.then_inc(self.s_link, 1)
            eng.wait_ge(self.s_link, v * k.links + (b["links"] + steps[0]))

        if kind in ("resid", "acc", "sumsq"):
            xp = pair(self.x, v)
            if isinstance(v, int) and v < 2 and ph.x_after:
                eng.wait_ge(self.s_fin, ph.x_after)
            link(eng.tensor_tensor(xp, banks[:, :, 0:T], xp, ALU.add))
            eng.tensor_tensor(xp, banks[:, :, T:2 * T], xp, ALU.add).then_inc(self.s_free, 1)
            return
        if kind == "plain":
            eng.tensor_reduce(pair(ph.out, v, ph.t0), halves, AX.X, ALU.add).then_inc(self.s_free, 1)
            return
        if kind == "tok":
            at = bass.ds(v * UNIT, UNIT) if not isinstance(v, int) else slice(v * UNIT, (v + 1) * UNIT)
            eng.tensor_copy(ph.out[:, :, at], banks[:, :, 0:T]).then_inc(self.s_free, 1)
            return
        if k.fin:
            at_least(eng, self.s_fin, v + (b["fin"] - 1))
        elif isinstance(v, int) and v < 2:
            at_least(eng, self.s_fin, v + (b["fin"] - 1))
        if k.pool:
            at_least(eng, self.s_pool, v + (b["pool"] - 1))
        elif isinstance(v, int) and v < 2:
            at_least(eng, self.s_pool, v + (b["pool"] - 1))
        cur = self.tb[:, s, :, 3:3 + T]
        if kind == "glu_gate":
            eng.tensor_reduce(cur, halves, AX.X, ALU.add).then_inc(self.s_free, 1)
            return
        eng.tensor_reduce(self.ta[:], halves, AX.X, ALU.add).then_inc(self.s_free, 1)
        eng.wait_ge(self.s_free, free)
        th = self.th[:, s]
        if kind == "br_attn":
            eng.tensor_tensor(pair(ph.out, v, ph.t0), self.ta[:], pair(ph.out, v, ph.t0),
                              ALU.mult).then_inc(self.s_evac, 1)
            return
        if kind == "br_ssm":
            link(eng.tensor_tensor(cur, self.ta[:], pair(ph.src, v, ph.g0), ALU.mult))
            eng.tensor_tensor(th, cur, pair(ph.src, v), ALU.add).then_inc(self.s_evac, 1)
            return
        if kind == "glu_val":
            for t in range(2):
                ins = eng.scalar_tensor_tensor(out=self.th[:, s, t, :], in0=self.ta[:, t, :],
                                               scalar=self.par("b_glu", v * 2 + t),
                                               in1=tile(ph.src, v * 2 + t), op0=ALU.add, op1=ALU.mult)
            ins.then_inc(self.s_evac, 1)
            return
        rs = self.rstd[:].unsqueeze(1).to_broadcast([P, 2, T])
        if kind == "scaled":
            eng.tensor_tensor(pair(ph.out, v, ph.t0), self.ta[:], rs, ALU.mult).then_inc(self.s_evac, 1)
            return
        scale = eng.tensor_tensor(cur, self.ta[:], rs, ALU.mult)
        if kind in ("z", "sigmoid"):
            scale.then_inc(self.s_evac, 1)
            return
        link(scale)
        if kind == "rwkv":
            link(eng.tensor_tensor(self.ta[:], self.tb[:, s, :, 2:2 + T], cur, ALU.subtract))
            for t in range(2):
                ins = eng.scalar_tensor_tensor(out=tile(ph.out, v * 2 + (ph.t0 + t)), in0=self.ta[:, t, :],
                                               scalar=self.par("mu", v * 2 + t), in1=cur[:, t, :],
                                               op0=ALU.mult, op1=ALU.add)
            ins.then_inc(self.s_evac, 1)
        elif kind in ("conv", "gate"):
            taps = ph.taps
            for t in range(2):
                ins = eng.tensor_scalar(self.th[:, s, t, :], cur[:, t, :],
                                        self.par(ph.g, v * (2 * taps) + (ph.g0 + t * taps + taps - 1)),
                                        self.par(ph.g + "b", v * 2 + (ph.p0 + t)), ALU.mult, ALU.add)
            link(ins)
            for q in range(taps - 1):
                for t in range(2):
                    ins = eng.scalar_tensor_tensor(
                        out=self.th[:, s, t, :], in0=self.tb[:, s, t, 4 - taps + q:4 - taps + q + T],
                        scalar=self.par(ph.g, v * (2 * taps) + (ph.g0 + t * taps + q)),
                        in1=self.th[:, s, t, :], op0=ALU.mult, op1=ALU.add)
                if q < taps - 2:
                    link(ins)
            ins.then_inc(self.s_evac, 1)
        elif kind == "relu2":
            eng.scalar_tensor_tensor(out=th, in0=cur, scalar=0.0, in1=cur, op0=ALU.max,
                                     op1=ALU.mult).then_inc(self.s_evac, 1)
        elif kind == "val":
            eng.tensor_tensor(th, cur, pair(ph.src, v), ALU.mult).then_inc(self.s_evac, 1)
        elif kind == "bias":
            for t in range(2):
                ins = eng.tensor_scalar(tile(ph.out, v * 2 + (ph.t0 + t)), cur[:, t, :],
                                        self.par(ph.g, v * 2 + (ph.g0 + t)), None, ALU.add)
            ins.then_inc(self.s_evac, 1)

    def pool(self, eng, phs):
        for ph in phs:
            if ph.k.pool:
                def step(v, j, ph=ph):
                    self.pool_finish(eng, ph, v, (ph.base["u"] + j) % 2)
                self.loop(eng, ph, step)

    def pool_finish(self, eng, ph, v, s):
        b = ph.base
        eng.wait_ge(self.s_fin, v + (b["fin"] + 1))
        if ph.kind in ("resid", "emit", "sumsq"):
            if isinstance(v, int) and v == 0:
                at_least(eng, self.s_sum, b["norm"])
                ins = eng.tensor_copy(self.sq[:], self.tq[:])
            else:
                at_least(eng, self.s_pool, v + b["pool"])
                ins = eng.tensor_tensor(self.sq[:], self.sq[:], self.tq[:], ALU.add)
            if ph.kind == "sumsq":
                ins.then_inc(self.s_pool, 1)
                return
        out = pair(ph.out, v, ph.t0)
        eng.tensor_tensor(out[:, :, 1, :], self.th[:, s], out[:, :, 0, :].bitcast(F32),
                          ALU.subtract).then_inc(self.s_pool, 1)

    def pe(self, eng, phs, aside=None):
        for ph in phs:
            def step(v, j, ph=ph):
                self.unit(eng, ph, v, j)
                if isinstance(v, int) and v == 0 and ph.sum_after:
                    self.sum_squares(eng, ph)
                if isinstance(v, int) and v == 0 and aside and ph is phs[-1]:
                    aside(eng)
            self.loop(eng, ph, step)

    def unit(self, eng, ph, v, j):
        b = ph.base
        s = (b["u"] + j) % 2
        at_least(eng, self.s_free, v + (b["u"] - 1))
        for k in range(ph.nc):
            n = j * ph.nc + k
            slot = (b["c"] + n) % RING
            eng.wait_ge(self.s_lo, (v - j) * ph.nc + (b["c"] + n + 1))
            if isinstance(v, int) and v == 0 and ph.after:
                eng.wait_ge(self.s_pool, ph.after.base["pool"] + 2 * (k + 1))
            for t in range(2):
                bank = self.acc[:, 2 * s + t, :]
                for q in range(CK):
                    kt = CK * k + q
                    first, final = kt == 0, kt == CK * ph.nc - 1
                    a = ph.act[:, kt]
                    if ph.kind == "tok":
                        cols = slice(q * UNIT, (q + 1) * UNIT)
                        toks = slice(t * P, (t + 1) * P)
                        eng.matmul(bank[:, 0:UNIT], a[:, 0, toks], self.hi[:, slot, cols], start=first, stop=False)
                        eng.matmul(bank[:, 0:UNIT], a[:, 1, toks], self.hi[:, slot, cols], start=False, stop=False)
                        ins = eng.matmul(bank[:, 0:UNIT], a[:, 0, toks], self.lo[:, slot, cols],
                                         start=False, stop=final)
                    else:
                        cols = slice(q * UNIT + t * P, q * UNIT + (t + 1) * P)
                        eng.matmul(bank, self.hi[:, slot, cols], a.rearrange("p h n -> p (h n)"),
                                   start=first, stop=False)
                        ins = eng.matmul(bank[:, 0:T], self.lo[:, slot, cols], a[:, 0, :],
                                         start=False, stop=final)
            ins.then_inc(self.s_used, 1)

    def sum_squares(self, eng, ph):
        eng.wait_ge(self.s_pool, ph.base["pool"])
        at_least(eng, self.s_root, ph.norm - 1)
        for t in range(2):
            ins = eng.matmul(self.work[:, 3, 0:T], self.const("ones"), self.sq[:, t, :],
                             start=t == 0, stop=t == 1)
        ins.then_inc(self.s_sum, 1)


def semaphores(nc, stack):
    taken = []

    def release():
        nc.clear_and_free_semaphores(taken)
        nc.all_engine_barrier()
    stack.callback(release)

    def sem(name):
        taken.append(nc.alloc_semaphore(name=name))
        return taken[-1]
    return sem


class Link:

    def __init__(self, eng, s):
        self.eng, self.s, self.n = eng, s, 0

    def __call__(self, ins):
        self.n += 1
        ins.then_inc(self.s, 1)
        self.eng.wait_ge(self.s, self.n)


def over(ap, n):
    return ap.unsqueeze(1).to_broadcast([ap.shape[0], n, ap.shape[1]])


def spread(ap, n):
    return ap.unsqueeze(2).to_broadcast([ap.shape[0], ap.shape[1], n])


def rwkv_prepare(nc, dram, s, u, b):
    with ExitStack() as st:
        sem = semaphores(nc, st)
        w2 = alloc(nc, st, "w2", [P, 1024])
        a2 = alloc(nc, st, "a2", [P, 1024])
        f2 = alloc(nc, st, "f2", [P, 2 * RW, Q + 1])
        mid = alloc(nc, st, "mid", [P, 2 * RW])
        karg = alloc(nc, st, "karg", [P, RW])
        f1, kk, bb, kr, vt, bt, kt, sfac = (b[n] for n in ("f1", "kk", "bb", "kr", "vt", "bt", "kt", "sfac"))
        scr = kr[:].rearrange("p a b c q -> p (a b c q)")
        sa, sn = scr[:, 0:2048], scr[:, 2048:4096]
        vts = vt[:].rearrange("p c a -> p (c a)")
        r, k, v = (u[:, t:t + RW, :].rearrange("p a t -> p (a t)") for t in (R0, K0, V0))
        kkf, bbf = (t[:].rearrange("p a t -> p (a t)") for t in (kk, bb))
        chunks = lambda t: t.rearrange("p (a q) -> p a q", q=Q)
        bones = s.const("half_ones")
        lw, ls = sem("low_rank_loaded"), sem("vector_link_p")
        tw, dec, icl = sem("tanh_ready"), sem("decay_product"), sem("iclr_product")
        sg, ig = sem("decays_ready"), sem("iclr_ready")
        cs, ex, kraw, ksq = sem("sums_ready"), sem("exps_ready"), sem("kk_raw"), sem("kk_squared")
        nsum, nroot, nuse = sem("norm_sum"), sem("norm_root"), sem("kprime_inputs")
        bon, bsum, vtr, vcp, bvr = (sem(n) for n in ("bonus_terms", "bonus_sum", "v_turned",
                                                     "v_copied", "bonus_ready"))
        hat, tts, ttc, tmp = sem("hats_ready"), sem("hats_turned"), sem("hats_copied"), sem("scalar_link_p")
        slot = lambda psum, i: psum[:, i // 2, (i % 2) * T:(i % 2 + 1) * T]
        with nc.Block() as block:
            @block.sync
            def _(eng):
                eng.dma_start(w2[:], dram["w2"]).then_inc(lw, 16)
                eng.dma_start(a2[:], dram["a2"]).then_inc(lw, 16)

            @block.tensor
            def _(eng):
                eng.wait_ge(lw, 32)
                for j in range(RW):
                    ins = eng.matmul(slot(s.acc, j), a2[:, j * P:(j + 1) * P], u[:, PA0, :], start=True, stop=True)
                    ins.then_inc(icl, 1)
                eng.wait_ge(tw, 1)
                for j in range(RW):
                    ins = eng.matmul(slot(s.work, j), w2[:, j * P:(j + 1) * P], sn[:, 0:T], start=True, stop=True)
                    ins.then_inc(dec, 1)
                eng.wait_ge(ksq, 1)
                eng.wait_ge(sg, 1)
                for q in range(4):
                    ins = eng.matmul(s.work[:, q, :], bones, sa[:, 512 * q:512 * q + 512], start=True, stop=True)
                ins.then_inc(nsum, 1)
                eng.wait_ge(bon, 1)
                eng.wait_ge(ig, 1)
                for q in range(4):
                    ins = eng.matmul(s.acc[:, q, :], bones, sa[:, 512 * q:512 * q + 512], start=True, stop=True)
                ins.then_inc(bsum, 1)
                eng.wait_ge(nroot, 1)
                for c in range(NCH):
                    for j in range(RW):
                        ins = eng.transpose(s.work[:, 2 * c + j // 4, (j % 4) * P:(j % 4 + 1) * P],
                                            u[:, V0 + j, c * Q:(c + 1) * Q], s.const("ident"))
                ins.then_inc(vtr, 1)
                eng.wait_ge(hat, 1)
                eng.wait_ge(bvr, 1)
                for i, src in enumerate((bb, u[:, K0:K0 + RW, :])):
                    for j in range(RW):
                        ins = eng.transpose(s.acc[:, 2 * i + j // 4, (j % 4) * P:(j % 4 + 1) * P],
                                            src[:, j, 0:Q], s.const("ident"))
                ins.then_inc(tts, 1)

            @block.scalar
            def _(eng):
                eng.activation(sn[:, 0:T], u[:, PW0, :], ACT.Tanh).then_inc(tw, 1)
                for j in range(RW):
                    eng.wait_ge(icl, 2 * (j // 2) + 2)
                    ins = eng.activation(bb[:, j, :], slot(s.acc, j), ACT.Sigmoid, bias=s.par("a0", j))
                ins.then_inc(ig, 1)
                for j in range(RW):
                    eng.wait_ge(dec, 2 * (j // 2) + 2)
                    ins = eng.activation(kk[:, j, :], slot(s.work, j), ACT.Sigmoid, bias=s.par("w0", j))
                ins.then_inc(sg, 1)
                eng.activation(u[:, PG0:PG0 + 2, :], u[:, PG0:PG0 + 2, :], ACT.Sigmoid)
                eng.wait_ge(cs, 1)
                eng.activation(f2[:], f1[:], ACT.Exp, scale=E_HALF).then_inc(tmp, 1)
                eng.wait_ge(tmp, 1)
                eng.activation(f1[:], f1[:], ACT.Exp, scale=-E_HALF)
                eng.activation(sfac[:], karg[:], ACT.Exp, scale=-E_HALF).then_inc(ex, 1)
                eng.wait_ge(kraw, 1)
                eng.activation(sa, kkf, ACT.Square).then_inc(ksq, 1)
                eng.wait_ge(nsum, 1)
                eng.activation(sn, s.work[:].rearrange("p a b -> p (a b)"), ACT.Sqrt).then_inc(nroot, 1)
                eng.wait_ge(vtr, 1)
                eng.wait_ge(bon, 1)
                eng.activation(vt[:].rearrange("p c a -> p (c a)"), s.work[:].rearrange("p a b -> p (a b)"),
                               ACT.Copy).then_inc(vcp, 1)
                eng.wait_ge(tts, 1)
                eng.activation(bt[:], s.acc[:, 0:2, :].rearrange("p a b -> p (a b)"), ACT.Copy)
                eng.activation(kt[:], s.acc[:, 2:4, :].rearrange("p a b -> p (a b)"), ACT.Copy)

            @block.vector
            def _(eng):
                link = Link(eng, ls)
                eng.memset(f1[:, :, 0:1], 0.0)
                eng.wait_ge(sg, 1)
                for i in range(2 * RW):
                    ins = eng.tensor_tensor_scan(f1[:, i, 1:Q + 1], s.const("ones"), kk[:, i // 2, (i % 2) * Q:(i % 2 + 1) * Q],
                                                 0.0, ALU.mult, ALU.add)
                link(ins)
                f4 = f1[:].rearrange("p (j c) q -> p j c q", c=2)
                eng.tensor_tensor(karg[:], f4[:, :, 0, Q], f4[:, :, 0, Q // 2], ALU.subtract)
                link(eng.tensor_copy(mid[:], f1[:, :, Q // 2]))
                eng.tensor_tensor(f1[:], f1[:], spread(mid[:], Q + 1), ALU.subtract)
                eng.tensor_tensor(karg[:], karg[:], mid[:].rearrange("p (j c) -> p j c", c=2)[:, :, 1],
                                  ALU.add).then_inc(cs, 1)
                for j in range(RW):
                    ins = eng.tensor_scalar(kk[:, j, :], u[:, K0 + j, :], s.par("k_k", j), None, ALU.mult)
                ins.then_inc(kraw, 1)
                eng.wait_ge(kraw, 1)
                eng.wait_ge(ig, 1)
                for j in range(RW):
                    ins = eng.tensor_scalar(vts[:, j * T:(j + 1) * T], bb[:, j, :], -1.0, s.par("k_a", j),
                                            ALU.add, ALU.mult)
                link(ins)
                link(eng.scalar_tensor_tensor(out=k, in0=vts, scalar=1.0, in1=k, op0=ALU.add, op1=ALU.mult))
                eng.wait_ge(nroot, 1)
                link(eng.tensor_scalar(sn, sn, 1e-12, None, ALU.max))
                link(eng.reciprocal(sn, sn))
                link(eng.tensor_tensor(kkf, kkf, sn, ALU.mult))
                eng.tensor_tensor(bbf, kkf, bbf, ALU.mult)
                for j in range(RW):
                    ins = eng.scalar_tensor_tensor(out=scr[:, j * T:(j + 1) * T], in0=u[:, R0 + j, :],
                                                   scalar=s.par("r_k", j), in1=u[:, K0 + j, :],
                                                   op0=ALU.mult, op1=ALU.mult)
                ins.then_inc(bon, 1)
                eng.wait_ge(bon, 1)
                eng.wait_ge(ex, 1)
                eng.tensor_tensor(chunks(bbf), chunks(bbf), f2[:, :, 1:Q + 1], ALU.mult)
                eng.tensor_tensor(chunks(k), chunks(k), f2[:, :, 1:Q + 1], ALU.mult).then_inc(hat, 1)
                eng.wait_ge(bsum, 1)
                eng.wait_ge(vtr, 1)
                eng.tensor_tensor(v, v, s.acc[:].rearrange("p a b -> p (a b)"), ALU.mult).then_inc(bvr, 1)


def rwkv_chunks(nc, s, u, b):
    with ExitStack() as st:
        sem = semaphores(nc, st)
        ab = alloc(nc, st, "ab", [P, 2, 4, 2, Q])
        cr = alloc(nc, st, "cr", [P, 2, 4, 2, Q])
        xm, zm, pm, lt = (alloc(nc, st, n, [P, 2, 4, Q]) for n in ("xm", "zm", "pm", "lt"))
        rh, us = (alloc(nc, st, n, [P, 2, 256]) for n in ("rh", "us"))
        sp = alloc(nc, st, "sp", [P, RW, 64])
        f1, kk, bb, kr, vt, bt, kt, sfac = (b[n] for n in ("f1", "kk", "bb", "kr", "vt", "bt", "kt", "sfac"))
        banks = (s.work, s.acc)
        (zr, krb, sc, mk, tr, xz, zz, ltr, pr, pc, qr, rr, rc, ur, uc, yr, yc, sr, sw, lk, plk) = (sem(n) for n in (
            "kr_zeroed", "kr_built", "scored", "masked", "a_turned", "x_ready", "z_started", "l_ready",
            "lx_ready", "lx_copied", "xlx_ready", "rhs_ready", "rhs_copied", "u_ready", "u_copied", "y_ready",
            "y_copied", "state_sum", "state_ready", "vector_link_c", "pool_link_c"))
        pairs = [(m, gi) for m in range(4) for gi in range(2)]
        tops = lambda name: over(s.const(name), 4)
        with nc.Block() as block:
            @block.gpsimd
            def _(eng):
                link = Link(eng, plk)
                eng.memset(kr[:], 0.0).then_inc(zr, 1)
                for m in range(4):
                    for gi in range(2):
                        it = 2 * m + gi
                        eng.wait_ge(mk, 2 * it + 1)
                        at_least(eng, ur, it - 1)
                        link(eng.tensor_tensor(zm[:, gi], ab[:, gi, :, 0, :], tops("lev0"), ALU.mult))
                        eng.tensor_tensor(zm[:, gi], tops("ident"), zm[:, gi], ALU.subtract).then_inc(zz, 1)
                    for q in range(1, LEVELS):
                        for gi in range(2):
                            at_least(eng, pr, (LEVELS - 1) * 2 * m + 2 * (q - 2) + gi + 1 if q > 1 else
                                     (LEVELS - 1) * 2 * (m - 1) + 2 * (LEVELS - 2) + gi + 1)
                            eng.tensor_tensor(lt[:, gi], ab[:, gi, :, 0, :], tops(f"lev{q}"),
                                              ALU.mult).then_inc(ltr, 1)

            @block.vector
            def _(eng):
                link = Link(eng, lk)
                f4 = f1[:].rearrange("p (j c) q -> p j c q", c=2)

                def build(c):
                    if c == 0:
                        eng.wait_ge(zr, 1)
                    else:
                        eng.wait_ge(sc, 4)
                    toks = slice(c * Q, (c + 1) * Q)
                    for h in range(2):
                        p = slice(64 * h, 64 * h + 64)
                        eng.tensor_tensor(kr[p, :, h, 0, :], kk[p, :, toks], f4[p, :, c, 0:Q], ALU.mult)
                        ins = eng.tensor_tensor(kr[p, :, h, 1, :], u[p, R0:R0 + RW, toks], f4[p, :, c, 1:Q + 1],
                                                ALU.mult)
                    ins.then_inc(krb, 1)

                for m in range(4):
                    if m % 2 == 0:
                        build(m // 2)
                    for gi in range(2):
                        it = 2 * m + gi
                        bk = banks[gi]
                        eng.wait_ge(sc, it + 1)
                        at_least(eng, yr, it - 1)
                        mask = over(s.consts[:, CONST_COLS["upper"]:CONST_COLS["upper"] + 2 * Q], 4)
                        for n, dst in ((0, ab), (2, cr)):
                            eng.tensor_tensor(dst[:, gi].rearrange("p h a q -> p h (a q)"),
                                              bk[:, n:n + 2, :].rearrange("p a (h q) -> p (a h) q", h=2),
                                              mask, ALU.mult).then_inc(mk, 1)
                        eng.wait_ge(tr, it + 1)
                        at_least(eng, qr, (LEVELS - 1) * 2 * m)
                        link(eng.scalar_tensor_tensor(out=xm[:, gi], in0=bk[:, 0, :].rearrange("p (h q) -> p h q", h=4),
                                                      scalar=-1.0, in1=tops("top_left"),
                                                      op0=ALU.mult, op1=ALU.mult))
                        eng.tensor_tensor(xm[:, gi], xm[:, gi], tops("ident"), ALU.add).then_inc(xz, 1)
                    for q in range(1, LEVELS):
                        for gi in range(2):
                            bk = banks[gi]
                            eng.wait_ge(qr, (LEVELS - 1) * 2 * m + 2 * (q - 1) + gi + 1)
                            eng.wait_ge(xz, LEVELS * 2 * m + 2 * (q - 1) + gi + 1)
                            if q == 1:
                                eng.wait_ge(zz, 2 * m + gi + 1)
                            if q < LEVELS - 1:
                                eng.tensor_tensor(xm[:, gi], xm[:, gi], bk[:, 2, :].rearrange("p (h q) -> p h q", h=4),
                                                  ALU.subtract)
                            eng.tensor_tensor(zm[:, gi], zm[:, gi], bk[:, 3, :].rearrange("p (h q) -> p h q", h=4),
                                              ALU.subtract).then_inc(xz, 1)
                    if m < 2:
                        for gi in range(2):
                            it = 2 * m + gi
                            eng.wait_ge(sr, it + 1)
                            for t in range(2):
                                j = 2 * (it % 4) + t
                                ins = eng.tensor_scalar(sp[:, j, :], banks[gi][:, 2, 64 * t:64 * t + 64],
                                                        sfac[:, j:j + 1], None, ALU.mult)
                            ins.then_inc(sw, 1)

            @block.scalar
            def _(eng):
                for m in range(4):
                    for q in range(1, LEVELS):
                        for gi in range(2):
                            n = (LEVELS - 1) * 2 * m + 2 * (q - 1) + gi
                            eng.wait_ge(pr, n + 1)
                            at_least(eng, qr, n - 1)
                            eng.activation(pm[:, gi], banks[gi][:, 1, :].rearrange("p (h q) -> p h q", h=4),
                                           ACT.Copy).then_inc(pc, 1)
                        if q == 1:
                            for gi in range(2):
                                it = 2 * m + gi
                                eng.wait_ge(rr, it + 1)
                                at_least(eng, ur, it - 1)
                                eng.activation(rh[:, gi], banks[gi][:, 0, 0:256], ACT.Copy,
                                               scale=-1.0).then_inc(rc, 1)
                    for gi in range(2):
                        it = 2 * m + gi
                        eng.wait_ge(ur, it + 1)
                        at_least(eng, yr, it - 1)
                        eng.activation(us[:, gi], banks[gi][:, 0, 256:512], ACT.Copy).then_inc(uc, 1)
                    for gi in range(2):
                        it = 2 * m + gi
                        c, g = it // 4, it % 4
                        eng.wait_ge(yr, it + 1)
                        if c == 0:
                            eng.wait_ge(krb, 1)
                        else:
                            eng.wait_ge(krb, 2)
                        eng.activation(u[:, R0 + 2 * g:R0 + 2 * g + 2, c * Q:(c + 1) * Q],
                                       banks[gi][:, 1, 0:256].rearrange("p (a q) -> p a q", a=2),
                                       ACT.Copy).then_inc(yc, 1)

            @block.tensor
            def _(eng):
                for m in range(4):
                    c = m // 2
                    eng.wait_ge(krb, c + 1)
                    heads = lambda gi: [(2 * (2 * m % 4 + gi) + h // 2, h % 2, h) for h in range(4)]
                    for gi in range(2):
                        it = 2 * m + gi
                        bk = banks[gi]
                        at_least(eng, yc, it - 1)
                        at_least(eng, sw, min(it - 1, 4))
                        for t in range(2):
                            j = 2 * (it % 4) + t
                            rhs = kr[:, j].rearrange("p h a q -> p (h a q)")
                            toks = slice(c * Q, (c + 1) * Q)
                            eng.matmul(bk[:, t, :], bb[:, j, toks], rhs, start=True, stop=True)
                            ins = eng.matmul(bk[:, 2 + t, :], u[:, K0 + j, toks], rhs, start=True, stop=True)
                        ins.then_inc(sc, 1)
                    for gi in range(2):
                        it = 2 * m + gi
                        eng.wait_ge(mk, 2 * it + 1)
                        for h in range(4):
                            ins = eng.transpose(banks[gi][:, 0, h * Q:(h + 1) * Q], ab[:, gi, h, 0, :], s.const("ident"))
                        ins.then_inc(tr, 1)
                    for q in range(1, LEVELS):
                        for gi in range(2):
                            it, n = 2 * m + gi, (LEVELS - 1) * 2 * m + 2 * (q - 1) + gi
                            bk = banks[gi]
                            eng.wait_ge(ltr, n + 1)
                            eng.wait_ge(xz, LEVELS * 2 * m + 2 * (q - 1) + gi + 1)
                            if q == 1:
                                eng.wait_ge(mk, 2 * it + 2)
                            for h in range(4):
                                ins = eng.matmul(bk[:, 1, h * Q:(h + 1) * Q], lt[:, gi, h, :], xm[:, gi, h, :],
                                                 start=True, stop=True)
                            ins.then_inc(pr, 1)
                        if q == 1:
                            for gi in range(2):
                                it = 2 * m + gi
                                for j, hh, h in heads(gi):
                                    out = banks[gi][:, 0, 64 * h:64 * h + 64]
                                    if c == 1:
                                        if h == 0:
                                            eng.wait_ge(sw, it - 3)
                                        eng.matmul(out, kr[:, j, hh, 0, :], sp[:, j, :], start=True, stop=False)
                                    hd = 2 * j + hh
                                    ins = eng.matmul(out, cr[:, gi, h, 0, :], vt[:, c, 64 * hd:64 * hd + 64],
                                                     start=c == 0, stop=True)
                                ins.then_inc(rr, 1)
                        for gi in range(2):
                            n = (LEVELS - 1) * 2 * m + 2 * (q - 1) + gi
                            bk = banks[gi]
                            eng.wait_ge(pc, n + 1)
                            if q == 1:
                                eng.wait_ge(zz, 2 * m + gi + 1)
                            for h in range(4):
                                if q < LEVELS - 1:
                                    eng.matmul(bk[:, 2, h * Q:(h + 1) * Q], zm[:, gi, h, :], pm[:, gi, h, :],
                                               start=True, stop=True)
                                ins = eng.matmul(bk[:, 3, h * Q:(h + 1) * Q], pm[:, gi, h, :], zm[:, gi, h, :],
                                                 start=True, stop=True)
                            ins.then_inc(qr, 1)
                    for gi in range(2):
                        it = 2 * m + gi
                        eng.wait_ge(rc, it + 1)
                        eng.wait_ge(xz, LEVELS * 2 * m + 2 * (LEVELS - 1) + gi + 1)
                        for h in range(4):
                            ins = eng.matmul(banks[gi][:, 0, 256 + 64 * h:320 + 64 * h], zm[:, gi, h, :],
                                             rh[:, gi, 64 * h:64 * h + 64], start=True, stop=True)
                        ins.then_inc(ur, 1)
                    for gi in range(2):
                        it = 2 * m + gi
                        eng.wait_ge(uc, it + 1)
                        for j, hh, h in heads(gi):
                            hd = 2 * j + hh
                            out = banks[gi][64 * hh:64 * hh + 64, 1, (h // 2) * Q:(h // 2 + 1) * Q]
                            if c == 1:
                                eng.matmul(out, sp[:, j, :], kr[:, j, hh, 1, :], start=True, stop=False)
                            eng.matmul(out, us[:, gi, 64 * h:64 * h + 64], ab[:, gi, h, 1, :], start=c == 0, stop=False)
                            ins = eng.matmul(out, vt[:, c, 64 * hd:64 * hd + 64], cr[:, gi, h, 1, :],
                                             start=False, stop=True)
                        ins.then_inc(yr, 1)
                        if c == 0:
                            for j, hh, h in heads(gi):
                                hd = 2 * j + hh
                                out = banks[gi][64 * hh:64 * hh + 64, 2, 64 * (h // 2):64 * (h // 2) + 64]
                                cols = slice(64 * hd, 64 * hd + 64)
                                eng.matmul(out, bt[:, cols], us[:, gi, 64 * h:64 * h + 64], start=True, stop=False)
                                ins = eng.matmul(out, kt[:, cols], vt[:, 0, cols], start=False, stop=True)
                            ins.then_inc(sr, 1)


def rwkv_output(nc, dram, s, u, b):
    with ExitStack() as st:
        sem = semaphores(nc, st)
        g2 = alloc(nc, st, "g2", [P, 2, 1024])
        yv = alloc(nc, st, "yv", [P, RW, T])
        kk, bb = b["kk"], b["bb"]
        flat = lambda t: t.rearrange("p a t -> p (a t)")
        y, bonus = u[:, R0:R0 + RW, :], u[:, V0:V0 + RW, :]
        bones = s.const("half_ones")
        ld, ms, md, sq, vs, ro, gs, fin, hi, lk = (sem(n) for n in (
            "gate_weight_loaded", "mean_sums", "centred", "centred_squared", "variance_sums",
            "deviation_ready", "gate_product", "mixed", "mixed_high", "vector_link_o"))
        slot = lambda i: s.work[:, i // 2, (i % 2) * T:(i % 2 + 1) * T]
        with nc.Block() as block:
            @block.sync
            def _(eng):
                eng.dma_start(g2[:], dram["g2"]).then_inc(ld, 16)

            @block.tensor
            def _(eng):
                for q in range(4):
                    eng.matmul(s.work[:, q, :], bones, flat(y)[:, 512 * q:512 * q + 512],
                               start=True, stop=True).then_inc(ms, 1)
                for q in range(4):
                    eng.wait_ge(sq, q + 1)
                    eng.matmul(s.acc[:, q, :], bones, flat(kk[:])[:, 512 * q:512 * q + 512],
                               start=True, stop=True).then_inc(vs, 1)
                eng.wait_ge(ld, 16)
                for j in range(RW):
                    for q in range(2):
                        ins = eng.matmul(slot(j), g2[:, q, j * P:(j + 1) * P], u[:, PG0 + q, :],
                                         start=q == 0, stop=q == 1)
                ins.then_inc(gs, 1)

            @block.scalar
            def _(eng):
                for q in range(4):
                    cols = slice(512 * q, 512 * q + 512)
                    eng.wait_ge(md, q + 1)
                    eng.activation(flat(kk[:])[:, cols], flat(yv[:])[:, cols], ACT.Square).then_inc(sq, 1)
                for q in range(4):
                    cols = slice(512 * q, 512 * q + 512)
                    eng.wait_ge(vs, q + 1)
                    eng.activation(flat(bb[:])[:, cols], s.acc[:, q, :], ACT.Sqrt, scale=1.0 / 64,
                                   bias=s.eps[:, 1:2]).then_inc(ro, 1)
                for h in range(2):
                    eng.wait_ge(fin, h + 1)
                    eng.activation(s.a0[:, RW + 4 * h:RW + 4 * h + 4, 0, :], yv[:, 4 * h:4 * h + 4, :],
                                   ACT.Copy).then_inc(hi, 1)

            @block.vector
            def _(eng):
                link = Link(eng, lk)
                for q in range(4):
                    cols = slice(512 * q, 512 * q + 512)
                    eng.wait_ge(ms, q + 1)
                    eng.scalar_tensor_tensor(out=flat(yv[:])[:, cols], in0=s.work[:, q, :], scalar=-1.0 / 64,
                                             in1=flat(y)[:, cols], op0=ALU.mult, op1=ALU.add).then_inc(md, 1)
                for h in range(2):
                    cols = slice(1024 * h, 1024 * h + 1024)
                    eng.wait_ge(ro, 2 * h + 2)
                    link(eng.reciprocal(flat(bb[:])[:, cols], flat(bb[:])[:, cols]))
                    link(eng.tensor_tensor(flat(yv[:])[:, cols], flat(yv[:])[:, cols], flat(bb[:])[:, cols], ALU.mult))
                    for j in range(4 * h, 4 * h + 4):
                        ins = eng.tensor_scalar(yv[:, j, :], yv[:, j, :], s.par("ln_w", j), s.par("ln_b", j),
                                                ALU.mult, ALU.add)
                    link(ins)
                    link(eng.tensor_tensor(flat(yv[:])[:, cols], flat(yv[:])[:, cols], flat(bonus)[:, cols], ALU.add))
                    eng.wait_ge(gs, 1)
                    eng.tensor_tensor(flat(yv[:])[:, cols], flat(yv[:])[:, cols],
                                      s.work[:, 2 * h:2 * h + 2, :].rearrange("p a b -> p (a b)"),
                                      ALU.mult).then_inc(fin, 1)
                for h in range(2):
                    eng.wait_ge(hi, h + 1)
                    eng.tensor_tensor(s.a0[:, RW + 4 * h:RW + 4 * h + 4, 1, :], yv[:, 4 * h:4 * h + 4, :],
                                      s.a0[:, RW + 4 * h:RW + 4 * h + 4, 0, :].bitcast(F32), ALU.subtract)


def rwkv(nc, dram, s, u):
    with ExitStack() as st:
        b = {n: alloc(nc, st, n, shape) for n, shape in (
            ("f1", [P, 2 * RW, Q + 1]), ("kk", [P, RW, T]), ("bb", [P, RW, T]),
            ("kr", [P, RW, 2, 2, Q]), ("vt", [P, NCH, 1024]), ("bt", [P, 1024]), ("kt", [P, 1024]),
            ("sfac", [P, RW]))}
        rwkv_prepare(nc, dram, s, u, b)
        rwkv_chunks(nc, s, u, b)
        rwkv_output(nc, dram, s, u, b)


def ssd(nc, s, u):
    with ExitStack() as st:
        sem = semaphores(nc, st)
        dtt, da, ax, ex, rz, z2, pl = (alloc(nc, st, n, [P, NCH, NH]) for n in (
            "dtt", "da", "ax", "ex", "rz", "z2", "pl"))
        ea = alloc(nc, st, "ea", [P, NH])
        dec = alloc(nc, st, "dec", [P, NH])
        xdt = alloc(nc, st, "xdt", [P, NCH, 1024])
        xdd = alloc(nc, st, "xdd", [P, 1024])
        btok = alloc(nc, st, "btok", [P, 2, P])
        stt = alloc(nc, st, "stt", [P, 1024])
        cbm = alloc(nc, st, "cbm", [P, 2, NCH, P])
        dm, el, ec, mm, cx = (alloc(nc, st, n, [P, 2, 4, P]) for n in ("dm", "el", "ec", "mm", "cx"))
        ys = alloc(nc, st, "ys", [P, RW, T])
        sqy = alloc(nc, st, "sqy", [P, RW, T])
        inv = alloc(nc, st, "inv", [P, 2, T])
        banks = (s.work, s.acc)
        (dtr, lk, axr, exr, ear, dar, decs, decr, xtr, xdr, bcr, bck, str_, stc, dmr, sgr, ecr, elr, mmr, cxr,
         yr, yd, sqr, smr, inr, outr, hir, pk) = (sem(n) for n in (
            "dt_turned", "vector_link_s", "dt_abs", "dt_exp", "a_exp", "da_ready", "end_sums", "end_decays",
            "x_turned", "xdt_ready", "bc_products", "b_copied", "states_summed", "states_copied",
            "da_masked", "segments_ready", "starts_exp", "segments_exp", "m_ready", "c_scaled",
            "y_summed", "y_read", "y_squared", "y_norm_sums", "y_norm_root", "ssd_mixed", "ssd_high",
            "pool_link_s"))
        flat = lambda t: t.rearrange("p a t -> p (a t)")
        def ssd_y(eng, it):
            c, q, gi = it // 4, it % 4, it % 2
            bk = banks[gi]
            eng.wait_ge(mmr, it + 1)
            at_least(eng, yd, it - 1)
            if c == 1:
                eng.wait_ge(cxr, it - 3)
            for h in range(4):
                hd = 4 * q + h
                out = bk[64 * (h % 2):64 * (h % 2) + 64, 2, (h // 2) * P:(h // 2 + 1) * P]
                ins = eng.matmul(out, xdt[:, c, 64 * hd:64 * hd + 64], mm[:, gi, h, :], start=True, stop=c == 0)
                if c == 1:
                    ins = eng.matmul(out, stt[:, 64 * hd:64 * hd + 64], cx[:, gi, h, :], start=False, stop=True)
            ins.then_inc(yr, 1)

        def ssd_y_last(eng):
            ssd_y(eng, 7)
            for g in range(2):
                eng.wait_ge(sqr, g + 1)
                if g == 0:
                    eng.wait_ge(yd, 8)
                for j in range(4):
                    ins = eng.matmul(s.work[:, 3 * g, 0:T], s.const("ones"), sqy[:, 4 * g + j, :],
                                     start=j == 0, stop=j == 3)
                ins.then_inc(smr, 1)

        with nc.Block() as block:
            @block.tensor
            def _(eng):
                ident = s.const("ident")
                for c in range(NCH):
                    ins = eng.transpose(s.work[:, 0, c * P:(c + 1) * P], u[:, PW0, c * Q:(c + 1) * Q], ident)
                ins.then_inc(dtr, 1)
                for g in range(2):
                    for c in range(NCH):
                        toks = slice(c * Q, (c + 1) * Q)
                        eng.matmul(s.work[:, 1, (2 * g + c) * P:(2 * g + c + 1) * P], u[:, B0 + g, toks],
                                   u[:, C0 + g, toks], start=True, stop=True)
                for g in range(2):
                    ins = eng.transpose(s.work[:, 2, g * P:(g + 1) * P], u[:, B0 + g, 0:Q], ident)
                ins.then_inc(bcr, 1)
                for c in range(NCH):
                    for j in range(RW):
                        ins = eng.transpose(s.acc[:, 2 * c + j // 4, (j % 4) * P:(j % 4 + 1) * P],
                                            u[:, XS0 + j, c * Q:(c + 1) * Q], ident)
                ins.then_inc(xtr, 1)
                eng.wait_ge(dar, 1)
                eng.matmul(s.work[:, 3, 0:NH], s.const("lower"), da[:, 0, :], start=True, stop=True).then_inc(decs, 1)
                eng.wait_ge(xdr, 2)
                eng.wait_ge(bck, 1)
                for g in range(2):
                    ins = eng.matmul(s.acc[:, g, :], btok[:, g, :], xdd[:, 512 * g:512 * g + 512], start=True, stop=True)
                ins.then_inc(str_, 1)
                for it in range(8):
                    c, q, gi = it // 4, it % 4, it % 2
                    bk = banks[gi]
                    if it == 0:
                        eng.wait_ge(bck, 2)
                        eng.wait_ge(decr, 1)
                    if it == 1:
                        eng.wait_ge(stc, 1)
                    eng.wait_ge(dmr, it + 1)
                    at_least(eng, elr, it - 1)
                    rhs = dm[:, gi].rearrange("p h q -> p (h q)")
                    if c == 1:
                        at_least(eng, ecr, it - 5)
                        eng.matmul(bk[:, 1, :], s.const("ones"), rhs, start=True, stop=True)
                    eng.matmul(bk[:, 0, :], s.const("lower"), rhs, start=True, stop=True).then_inc(sgr, 1)
                    if it >= 1:
                        ssd_y(eng, it - 1)
                ssd_y_last(eng)

            @block.scalar
            def _(eng):
                eng.activation(ea[:], s.par("a_log"), ACT.Exp).then_inc(ear, 1)
                eng.wait_ge(axr, 1)
                eng.activation(ex[:], ax[:], ACT.Exp, scale=-1.0).then_inc(exr, 1)
                eng.wait_ge(bcr, 1)
                eng.activation(flat(btok[:]), s.work[:, 2, 0:2 * P], ACT.Copy).then_inc(bck, 1)
                eng.wait_ge(decs, 1)
                eng.activation(dec[:], s.work[:, 3, 0:NH], ACT.Exp).then_inc(decr, 1)
                eng.wait_ge(str_, 1)
                eng.activation(stt[:], s.acc[:, 0:2, :].rearrange("p a b -> p (a b)"), ACT.Copy).then_inc(stc, 1)
                for it in range(8):
                    gi = it % 2
                    bk = banks[gi]
                    eng.wait_ge(sgr, it + 1)
                    at_least(eng, mmr, it - 1)
                    if it >= 4:
                        at_least(eng, cxr, it - 5)
                        eng.activation(ec[:, gi].rearrange("p h q -> p (h q)"), bk[:, 1, :], ACT.Exp).then_inc(ecr, 1)
                    eng.activation(el[:, gi].rearrange("p h q -> p (h q)"), bk[:, 0, :], ACT.Exp).then_inc(elr, 1)
                for g in range(2):
                    eng.wait_ge(outr, g + 1)
                    eng.activation(sqy[:, 4 * g:4 * g + 4, :], ys[:, 4 * g:4 * g + 4, :], ACT.Square).then_inc(sqr, 1)
                for g in range(2):
                    eng.wait_ge(smr, g + 1)
                    eng.activation(inv[:, g, :], s.work[:, 3 * g, 0:T], ACT.Sqrt, scale=1.0 / 512,
                                   bias=s.eps[:, 0:1]).then_inc(inr, 1)
                for g in range(2):
                    eng.wait_ge(outr, 3 + g)
                    eng.activation(s.a0[:, 4 * g:4 * g + 4, 0, :], ys[:, 4 * g:4 * g + 4, :], ACT.Copy).then_inc(hir, 1)

            @block.gpsimd
            def _(eng):
                for it in range(4, 8):
                    q, gi = it % 4, it % 2
                    eng.wait_ge(ecr, it - 3)
                    at_least(eng, yr, it - 1)
                    eng.tensor_tensor(cx[:, gi], ec[:, gi], over(u[:, C0 + q // 2, Q:2 * Q], 4),
                                      ALU.mult).then_inc(cxr, 1)

            @block.vector
            def _(eng):
                link = Link(eng, lk)
                eng.wait_ge(dtr, 1)
                raw = s.work[:, 0, 0:2 * P].rearrange("p (c n) -> p c n", c=NCH)[:, :, DT_ROW:DT_ROW + NH]
                link(eng.tensor_tensor(dtt[:], raw, over(s.par("dt_bias"), NCH), ALU.add))
                link(eng.scalar_tensor_tensor(out=ax[:], in0=dtt[:], scalar=-1.0, in1=dtt[:], op0=ALU.mult, op1=ALU.max))
                eng.tensor_scalar(dtt[:], dtt[:], 0.0, None, ALU.max).then_inc(axr, 1)
                eng.wait_ge(exr, 1)
                link(eng.tensor_scalar(rz[:], ex[:], 2.0, None, ALU.add))
                link(eng.reciprocal(rz[:], rz[:]))
                link(eng.tensor_tensor(rz[:], rz[:], ex[:], ALU.mult))
                link(eng.tensor_tensor(z2[:], rz[:], rz[:], ALU.mult))
                link(eng.tensor_scalar(pl[:], z2[:], 1.0 / 17, None, ALU.mult))
                for q in range(7, 0, -1):
                    link(eng.scalar_tensor_tensor(out=pl[:], in0=pl[:], scalar=1.0 / (2 * q + 1), in1=z2[:],
                                                  op0=ALU.add, op1=ALU.mult))
                link(eng.scalar_tensor_tensor(out=pl[:], in0=pl[:], scalar=1.0, in1=rz[:], op0=ALU.add, op1=ALU.mult))
                link(eng.scalar_tensor_tensor(out=dtt[:], in0=pl[:], scalar=2.0, in1=dtt[:], op0=ALU.mult, op1=ALU.add))
                eng.wait_ge(ear, 1)
                eng.scalar_tensor_tensor(out=da[:], in0=dtt[:], scalar=-1.0, in1=over(ea[:], NCH),
                                         op0=ALU.mult, op1=ALU.mult).then_inc(dar, 1)
                eng.wait_ge(xtr, 1)
                for c in range(NCH):
                    ins = eng.tensor_tensor(xdt[:, c, :].rearrange("p (h n) -> p h n", n=64),
                                            s.acc[:, 2 * c:2 * c + 2, :].rearrange("p a (h n) -> p (a h) n", n=64),
                                            spread(dtt[:, c, :], 64), ALU.mult)
                ins.then_inc(xdr, 1)
                eng.wait_ge(xdr, 1)
                eng.wait_ge(decr, 1)
                eng.tensor_tensor(xdd[:].rearrange("p (h n) -> p h n", n=64),
                                  xdt[:, 0, :].rearrange("p (h n) -> p h n", n=64), spread(dec[:], 64),
                                  ALU.mult).then_inc(xdr, 1)
                eng.wait_ge(bck, 1)
                eng.tensor_tensor(cbm[:].rearrange("p g c q -> p (g c) q"),
                                  s.work[:, 1, :].rearrange("p (g q) -> p g q", q=P), over(s.const("upper_in"), 4),
                                  ALU.mult).then_inc(bck, 1)

                def mask(it):
                    c, q, gi = it // 4, it % 4, it % 2
                    at_least(eng, sgr, it - 1)
                    eng.tensor_tensor(dm[:, gi], over(s.const("upper_in"), 4), spread(da[:, c, 4 * q:4 * q + 4], P),
                                      ALU.mult).then_inc(dmr, 1)

                eng.wait_ge(dar, 1)
                eng.wait_ge(bck, 2)
                mask(0)
                mask(1)
                for it in range(8):
                    c, q, gi = it // 4, it % 4, it % 2
                    eng.wait_ge(elr, it + 1)
                    at_least(eng, yr, it - 1)
                    eng.tensor_tensor(mm[:, gi], el[:, gi], over(cbm[:, q // 2, c, :], 4), ALU.mult).then_inc(mmr, 1)
                    if it + 2 < 8:
                        mask(it + 2)
                    eng.wait_ge(yr, it + 1)
                    for t in range(2):
                        j, toks = 2 * q + t, slice(c * Q, (c + 1) * Q)
                        ins = eng.scalar_tensor_tensor(out=ys[:, j, toks], in0=u[:, XS0 + j, toks],
                                                       scalar=s.par("ssd_d", j), in1=banks[gi][:, 2, t * P:(t + 1) * P],
                                                       op0=ALU.mult, op1=ALU.add)
                    ins.then_inc(yd, 1)
                eng.wait_ge(yd, 8)
                for g in range(2):
                    h = slice(4 * g, 4 * g + 4)
                    eng.tensor_tensor(ys[:, h, :], ys[:, h, :], u[:, Z0 + 4 * g:Z0 + 4 * g + 4, :],
                                      ALU.mult).then_inc(outr, 1)
                for g in range(2):
                    h = slice(4 * g, 4 * g + 4)
                    eng.wait_ge(inr, g + 1)
                    eng.wait_ge(sqr, g + 1)
                    link(eng.reciprocal(inv[:, g, :], inv[:, g, :]))
                    for j in range(4 * g, 4 * g + 4):
                        ins = eng.scalar_tensor_tensor(out=ys[:, j, :], in0=ys[:, j, :], scalar=s.par("ssd_g", j),
                                                       in1=inv[:, g, :], op0=ALU.mult, op1=ALU.mult)
                    ins.then_inc(outr, 1)
                for g in range(2):
                    h = slice(4 * g, 4 * g + 4)
                    eng.wait_ge(hir, g + 1)
                    eng.wait_ge(outr, 3 + g)
                    eng.tensor_tensor(s.a0[:, h, 1, :], ys[:, h, :], s.a0[:, h, 0, :].bitcast(F32), ALU.subtract)


class MemoryNorm:

    def __init__(self, dram, s, vx, kx, w_out, sem):
        self.dram, self.s, self.w_out = dram, s, w_out
        self.flat = vx[:].rearrange("p a n -> p (a n)")
        self.mem = self.flat.rearrange("p (a t) -> p a t", t=T)
        self.sq, self.root, self.rstd = kx, kx[:, 1, :], kx[:, 2, :]
        self.loaded, self.squared, self.summed, self.rooted, self.ready, self.link = (sem(n) for n in (
            "memory_loaded", "memory_squared", "memory_sum", "memory_root", "memory_rstd", "pool_link_m"))

    def sp(self, eng, q):
        n = KT * T // 4
        eng.dma_start(self.flat[:, q * n:(q + 1) * n], self.dram["mem"][:, q * n:(q + 1) * n]).then_inc(self.loaded, 16)

    def pe(self, eng):
        eng.wait_ge(self.squared, 1)
        eng.matmul(self.s.work[:, 0, 0:T], self.s.const("ones"), self.sq[:, 0, :], start=True,
                   stop=True).then_inc(self.summed, 1)

    def act(self, eng):
        eng.wait_ge(self.summed, 1)
        eng.activation(self.root, self.s.work[:, 0, 0:T], ACT.Sqrt, scale=1.0 / D,
                       bias=self.s.eps[:, 0:1]).then_inc(self.rooted, 1)

    def dve(self, eng):
        eng.wait_ge(self.rooted, 1)
        eng.reciprocal(self.rstd, self.root).then_inc(self.ready, 1)

    def pool_squares(self, eng):
        self.linked = Link(eng, self.link)
        eng.wait_ge(self.loaded, 64)
        self.linked(eng.tensor_tensor(self.sq[:], self.mem, self.mem, ALU.mult))
        for n in (8, 4, 2):
            self.linked(eng.tensor_tensor(self.sq[:, 0:n, :], self.sq[:, 0:n, :], self.sq[:, n:2 * n, :], ALU.add))
        eng.tensor_tensor(self.sq[:, 0, :], self.sq[:, 0, :], self.sq[:, 1, :], ALU.add).then_inc(self.squared, 1)

    def pool_parts(self, eng):
        s = self.s
        eng.wait_ge(self.ready, 1)
        self.linked(eng.tensor_tensor(self.mem, self.mem, over(self.rstd, KT), ALU.mult))
        for kt in range(KT):
            ins = eng.tensor_scalar(self.mem[:, kt, :], self.mem[:, kt, :], s.par("norm_mem_g", kt), None, ALU.mult)
        self.linked(ins)
        eng.wait_ge(s.s_used, self.w_out.base["c"] + self.w_out.units * self.w_out.nc)
        self.linked(eng.tensor_copy(s.a0[:, :, 0, :], self.mem))
        self.linked(eng.tensor_tensor(s.a0[:, :, 1, :], self.mem, s.a0[:, :, 0, :].bitcast(F32), ALU.subtract))


def cross_attention(nc, s, qx, kx, vx, pe_, pt, stats, a1, sem):
    scale = XD ** -0.5
    mx, sm = stats[:, 0:8], stats[:, 8:16]
    (scd, mxd, exd, nrd, trd, cpd, pvd, hid, lod, lk) = (sem(n) for n in (
        "scores", "maxima", "exps", "probs_normed", "probs_turned", "probs_copied", "outputs",
        "outputs_high", "outputs_low", "vector_link_x"))
    bank = lambda i: (s.work if i < 4 else s.acc)[:, i % 4, :]
    with nc.Block() as block:
        @block.tensor
        def _(eng):
            for i in range(8):
                h, t = i // 2, i % 2
                for d in range(4):
                    ins = eng.matmul(bank(i)[:, 0:T], qx[:, 4 * h + d, t * P:(t + 1) * P], kx[:, 4 * h + d, :],
                                     start=d == 0, stop=d == 3)
                ins.then_inc(scd, 1)
            for h in range(XH):
                eng.wait_ge(nrd, 2 * h + 2)
                for t in range(2):
                    for m in range(2):
                        ins = eng.transpose(bank(h)[:, (2 * m + t) * P:(2 * m + t + 1) * P],
                                            pe_[:, 2 * h + t, m * P:(m + 1) * P], s.const("ident"))
                ins.then_inc(trd, 1)
            for h in range(XH):
                eng.wait_ge(cpd, h + 1)
                for d in range(4):
                    b = bank(4 + (2 * h + d // 2) % 4)
                    if d % 2 == 0:
                        eng.wait_ge(exd, 8)
                        at_least(eng, lod, 2 * h + d // 2 - 3)
                    for m in range(2):
                        ins = eng.matmul(b[:, (d % 2) * T:(d % 2 + 1) * T],
                                         vx[:, m, XD * h + d * P:XD * h + (d + 1) * P], pt[:, h, m, :],
                                         start=m == 0, stop=m == 1)
                    if d % 2 == 1:
                        ins.then_inc(pvd, 1)

        @block.scalar
        def _(eng):
            for i in range(8):
                eng.wait_ge(mxd, i + 1)
                eng.activation(pe_[:, i, :], bank(i)[:, 0:T], ACT.Exp, bias=mx[:, i:i + 1], scale=scale,
                               accum_out=sm[:, i:i + 1]).then_inc(exd, 1)
            for h in range(XH):
                eng.wait_ge(trd, h + 1)
                eng.activation(pt[:, h].rearrange("p m q -> p (m q)"), bank(h), ACT.Copy).then_inc(cpd, 1)
            for n in range(8):
                eng.wait_ge(pvd, n + 1)
                eng.activation(a1[:, 2 * n:2 * n + 2, 0, :], bank(4 + n % 4).rearrange("p (a t) -> p a t", a=2),
                               ACT.Copy).then_inc(hid, 1)

        @block.vector
        def _(eng):
            link = Link(eng, lk)
            for i in range(8):
                eng.wait_ge(scd, i + 1)
                link(eng.tensor_reduce(mx[:, i:i + 1], bank(i)[:, 0:T], AX.X, ALU.max))
                eng.tensor_scalar(mx[:, i:i + 1], mx[:, i:i + 1], -scale, None, ALU.mult).then_inc(mxd, 1)
            for i in range(8):
                eng.wait_ge(exd, i + 1)
                link(eng.reciprocal(sm[:, i:i + 1], sm[:, i:i + 1]))
                eng.tensor_scalar(pe_[:, i, :], pe_[:, i, :], sm[:, i:i + 1], None, ALU.mult).then_inc(nrd, 1)
            for n in range(8):
                eng.wait_ge(hid, n + 1)
                eng.tensor_tensor(a1[:, 2 * n:2 * n + 2, 1, :], bank(4 + n % 4).rearrange("p (a t) -> p a t", a=2),
                                  a1[:, 2 * n:2 * n + 2, 0, :].bitcast(F32), ALU.subtract).then_inc(lod, 1)


def stream_block(nc, s, phs):
    with nc.Block() as block:
        @block.sync
        def _(eng):
            for ph in phs:
                s.sp(eng, ph)

        @block.scalar
        def _(eng):
            s.act(eng, phs)

        @block.vector
        def _(eng):
            s.dve(eng, phs)

        @block.gpsimd
        def _(eng):
            s.pool(eng, phs)

        @block.tensor
        def _(eng):
            s.pe(eng, phs)


def attention_and_mlp(nc, dram, s):
    with ExitStack() as st:
        a1 = alloc(nc, st, "a1", [P, KT, 2, T], F32R)
        with ExitStack() as qkv:
            qx, kx = (alloc(nc, qkv, n, [P, KT, T]) for n in ("qx", "kx"))
            vx = alloc(nc, qkv, "vx", [P, 2, D])
            with ExitStack() as rg:
                s.ring(rg, "_x")
                with nc.Block() as block:
                    @block.vector
                    def _(eng):
                        eng.memset(s.tb[:], 0.0)
                w_out = s.phase("w_out", "w_out", 8, 4, 2, s.a0, "resid", out=a1, g="norm_x_g")
                q = s.phase("wq", "wq", 8, 4, 2, a1, "scaled", out=qx, after=w_out, sum_after=True)
                memory = MemoryNorm(dram, s, vx, kx, w_out, semaphores(nc, rg))
                with nc.Block() as block:
                    @block.sync
                    def _(eng):
                        for c in range(2 * w_out.nc):
                            s.load(eng, w_out, c, c)
                            if c >= RING:
                                memory.sp(eng, c - RING)
                        s.sp(eng, w_out, skip=2 * w_out.nc)
                        s.sp(eng, q)

                    @block.scalar
                    def _(eng):
                        s.act(eng, [w_out, q], aside=memory.act)

                    @block.vector
                    def _(eng):
                        s.dve(eng, [w_out, q], aside=memory.dve)

                    @block.gpsimd
                    def _(eng):
                        memory.pool_squares(eng)
                        s.pool(eng, [w_out, q])
                        memory.pool_parts(eng)

                    @block.tensor
                    def _(eng):
                        s.pe(eng, [w_out, q], aside=memory.pe)
                k = s.phase("wk", "wk", 8, 4, 2, s.a0, "plain", out=kx)
                v = s.phase("wv", "wv", 8, 4, 2, s.a0, "tok", out=vx)
                stream_block(nc, s, [k, v])
            with ExitStack() as xs:
                pe_ = alloc(nc, xs, "probs", [P, 8, T])
                pt = alloc(nc, xs, "probs_t", [P, XH, 2, T])
                stats = alloc(nc, xs, "stats", [P, 16])
                cross_attention(nc, s, qx, kx, vx, pe_, pt, stats, a1, semaphores(nc, xs))
        with ExitStack() as rg:
            s.ring(rg, "_f")
            with nc.Block() as block:
                @block.vector
                def _(eng):
                    eng.memset(s.tb[:], 0.0)
            wo = s.phase("wo", "wo", 8, 4, 2, a1, "resid", out=s.a0, g="norm_ffn_g")
            phs = [wo]
            for q in range(4):
                up = s.phase("ffn1", "ffn1", 8, 4, 2, s.a0, "relu2", out=a1, w0=32 * q,
                             after=wo if q == 0 else None, sum_after=q == 0)
                down = s.phase("ffn2", "ffn2", 8, 4, 2, a1, "sumsq" if q == 3 else "acc", w0=32 * q, after=up)
                phs += [up, down]
            stream_block(nc, s, phs)


def final_norm(nc, s, g, out_dram=None):
    with ExitStack() as st, nc.Block() as block:
        sem = semaphores(nc, st)
        sm, rt, rs, nm = (sem(g + n) for n in ("_sum", "_root", "_rstd", "_normed"))

        @block.tensor
        def _(eng):
            for t in range(2):
                ins = eng.matmul(s.work[:, 3, 0:T], s.const("ones"), s.sq[:, t, :], start=t == 0, stop=t == 1)
            ins.then_inc(sm, 1)

        @block.scalar
        def _(eng):
            eng.wait_ge(sm, 1)
            eng.activation(s.root[:], s.work[:, 3, 0:T], ACT.Sqrt, scale=1.0 / D, bias=s.eps[:, 0:1]).then_inc(rt, 1)

        @block.vector
        def _(eng):
            eng.wait_ge(rt, 1)
            eng.reciprocal(s.rstd[:], s.root[:]).then_inc(rs, 1)
            eng.wait_ge(rs, 1)
            for kt in range(KT):
                eng.scalar_tensor_tensor(out=s.x[:, kt, :], in0=s.x[:, kt, :], scalar=s.par(g, kt), in1=s.rstd[:],
                                         op0=ALU.mult, op1=ALU.mult).then_inc(nm, 1)

        if out_dram is not None:
            @block.sync
            def _(eng):
                for q in range(4):
                    eng.wait_ge(nm, 4 * q + 4)
                    eng.dma_start(out_dram[:, 1024 * q:1024 * q + 1024],
                                  s.x[:, 4 * q:4 * q + 4, :].rearrange("p a t -> p (a t)")).then_inc(rs, 16)
                eng.wait_ge(rs, 65)


def window_attention(nc, s, ua):
    with ExitStack() as st:
        sem = semaphores(nc, st)
        kz = alloc(nc, st, "kz", [P, 2, 2, T])
        vtk = alloc(nc, st, "vtk", [P, 2, P])
        bias = alloc(nc, st, "alibi", [P, NH, T])
        sc = alloc(nc, st, "sc", [P, NH, T])
        pt = alloc(nc, st, "ptw", [P, NH, 2, P])
        mxs, nmx, sm, sk = (alloc(nc, st, n, [P, 2, NH]) for n in ("mxs", "nmx", "smw", "skw"))
        slp = alloc(nc, st, "slp", [P, NH])
        (kzr, vtr, vtc, alr, scr, scs, mxr, exr, skr, nrm, trr, ptr, pvr, hir, lk, pk) = (sem(n) for n in (
            "keys_placed", "v2_turned", "v2_copied", "alibi_ready", "scores2", "scores2_biased", "maxima2",
            "exps2", "sink_exps", "probs2_normed", "probs2_turned", "probs2_copied", "outputs2",
            "outputs2_copied", "vector_link_w", "pool_link_w"))
        banks = lambda i: (s.work if i < 4 else s.acc)[:, i % 4, :]
        nk = (P, 2 * P)
        POOL_HEADS = 4
        with nc.Block() as block:
            @block.gpsimd
            def _(eng):
                eng.tensor_scalar(slp[:], s.par("slopes"), -1.0, None, ALU.mult).then_inc(pk, 1)
                eng.memset(kz[:], 0.0).then_inc(kzr, 1)
                eng.wait_ge(pk, 1)
                for h in range(POOL_HEADS):
                    ins = eng.tensor_scalar(bias[:, h, :], s.const("dist", 2 * P), slp[:, h:h + 1], None, ALU.mult)
                ins.then_inc(alr, 1)

            @block.tensor
            def _(eng):
                for m in range(2):
                    ins = eng.transpose(s.acc[:, 3, m * P:(m + 1) * P], ua[:, V2, m * P:(m + 1) * P], s.const("ident"))
                ins.then_inc(vtr, 1)
                eng.wait_ge(kzr, 2)
                eng.wait_ge(vtc, 1)
                for n in range(2):
                    for j in range(8):
                        i = 8 * n + j
                        at_least(eng, scs, i - 7)
                        if n == 1 and j == 0:
                            eng.wait_ge(hir, 2)
                        ins = eng.matmul(banks(j)[:, 0:2 * nk[n]], ua[:, Q2 + j, n * P:(n + 1) * P],
                                         kz[:, j // 4, :, 0:nk[n]], start=True, stop=True)
                        ins.then_inc(scr, 1)
                    turns = NH // 4 * (n + 1)
                    for b in range(turns):
                        if n == 0:
                            eng.wait_ge(nrm, 4 * b + 4)
                            four = [(4 * b + q, 0) for q in range(4)]
                        else:
                            eng.wait_ge(nrm, NH + 2 * b + 2)
                            four = [(2 * b + q // 2, q % 2) for q in range(4)]
                        eng.wait_ge(scs, 8 * n + 8)
                        for q, (h, m) in enumerate(four):
                            ins = eng.transpose(banks(b)[:, q * P:(q + 1) * P], sc[:, h, m * P:(m + 1) * P],
                                                s.const("ident"))
                        ins.then_inc(trr, 1)
                    for b in range(2):
                        eng.wait_ge(ptr, (4 if n == 0 else 12))
                        for j in range(4 * b, 4 * b + 4):
                            for hh in range(2):
                                h = 2 * j + hh
                                g = h // 8
                                out = banks(2 * n + b)[64 * hh:64 * hh + 64, (j % 4) * P:(j % 4 + 1) * P]
                                for m in range(n + 1):
                                    ins = eng.matmul(out, vtk[:, m, 64 * g:64 * g + 64], pt[:, h, m, :],
                                                     start=m == 0, stop=m == n)
                        ins.then_inc(pvr, 1)

            @block.scalar
            def _(eng):
                eng.wait_ge(pk, 1)
                for h in range(POOL_HEADS, NH):
                    ins = eng.activation(bias[:, h, :], s.const("dist", 2 * P), ACT.Copy, scale=slp[:, h:h + 1])
                ins.then_inc(alr, 1)
                eng.wait_ge(vtr, 1)
                eng.activation(vtk[:].rearrange("p m d -> p (m d)"), s.acc[:, 3, 0:2 * P], ACT.Copy).then_inc(vtc, 1)
                for n in range(2):
                    eng.wait_ge(mxr, n + 1)
                    eng.activation(sk[:, n, :], sk[:, n, :], ACT.Exp).then_inc(skr, 1)
                    for h in range(NH):
                        eng.activation(sc[:, h, 0:nk[n]], sc[:, h, 0:nk[n]], ACT.Exp, bias=nmx[:, n, h:h + 1],
                                       accum_out=sm[:, n, h:h + 1]).then_inc(exr, 1)
                    for b in range(4 * (n + 1)):
                        eng.wait_ge(trr, 4 * n + b + 1)
                        src = banks(b)
                        if n == 0:
                            dst = pt[:, 4 * b:4 * b + 4, 0, :]
                            eng.activation(dst, src.rearrange("p (h q) -> p h q", h=4), ACT.Copy).then_inc(ptr, 1)
                        else:
                            if b == 0:
                                eng.wait_ge(pvr, 2)
                            eng.activation(pt[:, 2 * b:2 * b + 2].rearrange("p h m q -> p (h m q)"), src,
                                           ACT.Copy).then_inc(ptr, 1)
                    for b in range(2):
                        eng.wait_ge(pvr, 2 * n + b + 1)
                        eng.activation(ua[:, Q2 + 4 * b:Q2 + 4 * b + 4, n * P:(n + 1) * P],
                                       banks(2 * n + b).rearrange("p (a q) -> p a q", a=4), ACT.Copy).then_inc(hir, 1)

            @block.vector
            def _(eng):
                link = Link(eng, lk)
                eng.wait_ge(kzr, 1)
                for g in range(2):
                    for hh in range(2):
                        ins = eng.tensor_copy(kz[64 * hh:64 * hh + 64, g, hh, :], ua[64 * g:64 * g + 64, K2, :])
                ins.then_inc(kzr, 1)
                eng.wait_ge(alr, 2)
                for n in range(2):
                    w = nk[n]
                    if n == 1:
                        eng.wait_ge(trr, 4)
                    for j in range(8):
                        eng.wait_ge(scr, 8 * n + j + 1)
                        eng.scalar_tensor_tensor(out=sc[:, 2 * j:2 * j + 2, 0:w],
                                                 in0=banks(j)[:, 0:2 * w].rearrange("p (h q) -> p h q", h=2),
                                                 scalar=64 ** -0.5, in1=bias[:, 2 * j:2 * j + 2, 2 * P - w:2 * P],
                                                 op0=ALU.mult, op1=ALU.add).then_inc(scs, 1)
                    eng.wait_ge(scs, 8 * n + 8)
                    link(eng.tensor_reduce(mxs[:, n, :], sc[:, :, 0:w], AX.X, ALU.max))
                    link(eng.tensor_tensor(mxs[:, n, :], mxs[:, n, :], s.par("sinks"), ALU.max))
                    eng.tensor_scalar(nmx[:, n, :], mxs[:, n, :], -1.0, None, ALU.mult)
                    eng.tensor_tensor(sk[:, n, :], s.par("sinks"), mxs[:, n, :], ALU.subtract).then_inc(mxr, 1)
                    eng.wait_ge(skr, n + 1)
                    eng.wait_ge(exr, NH * (n + 1))
                    link(eng.tensor_tensor(sm[:, n, :], sm[:, n, :], sk[:, n, :], ALU.add))
                    link(eng.reciprocal(sm[:, n, :], sm[:, n, :]))
                    for h in range(NH):
                        eng.tensor_scalar(sc[:, h, 0:w], sc[:, h, 0:w], sm[:, n, h:h + 1], None,
                                          ALU.mult).then_inc(nrm, 1)


def s5_and_gates(nc, dram, s, ua, gates):
    QT = ST // 4
    TURNS = 15
    AFTER_TURN, AFTER_BU, AFTER_OUT = (1, 5, 8, 12), (2, 6, 9, 13), (5, 8, 12, 15)
    c1, c2 = 6.28125, 0.0019340515136718750
    c3 = 2 * np.pi - c1 - c2
    magic = 1.5 * 2.0 ** 23
    with ExitStack() as st:
        sem = semaphores(nc, st)
        br, bi, cr, ci, bbr, bbi, tb2 = (alloc(nc, st, "s_" + n, [P, ST, 16]) for n in (
            "br", "bi", "cr", "ci", "bbr", "bbi", "tmp"))
        dt, ar, th, mag, kq, rr, co, si, abr, abi, den, zr, zi, t1 = (alloc(nc, st, "s_" + n, [P, ST]) for n in (
            "dt", "ar", "th", "mag", "kq", "rr", "cos", "sin", "abr", "abi", "den", "zr", "zi", "t1"))
        em = alloc(nc, st, "s_em", [P, 8, 2, ST])
        sqs = alloc(nc, st, "s_sqs", [P, 2, ST])
        bd, cd = (alloc(nc, st, n, [P, 2, QT, P]) for n in ("s_bd", "s_cd"))
        btn = alloc(nc, st, "s_bt", [P, 2, QT, P])
        er, ei, xr, xi = (alloc(nc, st, n, [P, QT, T]) for n in ("s_er", "s_ei", "s_xr", "s_xi"))
        q1, q2, q3 = (alloc(nc, st, n, [P, 2, T]) for n in ("s_q1", "s_q2", "s_q3"))
        w1, w2 = (q[:].rearrange("p a t -> p (a t)").rearrange("p (a t) -> p a t", a=QT) for q in (q1, q2))
        (ld, dtd, thd, magd, rrd, sid, rcd, cod, lk, bdz, bbd, bdr, btr, btc, bur, bud, xrd, cdr, yr, ysd, gld,
         hid, pk) = (sem(n) for n in (
             "states_loaded", "steps_exp", "angles_ready", "decays_exp", "angle_reduced", "sines_ready",
             "angle2_reduced", "cosines_ready", "vector_link_5", "bc_zeroed", "b_scaled", "b_placed", "b_turned",
             "b_copied5", "bu_ready", "bu_read", "states_ready5", "c_placed", "y_summed5", "y_ready5",
             "gelu_ready", "a0_high_parts", "pool_link_5"))
        bank = lambda i: s.work[:, i, :]
        gate_slot = lambda v: (gates.base["u"] + v) % 2
        with nc.Block() as block:
            @block.sync
            def _(eng):
                for n, d in (("b_re", br), ("b_im", bi), ("c_re", cr), ("c_im", ci)):
                    eng.dma_start(d[:], dram[n]).then_inc(ld, 16)
                s.sp(eng, gates)

            @block.gpsimd
            def _(eng):
                def place(dst, src, q, sign):
                    for b in range(QT):
                        for g in range(2):
                            rows, at = slice(64 * g, 64 * g + 64), 32 * b + 16 * g
                            ins = eng.tensor_scalar(dst[rows, b, at:at + 16], src[rows, QT * q + b, :], sign, None,
                                                    ALU.mult)
                    return ins
                eng.memset(bd[:], 0.0)
                eng.memset(cd[:], 0.0).then_inc(bdz, 1)
                eng.wait_ge(bdz, 1)
                link = Link(eng, pk)
                eng.wait_ge(sid, 1)
                eng.wait_ge(cod, 1)
                eng.tensor_copy(em[:, 0, 0, :], co[:])
                link(eng.tensor_copy(em[:, 0, 1, :], si[:]))
                for n in range(7):
                    c, sn = em[:, n, 0, :], em[:, n, 1, :]
                    eng.tensor_tensor(sqs[:, 0, :], c, c, ALU.mult)
                    eng.tensor_tensor(sqs[:, 1, :], sn, sn, ALU.mult)
                    link(eng.tensor_tensor(em[:, n + 1, 1, :], c, sn, ALU.mult))
                    eng.tensor_tensor(em[:, n + 1, 0, :], sqs[:, 0, :], sqs[:, 1, :], ALU.subtract)
                    link(eng.tensor_scalar(em[:, n + 1, 1, :], em[:, n + 1, 1, :], 2.0, None, ALU.mult))
                eng.wait_ge(bbd, 1)
                eng.wait_ge(ld, 64)
                for q in range(4):
                    at_least(eng, btr, q)
                    place(bd[:, 0], bbr, q, 1.0)
                    place(bd[:, 1], bbi, q, 1.0).then_inc(bdr, 1)
                    at_least(eng, yr, q)
                    place(cd[:, 0], cr, q, 1.0)
                    place(cd[:, 1], ci, q, -1.0).then_inc(cdr, 1)

            @block.scalar
            def _(eng):
                eng.activation(dt[:], s.par("ldt"), ACT.Exp).then_inc(dtd, 1)
                s.act_split(eng, gates, 0, 0)
                eng.wait_ge(thd, 1)
                eng.activation(mag[:], ar[:], ACT.Exp).then_inc(magd, 1)
                eng.wait_ge(rrd, 1)
                eng.activation(si[:], rr[:], ACT.Sin).then_inc(sid, 1)
                eng.wait_ge(rcd, 1)
                eng.activation(co[:], kq[:], ACT.Sin).then_inc(cod, 1)
                for v in range(1, gates.units + 1):
                    if v < gates.units:
                        s.act_split(eng, gates, v, v)
                    if v - 1 in AFTER_TURN:
                        q = AFTER_TURN.index(v - 1)
                        eng.wait_ge(btr, q + 1)
                        at_least(eng, bur, 2 * q)
                        for im in range(2):
                            ins = eng.activation(btn[:, im].rearrange("p a c -> p (a c)"), bank(im), ACT.Copy)
                        ins.then_inc(btc, 1)
                    s.act_finish(eng, gates, v - 1, gate_slot(v - 1))
                eng.wait_ge(s.s_used, gates.base["c"] + gates.units * gates.nc)
                eng.activation(s.a0[:, 4:12, 0, :], ua[:, Q2:Q2 + 8, :], ACT.Copy).then_inc(hid, 1)
                for a in range(4):
                    eng.wait_ge(ysd, a + 1)
                    eng.activation(ua[:, S2 + a, :], ua[:, S2 + a, :], ACT.Gelu).then_inc(gld, 1)
                eng.wait_ge(gld, 4)
                eng.activation(s.a0[:, 0:4, 0, :], ua[:, S2:S2 + 4, :], ACT.Copy).then_inc(hid, 1)

            @block.tensor
            def _(eng):
                for v in range(gates.units):
                    s.unit(eng, gates, v, v)
                    if v in AFTER_OUT:
                        q = AFTER_OUT.index(v)
                        eng.wait_ge(cdr, q + 1)
                        eng.wait_ge(xrd, q + 1)
                        for b in range(QT):
                            for im, xs in ((0, xr), (1, xi)):
                                ins = eng.matmul(bank(2)[:, 0:T], cd[:, im, b, :], xs[:, b, :],
                                                 start=b + im == 0, stop=b == QT - 1 and im == 1)
                        ins.then_inc(yr, 1)
                    if v in AFTER_TURN:
                        q = AFTER_TURN.index(v)
                        eng.wait_ge(bdr, q + 1)
                        at_least(eng, bud, 2 * q - 1)
                        for im in range(2):
                            for b in range(QT):
                                ins = eng.transpose(bank(im)[:, b * P:(b + 1) * P], bd[:, im, b, :], s.const("ident"))
                        ins.then_inc(btr, 1)
                    if v in AFTER_BU:
                        q = AFTER_BU.index(v)
                        eng.wait_ge(btc, q + 1)
                        at_least(eng, bud, 2 * q)
                        at_least(eng, ysd, q)
                        for p in range(2):
                            for im in range(2):
                                for t in range(2):
                                    ins = eng.matmul(bank(2 * p + im)[:, t * T:(t + 1) * T], btn[:, im, 2 * p + t, :],
                                                     ua[:, S2 + q, :], start=True, stop=True)
                            ins.then_inc(bur, 1)

            @block.vector
            def _(eng):
                link = Link(eng, lk)
                tt, ts, stt = eng.tensor_tensor, eng.tensor_scalar, eng.scalar_tensor_tensor
                are, aim = s.par("are"), s.par("aim")
                done = [0]

                def split(n=1):
                    for _ in range(n):
                        v, k = divmod(done[0], gates.nc)
                        s.split_low(eng, gates, v, v, k)
                        if k == gates.nc - 1 and v:
                            s.evacuate(eng, gates, v - 1, gate_slot(v - 1))
                        done[0] += 1

                def reduce(out, turns, offset):
                    link(ts(kq[:], turns[:], magic, None, ALU.add))
                    link(ts(kq[:], kq[:], magic, None, ALU.subtract))
                    link(stt(out=out, in0=kq[:], scalar=-c1, in1=th[:], op0=ALU.mult, op1=ALU.add))
                    link(stt(out=out, in0=kq[:], scalar=-c2, in1=out, op0=ALU.mult, op1=ALU.add))
                    link(stt(out=out, in0=kq[:], scalar=-c3, in1=out, op0=ALU.mult, op1=ALU.add))
                    link(ts(out, out, offset, None, ALU.add))
                    return ts(out, out, 3.1415925, -3.1415925, ALU.min, ALU.max)

                eng.wait_ge(dtd, 1)
                tt(ar[:], are, dt[:], ALU.mult)
                tt(th[:], aim, dt[:], ALU.mult).then_inc(thd, 1)
                eng.wait_ge(thd, 1)
                split(2)
                link(ts(t1[:], th[:], 1 / (2 * np.pi), None, ALU.mult))
                reduce(rr[:], t1, 0.0).then_inc(rrd, 1)
                eng.wait_ge(rrd, 1)
                link(ts(t1[:], t1[:], 0.25, None, ALU.add))
                link(reduce(t1[:], t1, np.pi / 2))
                ts(kq[:], t1[:], 1.0, None, ALU.mult).then_inc(rcd, 1)
                eng.wait_ge(rcd, 1)
                split(2)
                tt(den[:], are, are, ALU.mult)
                link(tt(t1[:], aim, aim, ALU.mult))
                link(tt(den[:], den[:], t1[:], ALU.add))
                link(eng.reciprocal(den[:], den[:]))
                eng.wait_ge(magd, 1)
                eng.wait_ge(sid, 1)
                eng.wait_ge(cod, 1)
                tt(abr[:], mag[:], co[:], ALU.mult)
                link(tt(abi[:], mag[:], si[:], ALU.mult))
                link(ts(abr[:], abr[:], -1.0, None, ALU.add))
                split()
                tt(zr[:], abr[:], are, ALU.mult)
                link(tt(t1[:], abi[:], aim, ALU.mult))
                link(tt(zr[:], zr[:], t1[:], ALU.add))
                link(tt(zr[:], zr[:], den[:], ALU.mult))
                tt(zi[:], abi[:], are, ALU.mult)
                link(tt(t1[:], abr[:], aim, ALU.mult))
                link(tt(zi[:], zi[:], t1[:], ALU.subtract))
                link(tt(zi[:], zi[:], den[:], ALU.mult))
                split()
                eng.wait_ge(ld, 64)
                zrw, ziw = spread(zr[:], 16), spread(zi[:], 16)
                tt(bbr[:], br[:], zrw, ALU.mult)
                link(tt(tb2[:], bi[:], ziw, ALU.mult))
                link(tt(bbr[:], bbr[:], tb2[:], ALU.subtract))
                tt(bbi[:], bi[:], zrw, ALU.mult)
                link(tt(tb2[:], br[:], ziw, ALU.mult))
                tt(bbi[:], bbi[:], tb2[:], ALU.add).then_inc(bbd, 1)
                split(2)

                def output(q):
                    eng.wait_ge(yr, q + 1)
                    stt(out=ua[:, S2 + q, :], in0=ua[:, S2 + q, :], scalar=s.par("d2", q), in1=bank(2)[:, 0:T],
                        op0=ALU.mult, op1=ALU.add).then_inc(ysd, 1)

                for q in range(4):
                    mine = slice(QT * q, QT * q + QT)
                    eng.memset(ei[:, :, 0:1], 0.0)
                    link(eng.memset(er[:, :, 0:1], 1.0))
                    eng.wait_ge(pk, TURNS)
                    for n in range(8):
                        m = 2 ** n
                        c, sn = (spread(em[:, n, i, mine], m) for i in range(2))
                        e0r, e0i, v1, v2 = er[:, :, 0:m], ei[:, :, 0:m], w1[:, :, 0:m], w2[:, :, 0:m]
                        tt(v1, e0r, c, ALU.mult)
                        link(tt(v2, e0i, sn, ALU.mult))
                        link(tt(er[:, :, m:2 * m], v1, v2, ALU.subtract))
                        if m == T // 2:
                            split()
                        tt(v1, e0r, sn, ALU.mult)
                        link(tt(v2, e0i, c, ALU.mult))
                        link(tt(ei[:, :, m:2 * m], v1, v2, ALU.add))
                        if m in (2, 8, 32, 64, 128):
                            split()
                        if m == 8 and q:
                            output(q - 1)
                    for p in range(2):
                        eng.wait_ge(bur, 2 * q + p + 1)
                        pr = slice(2 * p, 2 * p + 2)
                        re, im = (bank(2 * p + i).rearrange("p (a t) -> p a t", a=2) for i in range(2))
                        tt(q1[:], er[:, pr], re, ALU.mult)
                        link(tt(q2[:], ei[:, pr], im, ALU.mult))
                        link(tt(xr[:, pr], q1[:], q2[:], ALU.add))
                        split()
                        tt(q1[:], er[:, pr], im, ALU.mult)
                        tt(q2[:], ei[:, pr], re, ALU.mult).then_inc(bud, 1)
                        eng.wait_ge(bud, 2 * q + p + 1)
                        link(tt(xi[:, pr], q1[:], q2[:], ALU.subtract))
                        split()
                        for jl in range(2 * p, 2 * p + 2):
                            j = QT * q + jl
                            for xs in (xr, xi):
                                ins = eng.tensor_tensor_scan(xs[:, jl, :], mag[:, j:j + 1].to_broadcast([P, T]),
                                                             xs[:, jl, :], 0.0, ALU.mult, ALU.add)
                        link(ins)
                        split()
                        tt(q1[:], er[:, pr], xr[:, pr], ALU.mult)
                        tt(q3[:], ei[:, pr], xr[:, pr], ALU.mult)
                        link(tt(q2[:], ei[:, pr], xi[:, pr], ALU.mult))
                        link(tt(xr[:, pr], q1[:], q2[:], ALU.subtract))
                        split()
                        link(tt(q1[:], er[:, pr], xi[:, pr], ALU.mult))
                        ins = tt(xi[:, pr], q3[:], q1[:], ALU.add)
                        if p == 0:
                            link(ins)
                        else:
                            ins.then_inc(xrd, 1)
                            eng.wait_ge(xrd, q + 1)
                assert done[0] == gates.units * gates.nc
                s.evacuate(eng, gates, gates.units - 1, gate_slot(gates.units - 1))
                output(3)
                eng.wait_ge(hid, 1)
                tt(s.a0[:, 4:12, 1, :], ua[:, Q2:Q2 + 8, :], s.a0[:, 4:12, 0, :].bitcast(F32), ALU.subtract)
                eng.wait_ge(hid, 2)
                link(tt(s.a0[:, 0:4, 1, :], ua[:, S2:S2 + 4, :], s.a0[:, 0:4, 0, :].bitcast(F32), ALU.subtract))


def clear_pads(nc, s):
    with nc.Block() as block:
        @block.vector
        def _(eng):
            eng.memset(s.tb[:], 0.0)


def second_block(nc, dram, s, out_dram):
    final_norm(nc, s, "final1_g")
    with ExitStack() as st:
        ub = alloc(nc, st, "ub", [P, 2 * KT, T])
        with ExitStack() as uas:
            ua = alloc(nc, uas, "ua", [P, GA2, T])
            with ExitStack() as rg:
                s.ring(rg, "_2")
                clear_pads(nc, s)
                emit = s.phase("emit", "", KT // 2, 0, 2, None, "emit", out=s.a0, g="norm2_g")
                pa = s.phase("in_a", "w_in_2", GA2 // 2, 4, 2, s.a0, "bias", out=ua, g="b_in", after=emit,
                             sum_after=True)
                pb = s.phase("in_b", "w_in_2", KT, 4, 2, s.a0, "sigmoid", out=ub, g="b_in", g0=GA2,
                             w0=4 * GA2 // 2)
                with nc.Block() as block:
                    @block.sync
                    def _(eng):
                        s.sp(eng, pa)

                    @block.scalar
                    def _(eng):
                        s.act(eng, [pa], emit=emit)

                    @block.vector
                    def _(eng):
                        s.dve(eng, [pa])

                    @block.gpsimd
                    def _(eng):
                        for v in range(KT // 2):
                            s.pool_finish(eng, emit, v, v % 2)

                    @block.tensor
                    def _(eng):
                        s.pe(eng, [pa])
            window_attention(nc, s, ua)
            with ExitStack() as rg:
                s.ring(rg, "_g", parts=False)
                s5_and_gates(nc, dram, s, ua, pb)
        with ExitStack() as ms:
            a1 = alloc(nc, ms, "a1_2", [P, KT, 2, T], F32R)
            gl = alloc(nc, ms, "gl", [P, 4, T])
            with ExitStack() as rg:
                s.ring(rg, "_m")
                clear_pads(nc, s)
                g1 = s.phase("glu_g", "glu", 2, 1, 4, s.a0, "glu_gate", out=gl, g="b_glu", g0=4)
                g2 = s.phase("glu_v", "glu", 2, 1, 4, s.a0, "glu_val", out=s.a0, t0=12, src=gl, w0=2)
                ba = s.phase("br_attn", "br_attn", 8, 2, 2, s.a0[:, 4:12], "br_attn", out=ub)
                bs = s.phase("br_ssm", "br_ssm", 8, 1, 4, s.a0[:, 12:16], "br_ssm", out=a1, src=ub, g0=KT, after=g2)
                wo = s.phase("w_out_2", "w_out_2", 8, 4, 2, a1, "resid", out=s.a0, g="ffn2_g", after=bs)
                stream_block(nc, s, [g1, g2, ba, bs, wo])
    with ExitStack() as st:
        a1 = alloc(nc, st, "a1_3", [P, KT, 2, T], F32R)
        gb = alloc(nc, st, "gb", [P, KT, T])
        with ExitStack() as rg:
            s.ring(rg, "_3")
            clear_pads(nc, s)
            phs = []
            for q, t0 in enumerate((0, KT, 2 * KT)):
                n = min(KT, FT2 - t0)
                gate = s.phase("gate", "up_gate", n // 2, 4, 2, s.a0, "gate", out=gb, g="c2", g0=3 * t0, p0=t0,
                               taps=3, w0=2 * t0, sum_after=q == 0)
                val = s.phase("val", "up_val", n // 2, 4, 2, s.a0, "val", out=a1, src=gb, w0=2 * t0)
                down = s.phase("down", "down", 8, n // 4, 4 if n % 16 else 2, a1, "sumsq" if q == 2 else "acc",
                               w0=32 * q, after=val)
                phs += [gate, val, down]
            stream_block(nc, s, phs)
    final_norm(nc, s, "final2_g", out_dram)


def build(nc, dram, out_dram):
    with ExitStack() as whole:
        s = Stream(nc, whole, dram)
        s_load = whole.enter_context(nc.semaphore("inputs_loaded"))
        s_prm = whole.enter_context(nc.semaphore("parameters_loaded"))
        s_zero = whole.enter_context(nc.semaphore("pads_zeroed"))
        mixers(nc, dram, s, s_load, s_prm, s_zero)
        attention_and_mlp(nc, dram, s)
        second_block(nc, dram, s, out_dram)


def alloc(nc, stack, name, shape, dt=F32):
    return stack.enter_context(nc.sbuf_tensor(name, shape, dt))


def zero_pads(eng, s, s_zero):
    eng.memset(s.eps[:, 0:1], EPS)
    eng.memset(s.eps[:, 1:2], RWKV_EPS)
    eng.memset(s.tb[:], 0.0).then_inc(s_zero, 1)


def mixers(nc, dram, s, s_load, s_prm, s_zero):
    with ExitStack() as st:
        u = alloc(nc, st, "u", [P, U_TILES, T])
        with ExitStack() as rg:
            s.ring(rg, "_in")
            emit = s.phase("emit", "", KT // 2, 0, 2, None, "emit", out=s.a0, g="norm_mix_g")
            rw = s.phase("rwkv_in", "w_in", RWKV_TILES // 2, 4, 2, s.a0, "rwkv", out=u, after=emit,
                           sum_after=True)
            z = s.phase("z_in", "w_in", RW // 2, 4, 2, s.a0, "z", out=u, t0=Z0, w0=4 * Z0 // 2)
            conv = s.phase("xbc_in", "w_in", 6, 4, 2, s.a0, "conv", out=u, t0=XS0, w0=4 * XS0 // 2,
                           g="conv", taps=4)
            phs = [rw, z, conv]
            with nc.Block() as block:
                @block.sync
                def _(eng):
                    eng.dma_start(s.prm[:], dram["prm"]).then_inc(s_prm, 16)
                    eng.dma_start(s.x[:].rearrange("p a b -> p (a b)"), dram["x"]).then_inc(s_load, 16)
                    s.prefetch(eng, rw)
                    eng.dma_start(s.consts[:], dram["consts"]).then_inc(s_prm, 16)
                    s.sp(eng, rw, skip=RING)
                    s.sp(eng, z)
                    s.sp(eng, conv)

                @block.scalar
                def _(eng):
                    eng.wait_ge(s_prm, 16)
                    eng.wait_ge(s_load, 16)
                    s.act(eng, phs, emit=emit)

                @block.vector
                def _(eng):
                    zero_pads(eng, s, s_zero)
                    eng.wait_ge(s_zero, 1)
                    eng.wait_ge(s_prm, 32)
                    s.dve(eng, phs)

                @block.gpsimd
                def _(eng):
                    for v in range(KT // 2):
                        s.pool_finish(eng, emit, v, v % 2)

                @block.tensor
                def _(eng):
                    eng.wait_ge(s_prm, 32)
                    s.pe(eng, phs)
        rwkv(nc, dram, s, u)
        ssd(nc, s, u)


def tiled(a):
    rows, cols = a.shape
    return np.ascontiguousarray(
        a.reshape(rows // (CK * P), CK, P, cols // UNIT, UNIT).transpose(3, 0, 2, 1, 4)
        .reshape(-1, P, CK * UNIT))


def columns(v):
    return np.ascontiguousarray(np.asarray(v).reshape(-1, P).T)


def channel_major(a):
    n = a.shape[1] // P
    return np.ascontiguousarray(a.T.reshape(n, P, -1).transpose(1, 0, 2).reshape(P, -1))


def lay_out(i):
    f = {k: np.asarray(v) for k, v in i.items()}
    w = f["w_in"][0]
    ssd, rk = 2576, 3072
    zeros = np.zeros((D, 1), np.float32)

    def cols(a, b):
        return w[:, a:b]
    tile_pw = [cols(ssd + rk, ssd + rk + RANK), cols(2560, 2576), zeros.repeat(16, 1)]
    tile_pa = [cols(ssd + rk + RANK, ssd + rk + 2 * RANK), zeros.repeat(32, 1)]
    w_in = np.concatenate([cols(ssd, ssd + rk), cols(ssd + rk + 2 * RANK, 6096)] + tile_pw + tile_pa
                          + [cols(0, 1024), cols(1024, 2560)], axis=1)
    mu = f["rwkv_mu"][0]
    z16 = np.zeros(32, np.float32)
    mu = np.concatenate([mu[0:rk], mu[rk + 2 * RANK:], mu[rk:rk + RANK], z16, mu[rk + RANK:rk + 2 * RANK], z16])

    def taps(a):
        k, c = a.shape
        return a.reshape(k, c // P, P).transpose(2, 1, 0).reshape(P, -1)

    def rows(v):
        return np.broadcast_to(v[None, :], (P, v.shape[0]))

    def states(a):
        return a.reshape(ST, P).T
    slopes = (2.0 ** (-8.0 * np.arange(1, NH + 1) / NH)).astype(np.float32)
    prm = {
        "norm_mix_g": columns(f["norm_mix_g"]), "norm_x_g": columns(f["norm_x_g"]),
        "norm_mem_g": columns(f["norm_mem_g"]), "norm_ffn_g": columns(f["norm_ffn_g"]),
        "norm2_g": columns(f["attn_norm_g_2"]), "ffn2_g": columns(f["ffn_norm_g_2"]),
        "final1_g": columns(f["final_norm_g"]), "final2_g": columns(f["final_norm_g_2"]),
        "mu": columns(mu), "conv": taps(f["ssd_conv_w"][0, :, 0]), "convb": columns(f["ssd_conv_b"]),
        "ssd_d": columns(np.repeat(f["ssd_d"][0], 64)), "ssd_g": columns(f["ssd_norm_g"]),
        "w0": columns(f["rwkv_w0"]), "a0": columns(f["rwkv_a0"]), "k_k": columns(f["rwkv_k_k"]),
        "k_a": columns(f["rwkv_k_a"]), "r_k": columns(f["rwkv_r_k"].reshape(-1)),
        "ln_w": columns(f["rwkv_ln_w"]), "ln_b": columns(f["rwkv_ln_b"]),
        "dt_bias": rows(f["ssd_dt_bias"][0]), "a_log": rows(f["ssd_a_log"][0]),
        "sinks": rows(f["attn_sinks_2"][0]), "slopes": rows(slopes),
        "b_in": columns(f["b_in_2"]), "b_glu": columns(f["b_glu_2"]),
        "c2": taps(f["conv_w_2"][0]), "c2b": columns(f["conv_b_2"]),
        "are": states(f["ssm_a_re_2"][0]), "aim": states(f["ssm_a_im_2"][0]),
        "ldt": states(np.repeat(f["ssm_log_dt_2"][0], 64)), "d2": columns(f["ssm_d_2"]),
    }
    packed = np.concatenate([prm[n] for n in PARAMS.at], axis=1)
    assert packed.shape == (P, PARAMS.n)

    def pad_rows(a, n=P):
        return np.concatenate([a, np.zeros((n - a.shape[0], a.shape[1]), np.float32)])
    w1, w2 = f["ffn_w1"][0], f["ffn_w2"][0]
    up, down = f["w_up_2"][0], f["w_down_2"][0]
    return {
        "consts": constants(), "prm": packed,
        "x": channel_major(f["x"][0]), "mem": channel_major(f["mem"][0]),
        "w_in": tiled(w_in), "w_out": tiled(f["w_out"][0]),
        "w2": pad_rows(f["rwkv_w2"][0]), "a2": pad_rows(f["rwkv_a2"][0]),
        "g2": np.ascontiguousarray(f["rwkv_g2"][0].reshape(2, P, 1024).transpose(1, 0, 2)),
        "wq": tiled(f["xattn_wq"][0]), "wk": tiled(f["xattn_wk"][0]),
        "wv": tiled(f["xattn_wv"][0]), "wo": tiled(f["xattn_wo"][0]),
        "ffn1": tiled(w1), "ffn2": np.concatenate([tiled(w2[D * q:D * (q + 1)]) for q in range(4)]),
        "w_in_2": tiled(f["w_in_2"][0]), "w_out_2": tiled(f["w_out_2"][0]),
        "glu": tiled(np.concatenate([f["w_glu_2"][0][:, 512:], f["w_glu_2"][0][:, :512]], axis=1)),
        "br_attn": tiled(f["w_branch_attn_2"][0]), "br_ssm": tiled(f["w_branch_ssm_2"][0]),
        "up_val": tiled(up[:, :FF2]), "up_gate": tiled(up[:, FF2:]),
        "down": np.concatenate([tiled(down[a:b]) for a, b in ((0, D), (D, 2 * D), (2 * D, FF2))]),
        "b_re": state_rows(f["ssm_b_re_2"][0]), "b_im": state_rows(f["ssm_b_im_2"][0]),
        "c_re": state_rows(f["ssm_c_re_2"][0].transpose(0, 2, 1)),
        "c_im": state_rows(f["ssm_c_im_2"][0].transpose(0, 2, 1)),
    }


def state_rows(a):
    return np.ascontiguousarray(a.reshape(ST, P, 16).transpose(1, 0, 2))


def kernel(**inputs):
    import concourse.bacc as bacc
    from concourse.bass_utils import run_bass_kernel_spmd

    nc = bacc.Bacc("TRN2", target_bir_lowering=False, num_devices=1)
    arrays = lay_out(inputs)
    dram = {n: nc.dram_tensor("in_" + n, a.shape, F32, kind="ExternalInput").ap() for n, a in arrays.items()}
    out = nc.dram_tensor("out_dram", (P, KT * T), F32, kind="ExternalOutput").ap()
    build(nc, dram, out)
    r = run_bass_kernel_spmd(nc, [{"in_" + n: a for n, a in arrays.items()}], core_ids=[0])
    got = r.results[0]["out_dram"]
    return got.reshape(P, KT, T).transpose(2, 1, 0).reshape(1, T, D)
```
